# Optimizing a Trainium2 kernel written in Bass

```python
import jax, jax.numpy as jnp
from jax import lax
import numpy as np

D_MODEL = 1024
BATCH = 1
SEQ = 256
DEPTH = 1

N_HEADS_ATTN = 8
HEAD_DIM = 64
ATTN_WIDTH = N_HEADS_ATTN * HEAD_DIM
MOBA_BLOCK = 256
MOBA_TOPK = 3
Q_CHUNK = 32
ROPE_THETA = 500000.0
ROT_DIM = HEAD_DIM // 4
CONV_WIDTH = 512
CONV_K = 3
N_BRANCH = 2
IN_COLS = 3 * ATTN_WIDTH + 3 * CONV_WIDTH + N_BRANCH * D_MODEL
N_GROUPS = 4
EXPERTS_PER_GROUP = 8
N_EXPERTS = N_GROUPS * EXPERTS_PER_GROUP
TOPK_IN_GROUP = 2
D_EXPERT = 512
MOE_BLOCK = 128
N_MOD = 6
EPS = 1e-6


def rms_norm(x, g):
    xf = x.astype(jnp.float32)
    y = xf * lax.rsqrt(jnp.mean(xf * xf, axis=-1, keepdims=True) + EPS)
    return (y * g.astype(jnp.float32)).astype(x.dtype)

def modulate(h, shift, scale):
    return h * (1 + scale[:, None, :]) + shift[:, None, :]

def rope_tables(seq_len, dtype):
    pos = jnp.arange(seq_len, dtype=jnp.float32)
    inv_freq = ROPE_THETA ** (-jnp.arange(0, ROT_DIM, 2, dtype=jnp.float32) / ROT_DIM)
    ang = pos[:, None] * inv_freq[None, :]
    return jnp.cos(ang).astype(dtype), jnp.sin(ang).astype(dtype)

def partial_rope(x, cos, sin):
    half = ROT_DIM // 2
    x1, x2, xp = x[..., :half], x[..., half:ROT_DIM], x[..., ROT_DIM:]
    return jnp.concatenate([x1 * cos - x2 * sin, x2 * cos + x1 * sin, xp], axis=-1)

def moba_attention(q, k, v):
    B, H, S, dh = q.shape
    nb = -(-S // MOBA_BLOCK)
    pad = nb * MOBA_BLOCK - S
    kb = jnp.pad(k, ((0, 0), (0, 0), (0, pad), (0, 0))).reshape(B, H, nb, MOBA_BLOCK, dh)
    vb = jnp.pad(v, ((0, 0), (0, 0), (0, pad), (0, 0))).reshape(B, H, nb, MOBA_BLOCK, dh)
    kmean = jnp.mean(kb.astype(jnp.float32), axis=3)
    topk = min(MOBA_TOPK, nb)
    scale = HEAD_DIM ** -0.5
    b_ix = jnp.arange(B)[:, None, None, None]
    h_ix = jnp.arange(H)[None, :, None, None]
    blk_ids = jnp.arange(nb)
    t_in_blk = jnp.arange(MOBA_BLOCK)

    def chunk(ci):
        q0 = ci * Q_CHUNK
        qc = lax.dynamic_slice_in_dim(q, q0, Q_CHUNK, axis=2)
        qpos = q0 + jnp.arange(Q_CHUNK)
        cur = q0 // MOBA_BLOCK
        gate = jnp.einsum('bhqd,bhnd->bhqn', qc.astype(jnp.float32), kmean)
        gate = jnp.where(blk_ids < cur, gate, -jnp.inf)
        _, sel = lax.top_k(gate, topk)
        sel_valid = jnp.arange(topk) < cur
        k_sel = kb[b_ix, h_ix, sel]
        v_sel = vb[b_ix, h_ix, sel]
        s_sel = jnp.einsum('bhqd,bhqntd->bhqnt', qc, k_sel).astype(jnp.float32) * scale
        s_sel = jnp.where(sel_valid[:, None], s_sel, -jnp.inf)
        k_own = lax.dynamic_index_in_dim(kb, cur, axis=2, keepdims=False)
        v_own = lax.dynamic_index_in_dim(vb, cur, axis=2, keepdims=False)
        s_own = jnp.einsum('bhqd,bhtd->bhqt', qc, k_own).astype(jnp.float32) * scale
        kpos = cur * MOBA_BLOCK + t_in_blk
        s_own = jnp.where(kpos[None, :] <= qpos[:, None], s_own, -jnp.inf)
        logits = jnp.concatenate([s_sel.reshape(B, H, Q_CHUNK, topk * MOBA_BLOCK), s_own], axis=-1)
        p = jax.nn.softmax(logits, axis=-1).astype(v.dtype)
        p_sel = p[..., :topk * MOBA_BLOCK].reshape(B, H, Q_CHUNK, topk, MOBA_BLOCK)
        p_own = p[..., topk * MOBA_BLOCK:]
        return (jnp.einsum('bhqnt,bhqntd->bhqd', p_sel, v_sel)
                + jnp.einsum('bhqt,bhtd->bhqd', p_own, v_own))

    out = lax.map(chunk, jnp.arange(S // Q_CHUNK))
    return out.transpose(1, 2, 0, 3, 4).reshape(B, H, S, dh)

def short_gated_conv(xb, bg, cg, conv_w, conv_b):
    u = cg * xb
    y = lax.conv_general_dilated(u, conv_w[:, None, :], window_strides=(1,), padding=[(CONV_K - 1, 0)],
                                 dimension_numbers=('NWC', 'WIO', 'NWC'), feature_group_count=CONV_WIDTH)
    return bg * (y + conv_b)

def hierarchical_moe(h, w_rg, b_rg, w_re, b_re, w1, w3, w2):
    B, S, D = h.shape
    T = B * S
    xt = h.reshape(T, D)
    g_logits = (xt @ w_rg).astype(jnp.float32) + b_rg.astype(jnp.float32)
    g_prob = jax.nn.softmax(g_logits, axis=-1)
    g_idx = jnp.argmax(g_logits, axis=-1)
    g_w = jnp.take_along_axis(g_prob, g_idx[:, None], axis=-1)
    e_logits = ((xt @ w_re).astype(jnp.float32) + b_re.astype(jnp.float32)).reshape(T, N_GROUPS, EXPERTS_PER_GROUP)
    e_logits = jnp.take_along_axis(e_logits, g_idx[:, None, None], axis=1)[:, 0]
    e_val, e_loc = lax.top_k(e_logits, TOPK_IN_GROUP)
    e_w = jax.nn.softmax(e_val, axis=-1) * g_w
    e_id = g_idx[:, None].astype(jnp.int32) * EXPERTS_PER_GROUP + e_loc.astype(jnp.int32)

    n_assign = T * TOPK_IN_GROUP
    flat_e = e_id.reshape(-1)
    flat_w = e_w.reshape(-1)
    order = jnp.argsort(flat_e)
    sorted_e = flat_e[order]
    counts = jnp.bincount(flat_e, length=N_EXPERTS)
    padded = (counts + MOE_BLOCK - 1) // MOE_BLOCK * MOE_BLOCK
    start = jnp.cumsum(counts) - counts
    pad_end = jnp.cumsum(padded)
    pad_start = pad_end - padded
    dest = pad_start[sorted_e] + (jnp.arange(n_assign) - start[sorted_e])
    n_pad = (-(-n_assign // MOE_BLOCK) + N_EXPERTS) * MOE_BLOCK
    n_blocks = n_pad // MOE_BLOCK
    tok = jnp.full((n_pad,), T, jnp.int32).at[dest].set((order // TOPK_IN_GROUP).astype(jnp.int32))
    wpad = jnp.zeros((n_pad,), jnp.float32).at[dest].set(flat_w[order])
    blk_start = jnp.arange(n_blocks) * MOE_BLOCK
    blk_expert = jnp.minimum(jnp.sum(pad_end[None, :] <= blk_start[:, None], axis=-1), N_EXPERTS - 1)
    x_ext = jnp.concatenate([xt, jnp.zeros((1, D), xt.dtype)], axis=0)
    xs = x_ext[tok].reshape(n_blocks, MOE_BLOCK, D)

    def expert_block(args):
        xb, e = args
        hid = jax.nn.silu(xb @ w1[e]) * (xb @ w3[e])
        return hid @ w2[e]

    ys = lax.map(expert_block, (xs, blk_expert)).reshape(n_pad, D)
    ys = ys * wpad[:, None].astype(ys.dtype)
    out = jnp.zeros((T + 1, D), ys.dtype).at[tok].add(ys)[:T]
    return out.reshape(B, S, D)

def first_inputs(seed: int = 0) -> dict:
    key = jax.random.key(seed)
    ks = jax.random.split(key, 24)
    L, D = DEPTH, D_MODEL
    f32 = jnp.float32
    nrm = lambda k, shape, s: jax.random.normal(k, shape, f32) * s
    return {
        "x": nrm(ks[0], (BATCH, SEQ, D), 1.0),
        "c": nrm(ks[1], (BATCH, D), 1.0),
        "w_ada": nrm(ks[2], (L, D, N_MOD * D), 0.5 * D ** -0.5),
        "b_ada": nrm(ks[3], (L, N_MOD * D), 0.02),
        "g_norm1": 1.0 + nrm(ks[4], (L, D), 0.02),
        "g_norm2": 1.0 + nrm(ks[5], (L, D), 0.02),
        "w_in": nrm(ks[6], (L, D, IN_COLS), D ** -0.5),
        "g_q": 1.0 + nrm(ks[7], (L, HEAD_DIM), 0.02),
        "g_k": 1.0 + nrm(ks[8], (L, HEAD_DIM), 0.02),
        "conv_w": nrm(ks[9], (L, CONV_K, CONV_WIDTH), CONV_K ** -0.5),
        "conv_b": nrm(ks[10], (L, CONV_WIDTH), 0.02),
        "w_pa": nrm(ks[11], (L, ATTN_WIDTH, D), ATTN_WIDTH ** -0.5),
        "w_pb": nrm(ks[12], (L, CONV_WIDTH, D), CONV_WIDTH ** -0.5),
        "w_o": nrm(ks[13], (L, D, D), D ** -0.5),
        "w_rg": nrm(ks[14], (L, D, N_GROUPS), D ** -0.5),
        "b_rg": nrm(ks[15], (L, N_GROUPS), 0.01),
        "w_re": nrm(ks[16], (L, D, N_EXPERTS), D ** -0.5),
        "b_re": nrm(ks[17], (L, N_EXPERTS), 0.01),
        "w1": nrm(ks[18], (L, N_EXPERTS, D, D_EXPERT), D ** -0.5),
        "w3": nrm(ks[19], (L, N_EXPERTS, D, D_EXPERT), D ** -0.5),
        "w2": nrm(ks[20], (L, N_EXPERTS, D_EXPERT, D), D_EXPERT ** -0.5),
    }

def first_block(x, c, w_ada, b_ada, g_norm1, g_norm2, w_in, g_q, g_k, conv_w, conv_b,
              w_pa, w_pb, w_o, w_rg, b_rg, w_re, b_re, w1, w3, w2):
    B, S, D = x.shape
    cos, sin = rope_tables(S, x.dtype)
    splits = [ATTN_WIDTH, 2 * ATTN_WIDTH, 3 * ATTN_WIDTH,
              3 * ATTN_WIDTH + CONV_WIDTH, 3 * ATTN_WIDTH + 2 * CONV_WIDTH, 3 * ATTN_WIDTH + 3 * CONV_WIDTH]
    for l in range(DEPTH):
        mod = jax.nn.silu(c) @ w_ada[l] + b_ada[l]
        sh1, sc1, ga1, sh2, sc2, ga2 = jnp.split(mod, N_MOD, axis=-1)

        h = modulate(rms_norm(x, g_norm1[l]), sh1, sc1)
        z = h @ w_in[l]
        q, k, v, xb, bg, cg, gates = jnp.split(z, splits, axis=-1)
        to_heads = lambda t: t.reshape(B, S, N_HEADS_ATTN, HEAD_DIM).transpose(0, 2, 1, 3)
        q = partial_rope(rms_norm(to_heads(q), g_q[l]), cos, sin)
        k = partial_rope(rms_norm(to_heads(k), g_k[l]), cos, sin)
        v = to_heads(v)
        y_a = moba_attention(q, k, v).transpose(0, 2, 1, 3).reshape(B, S, ATTN_WIDTH)
        y_b = short_gated_conv(xb, bg, cg, conv_w[l], conv_b[l])
        gate_a, gate_b = jnp.split(jax.nn.sigmoid(gates), N_BRANCH, axis=-1)
        merged = gate_a * (y_a @ w_pa[l]) + gate_b * (y_b @ w_pb[l])
        x = x + ga1[:, None, :] * (merged @ w_o[l])

        h2 = modulate(rms_norm(x, g_norm2[l]), sh2, sc2)
        x = x + ga2[:, None, :] * hierarchical_moe(h2, w_rg[l], b_rg[l], w_re[l], b_re[l], w1[l], w3[l], w2[l])
    return x


PLE_DIM = 256
HG_HEADS = 4
HG_DK = 128
HG_DV = 128
HG_KW = HG_HEADS * HG_DK
HG_VW = HG_HEADS * HG_DV
HG_CHUNK = 64
FOX_HEADS = 8
FOX_DH = 64
FOX_W = FOX_HEADS * FOX_DH
FOX_BLOCK = 128
D_FF = ((-(-8 * D_MODEL // 3) + 255) // 256) * 256

OFF_HG_Q = 0
OFF_HG_F = OFF_HG_Q + HG_KW
OFF_HG_I = OFF_HG_F + HG_KW
OFF_HG_G = OFF_HG_I + HG_VW
OFF_FOX_Q = OFF_HG_G + HG_VW
OFF_FOX_K = OFF_FOX_Q + FOX_W
OFF_FOX_V = OFF_FOX_K + FOX_W
OFF_FOX_F = OFF_FOX_V + FOX_W
OFF_GATE = OFF_FOX_F + FOX_HEADS
IN_COLS_2 = OFF_GATE + 2 * D_MODEL


def rms_norm_2(x, g):
    xf = x.astype(jnp.float32)
    y = xf * lax.rsqrt(jnp.mean(xf * xf, axis=-1, keepdims=True) + EPS)
    return (y * g.astype(jnp.float32)).astype(x.dtype)

def hgrn2_mixer(q, f_logit, i, g, lb, o_gain):
    B, S, _ = q.shape
    f32 = jnp.float32
    qf = jax.nn.silu(q.astype(f32))
    fg = lb + (1.0 - lb) * jax.nn.sigmoid(f_logit.astype(f32))
    kf = 1.0 - fg
    logf = jnp.log(fg)
    vf = i.astype(f32)
    n = S // HG_CHUNK

    def to_chunks(t, d):
        return t.reshape(B, n, HG_CHUNK, HG_HEADS, d).transpose(1, 0, 3, 2, 4)

    qc = to_chunks(qf, HG_DK)
    kc = to_chunks(kf, HG_DK)
    vc = to_chunks(vf, HG_DV)
    bc = jnp.cumsum(to_chunks(logf, HG_DK), axis=3)
    causal = jnp.tril(jnp.ones((HG_CHUNK, HG_CHUNK), dtype=bool))[:, :, None]

    def step(state, xs):
        qt, kt, vt, bt = xs
        inter = jnp.einsum('bhtc,bhcv->bhtv', qt * jnp.exp(bt), state)
        diff = bt[:, :, :, None, :] - bt[:, :, None, :, :]
        decay = jnp.exp(jnp.where(causal, diff, -jnp.inf))
        scores = jnp.einsum('bhtc,bhsc,bhtsc->bhts', qt, kt, decay)
        intra = jnp.einsum('bhts,bhsv->bhtv', scores, vt)
        b_last = bt[:, :, -1:, :]
        new_state = (jnp.exp(b_last[:, :, 0, :])[..., None] * state
                     + jnp.einsum('bhsc,bhsv->bhcv', kt * jnp.exp(b_last - bt), vt))
        return new_state, inter + intra

    s0 = jnp.zeros((B, HG_HEADS, HG_DK, HG_DV), f32)
    _, o = lax.scan(step, s0, (qc, kc, vc, bc))
    o = o.transpose(1, 0, 3, 2, 4).reshape(B, S, HG_HEADS, HG_DV)
    o = rms_norm_2(o, o_gain).reshape(B, S, HG_VW)
    o = o * jax.nn.silu(g.astype(f32))
    return o.astype(q.dtype)

def forgetting_attention(q, k, v, f_logit, f_bias, q_gain, k_gain):
    B, S, _ = q.shape
    f32 = jnp.float32

    def heads(t):
        return t.reshape(B, S, FOX_HEADS, FOX_DH).transpose(0, 2, 1, 3)

    qh = rms_norm_2(heads(q), q_gain).astype(f32)
    kh = rms_norm_2(heads(k), k_gain).astype(f32)
    vh = heads(v)
    logf = jax.nn.log_sigmoid(f_logit.astype(f32) + f_bias.astype(f32))
    c = jnp.cumsum(logf, axis=1).transpose(0, 2, 1)
    scale = FOX_DH ** -0.5
    outs = []
    for blk in range(S // FOX_BLOCK):
        t0 = blk * FOX_BLOCK
        t1 = t0 + FOX_BLOCK
        s = jnp.einsum('bhtd,bhsd->bhts', qh[:, :, t0:t1], kh[:, :, :t1]) * scale
        s = s + c[:, :, t0:t1, None] - c[:, :, None, :t1]
        mask = (t0 + jnp.arange(FOX_BLOCK))[:, None] >= jnp.arange(t1)[None, :]
        s = jnp.where(mask, s, -jnp.inf)
        pr = jax.nn.softmax(s, axis=-1).astype(vh.dtype)
        outs.append(jnp.einsum('bhts,bhsd->bhtd', pr, vh[:, :, :t1]))
    o = jnp.concatenate(outs, axis=2)
    return o.transpose(0, 2, 1, 3).reshape(B, S, FOX_W)

def second_inputs(seed: int = 0) -> dict:
    key = jax.random.key(seed)
    ks = jax.random.split(key, 24)
    f32 = jnp.float32

    def w(k, shape, fan_in):
        return jax.random.normal(k, shape, f32) * (fan_in ** -0.5)

    def gain(k, shape):
        return 1.0 + 0.02 * jax.random.normal(k, shape, f32)

    return {
        "x": jax.random.normal(ks[0], (BATCH, SEQ, D_MODEL), f32),
        "p": jax.random.normal(ks[1], (DEPTH, BATCH, SEQ, PLE_DIM), f32),
        "norm_mix_g": gain(ks[2], (DEPTH, D_MODEL)),
        "w_in": w(ks[3], (DEPTH, D_MODEL, IN_COLS_2), D_MODEL),
        "hg_lb_logits": 0.1 * jax.random.normal(ks[4], (DEPTH + 1, HG_KW), f32),
        "hg_onorm_g": gain(ks[5], (DEPTH, HG_DV)),
        "fox_f_bias": jax.random.uniform(ks[6], (DEPTH, FOX_HEADS), f32, minval=1.0, maxval=4.0),
        "fox_q_norm_g": gain(ks[7], (DEPTH, FOX_DH)),
        "fox_k_norm_g": gain(ks[8], (DEPTH, FOX_DH)),
        "w_branch_a": w(ks[9], (DEPTH, HG_VW, D_MODEL), HG_VW),
        "w_branch_b": w(ks[10], (DEPTH, FOX_W, D_MODEL), FOX_W),
        "w_out": w(ks[11], (DEPTH, D_MODEL, D_MODEL), D_MODEL),
        "norm_ffn_g": gain(ks[12], (DEPTH, D_MODEL)),
        "w_ffn_gate": w(ks[13], (DEPTH, D_MODEL, D_FF), D_MODEL),
        "w_ffn_up": w(ks[14], (DEPTH, D_MODEL, D_FF), D_MODEL),
        "w_ffn_down": w(ks[15], (DEPTH, D_FF, D_MODEL), D_FF),
        "norm_ple_g": gain(ks[16], (DEPTH, D_MODEL)),
        "w_ple_gate": w(ks[17], (DEPTH, D_MODEL, D_MODEL), D_MODEL),
        "w_ple_proj": w(ks[18], (DEPTH, PLE_DIM, D_MODEL), PLE_DIM),
    }

def second_block(x, p, norm_mix_g, w_in, hg_lb_logits, hg_onorm_g, fox_f_bias, fox_q_norm_g,
              fox_k_norm_g, w_branch_a, w_branch_b, w_out, norm_ffn_g, w_ffn_gate, w_ffn_up,
              w_ffn_down, norm_ple_g, w_ple_gate, w_ple_proj):
    lower_bounds = jnp.cumsum(jax.nn.softmax(hg_lb_logits.astype(jnp.float32), axis=0), axis=0)
    for layer in range(DEPTH):
        h = rms_norm_2(x, norm_mix_g[layer])
        z = h @ w_in[layer]
        y_a = hgrn2_mixer(z[..., OFF_HG_Q:OFF_HG_F], z[..., OFF_HG_F:OFF_HG_I],
                          z[..., OFF_HG_I:OFF_HG_G], z[..., OFF_HG_G:OFF_FOX_Q],
                          lower_bounds[layer], hg_onorm_g[layer])
        y_b = forgetting_attention(z[..., OFF_FOX_Q:OFF_FOX_K], z[..., OFF_FOX_K:OFF_FOX_V],
                                   z[..., OFF_FOX_V:OFF_FOX_F], z[..., OFF_FOX_F:OFF_GATE],
                                   fox_f_bias[layer], fox_q_norm_g[layer], fox_k_norm_g[layer])
        gate_a = jax.nn.sigmoid(z[..., OFF_GATE:OFF_GATE + D_MODEL])
        gate_b = jax.nn.sigmoid(z[..., OFF_GATE + D_MODEL:IN_COLS_2])
        merged = gate_a * (y_a @ w_branch_a[layer]) + gate_b * (y_b @ w_branch_b[layer])
        x = x + merged @ w_out[layer]
        hf = rms_norm_2(x, norm_ffn_g[layer])
        x = x + (jax.nn.silu(hf @ w_ffn_gate[layer]) * (hf @ w_ffn_up[layer])) @ w_ffn_down[layer]
        hp = rms_norm_2(x, norm_ple_g[layer])
        x = x + jax.nn.sigmoid(hp @ w_ple_gate[layer]) * (p[layer] @ w_ple_proj[layer])
    return x


def setup_inputs(seed=0):
    out = dict(first_inputs(seed))
    for name, value in second_inputs(seed + 1).items():
        if name != "x":
            out[name + "_2"] = value
    return out


def reference(
    x, c, w_ada, b_ada, g_norm1, g_norm2, w_in, g_q, g_k, conv_w, conv_b, w_pa, w_pb, w_o, w_rg,
    b_rg, w_re, b_re, w1, w3, w2, p_2, norm_mix_g_2, w_in_2, hg_lb_logits_2, hg_onorm_g_2,
    fox_f_bias_2, fox_q_norm_g_2, fox_k_norm_g_2, w_branch_a_2, w_branch_b_2, w_out_2,
    norm_ffn_g_2, w_ffn_gate_2, w_ffn_up_2, w_ffn_down_2, norm_ple_g_2, w_ple_gate_2,
    w_ple_proj_2,
):
    x = first_block(
        x, c, w_ada, b_ada, g_norm1, g_norm2, w_in, g_q, g_k, conv_w, conv_b, w_pa, w_pb, w_o,
        w_rg, b_rg, w_re, b_re, w1, w3, w2,
    )
    return second_block(
        x, p_2, norm_mix_g_2, w_in_2, hg_lb_logits_2, hg_onorm_g_2, fox_f_bias_2,
        fox_q_norm_g_2, fox_k_norm_g_2, w_branch_a_2, w_branch_b_2, w_out_2, norm_ffn_g_2,
        w_ffn_gate_2, w_ffn_up_2, w_ffn_down_2, norm_ple_g_2, w_ple_gate_2, w_ple_proj_2,
    )


_drawn_inputs = setup_inputs


def setup_inputs(seed=0):
    import zlib

    import numpy as np

    out = dict(_drawn_inputs(seed))
    spreads = {}
    factors = {'g_norm1': 4.88,
     'g_norm2': 12.185,
     'g_q': 38.724,
     'g_k': 33.949,
     'conv_b': 37.905,
     'b_rg': 200.0,
     'b_re': 64.0,
     'norm_mix_g_2': 5.412,
     'hg_lb_logits_2': 8.0,
     'hg_onorm_g_2': 31.927,
     'fox_q_norm_g_2': 168.137,
     'fox_k_norm_g_2': 184.277,
     'norm_ffn_g_2': 23.02,
     'norm_ple_g_2': 200.0,
     'p_2': 10.075,
     'w_ple_gate_2': 21.269,
     'w_ple_proj_2': 10.056,
     'fox_f_bias_2': 7.11}
    for name, (base, spread) in spreads.items():
        noise = np.random.default_rng([zlib.crc32(name.encode()), seed]).standard_normal(out[name].shape)
        drawn = base * np.exp(spread * noise) if base else spread * noise
        out[name] = __import__('jax').numpy.asarray(drawn.astype(out[name].dtype))
    for name, factor in factors.items():
        out[name] = (out[name] * factor).astype(out[name].dtype)
    return out
```

```python
from contextlib import ExitStack

import concourse.bass as bass
from concourse import mybir
import numpy as np

F32 = mybir.dt.float32
I32 = mybir.dt.int32
ALU = mybir.AluOpType
ACT = mybir.ActivationFunctionType
AX = mybir.AxisListType

P = 128
D = 1024
KD = D // P
T = 256
TT = T // P
HEADS = 8
DH = 64
ROT = DH // 4
HALF = ROT // 2
CW = 512
CT = CW // P
GROUPS = 4
PER_GROUP = 8
EXPERTS = GROUPS * PER_GROUP
PAIRS = EXPERTS // 2
FE = 512
FT = FE // P
CAP = 64
EXTRA_ROUNDS = T // CAP - 1
DFF = 2816
FFT = DFF // P
PLE = 256
HG = 4
EPS = 1e-6
SCALE = DH ** -0.5
BIG = 1e30
COL = 512
SLOTS = 6
SLOT = KD * COL
LEVELS = [64, 32, 16, 8, 4, 2, 1]
SC = 3 * P

C_IDENT = 0
C_MEAN_D = C_IDENT + P
C_MEAN_V = C_MEAN_D + P
C_ONES = C_MEAN_V + P
C_CAUSAL = C_ONES + P
C_BEFORE = C_CAUSAL + SC
C_LEVEL = C_BEFORE + P
C_IOTA = C_LEVEL + len(LEVELS) * P
C_COS = C_IOTA + CAP
C_SIN = C_COS + TT * HALF
C_ALL = C_SIN + TT * HALF

PARAM_ROWS = [("c", KD), ("b_ada", 6 * KD), ("g_norm1", KD), ("g_norm2", KD), ("conv_w", 3 * CT), ("conv_b", CT),
              ("norm_mix_g_2", KD), ("hg_lb_logits_2", 2 * HG), ("hg_onorm_g_2", 1), ("norm_ffn_g_2", KD),
              ("norm_ple_g_2", KD)]
PARAM_AT = {}
PARAM_N = 0
for _name, _rows in PARAM_ROWS:
    PARAM_AT[_name] = PARAM_N
    PARAM_N += _rows


def constant_table():
    c = np.zeros((P, C_ALL), np.float32)
    i = np.arange(P)
    c[:, C_IDENT:C_IDENT + P] = np.eye(P)
    c[:, C_MEAN_D:C_MEAN_D + P] = 1.0 / D
    c[:, C_MEAN_V:C_MEAN_V + P] = 1.0 / P
    c[:, C_ONES:C_ONES + P] = 1.0
    causal = np.where(i[None, :] <= i[:, None], 0.0, -BIG)
    c[:, C_CAUSAL:C_CAUSAL + P] = causal
    c[:, C_CAUSAL + 2 * P:C_CAUSAL + 3 * P] = causal
    c[:, C_BEFORE:C_BEFORE + P] = i[:, None] < i[None, :]
    for n, m in enumerate(LEVELS):
        same = i[:, None] // (2 * m) == i[None, :] // (2 * m)
        c[:, C_LEVEL + n * P:C_LEVEL + (n + 1) * P] = same & (i[:, None] % (2 * m) < m) & (i[None, :] % (2 * m) >= m)
    c[:, C_IOTA:C_IOTA + CAP] = np.arange(CAP)
    freq = np.float32(500000.0) ** (-np.arange(0, ROT, 2, dtype=np.float32) / np.float32(ROT))
    angle = np.arange(T, dtype=np.float32)[:, None] * freq[None, :]
    for table, at in ((np.cos(angle), C_COS), (np.sin(angle), C_SIN)):
        c[:, at:at + TT * HALF] = table.reshape(TT, P, HALF).transpose(1, 0, 2).reshape(P, TT * HALF)
    return c


class Rotation:

    def __init__(self, psum, first, count, order, done, free, released, uncounted=()):
        self.psum, self.first, self.count, self.done, self.free = psum, first, count, done, free
        self.index = {name: n for n, name in enumerate(order)}
        assert len(self.index) == len(order)
        self.order, self.claimed = order, 0
        self.done_at, self.released = {}, {}
        freed, done_n = [0] * count, 0
        for n, name in enumerate(order):
            done_n += name not in uncounted
            self.done_at[name] = done_n
            if name in released:
                self.released[name] = released[name]
            else:
                freed[n % count] += 1
                self.released[name] = free[n % count], freed[n % count]

    def bank(self, name):
        return self.psum[:, self.first + self.index[name] % self.count, :]

    def claim(self, pe, name):
        assert self.index[name] == self.claimed, (name, self.order[self.claimed])
        self.claimed += 1
        if self.index[name] >= self.count:
            pe.wait_ge(*self.released[self.order[self.index[name] - self.count]])
        return self.bank(name)

    def ready(self, engine, name):
        engine.wait_ge(self.done, self.done_at[name])
        return self.bank(name)

    def freed(self, name):
        assert self.released[name][0] is self.free[self.index[name] % self.count]
        return self.released[name][0], 1


def two_blocks(nc, A, consts, out):
    with ExitStack() as ctx:
        def sb(name, shape, dt=F32):
            return ctx.enter_context(nc.sbuf_tensor(name, shape, dt))

        sems = {}

        def sem(name):
            if name not in sems:
                sems[name] = ctx.enter_context(nc.semaphore(name))
            return sems[name]

        ps = ctx.enter_context(nc.psum_tensor("ps", [P, 8, 512], F32))
        ring = sb("ring", [P, SLOTS, SLOT])
        cst = sb("cst", [P, C_ALL])
        prow = sb("prow", [P, P])
        pcol = sb("pcol", [P, PARAM_N])
        xT = sb("xT", [P, KD, T])
        hT = sb("hT", [P, KD, T])
        sq = sb("sq", [P, KD, T])
        rows = sb("rows", [P, TT, D])
        arena = sb("arena", [P, 24 * T])
        uT = sb("uT", [P, CT, T + 2])
        ybT = sb("ybT", [P, CT, T])
        yaT = sb("yaT", [P, CT, T])
        gates = sb("gates", [P, 2 * KD, T])
        sp = sb("sp", [P, 4, SC])
        pT = sb("pT", [P, 2, SC])
        wr = sb("wr", [P, KD, GROUPS + EXPERTS])
        wfox = sb("wfox", [P, KD, HEADS])
        br = sb("br", [P, GROUPS + EXPERTS])
        gain = sb("gain", [P, 4, DH])
        fbias = sb("fbias", [HEADS, 1])
        rstd = sb("rstd", [P, T])
        nwt = sq[:, 4:7, :]
        sc_c = sb("sc_c", [P, 3, KD])
        mod = sb("mod", [P, 6 * KD])
        scale1 = sb("scale1", [P, KD])
        scale2 = sb("scale2", [P, KD])
        ga1h = sb("ga1h", [P, KD])
        oghalf = sb("oghalf", [P, 1])
        lbt = sb("lbt", [P, 8, HG])
        nstat = sb("nstat", [P, 4, TT * HEADS])
        amax = sb("amax", [P, HEADS, 2])
        aneg = sb("aneg", [P, HEADS, 2])
        asum = sb("asum", [P, HEADS, 2])
        ainv = sb("ainv", [P, HEADS, 2])
        lg = sb("lg", [P, TT, GROUPS + EXPERTS])
        r1 = sb("r1", [P, 12, TT])
        rank = sb("rank", [P, TT, (1 + EXTRA_ROUNDS) * EXPERTS + 2])
        wgt = sb("wgt", [P, TT, (1 + EXTRA_ROUNDS) * EXPERTS + 2])
        flagf = sb("flagf", [1, 2])
        flag = sb("flag", [1, 1], I32)
        foxc = sb("foxc", [HEADS, T])

        ident = cst[:, C_IDENT:C_IDENT + P]
        mean_d = cst[:, C_MEAN_D:C_MEAN_D + P]
        mean_v = cst[:, C_MEAN_V:C_MEAN_V + P]
        ones = cst[:, C_ONES:C_ONES + P]
        causal = cst[:, C_CAUSAL:C_CAUSAL + SC]
        before = cst[:, C_BEFORE:C_BEFORE + P]
        iota = cst[:, C_IOTA:C_IOTA + CAP]
        cos = cst[:, C_COS:C_COS + TT * HALF].rearrange("p (t r) -> p t r", t=TT)
        sin = cst[:, C_SIN:C_SIN + TT * HALF].rearrange("p (t r) -> p t r", t=TT)

        def pc(name, at=0, n=None):
            a = PARAM_AT[name] + at
            return pcol[:, a:a + (dict(PARAM_ROWS)[name] if n is None else n)]

        def part(at, tiles):
            return arena[:, at * T:(at + tiles) * T]

        qrow = part(0, 4).rearrange("p (t c) -> p t c", t=TT)
        krow = part(4, 4).rearrange("p (t c) -> p t c", t=TT)
        vrow = part(8, 4).rearrange("p (t c) -> p t c", t=TT)
        qT = part(12, 4).rearrange("p (c t) -> p c t", t=T)
        kT = part(16, 4).rearrange("p (c t) -> p c t", t=T)
        xbT = part(20, 4).rearrange("p (c t) -> p c t", t=T)
        sp_flat = sp[:, :, :].rearrange("p a b -> p (a b)")
        norm_tmp = sp_flat[:, 0:2 * CW]
        rtmp = sp_flat[:, 2 * CW:].rearrange("p (n r) -> p n r", n=4)
        fl = sp_flat[0:HEADS, 0:3 * T].rearrange("p (n t) -> p n t", n=3)
        merged = gates[:, 0:KD, :]
        Sa = part(0, 1)[:, 0:TT * CAP].rearrange("p (t c) -> p t c", t=TT)
        Sb = part(1, 1)[:, 0:TT * CAP].rearrange("p (t c) -> p t c", t=TT)
        Sw = part(2, 1).rearrange("p (t c) -> p t c", t=TT)
        ST = part(3, 1)
        xs = [part(4 + 2 * e, 2).rearrange("p (k c) -> p k c", k=KD) for e in range(2)]
        sil = [part(8 + e, 1) for e in range(2)]
        hid = [part(10 + e, 1).rearrange("p (f c) -> p f c", f=FT) for e in range(2)]
        ys = part(12, 4)
        zeros = part(16, 2)
        khT = xbT
        bT = uT[:, :, :].rearrange("p c t -> p (c t)")[:, 0:HG * T].rearrange("p (h t) -> p h t", h=HG)
        qhT = rows[:, 0, :].rearrange("p (h t) -> p h t", h=HG)
        irow = rows[:, 1, :].rearrange("p (t c) -> p t c", t=TT)
        E = [sq[:, 4 * n:4 * n + 4, :] for n in range(2)]
        QE = [gates[:, 4 * n:4 * n + 4, :] for n in range(2)]
        KE = [gates[:, 8 + 4 * n:12 + 4 * n, :] for n in range(2)]
        hoT = khT
        hsq = E[0]
        sgT = yaT
        scT = ybT[:, :, :].rearrange("p c t -> p (c t)").rearrange("p (n t) -> p n t", t=P)
        scX = pT[:, :, :].rearrange("p a b -> p (a b)")[:, 0:HG * P].rearrange("p (h t) -> p h t", t=P)
        fmask = rows[:, 0, 0:SC]
        rt = uT[:, :, :].rearrange("p c t -> p (c t)")[:, 0:8 * TT * EXPERTS].rearrange("p (n t e) -> p n t e", t=TT, e=EXPERTS)
        act = arena[:, 0:FFT * T].rearrange("p (f t) -> p f t", t=T)
        fsil = sp[:, 0:2, 0:T]
        prows = yaT[:, 0:2, :]
        ppT = ybT[:, 0:2, :]
        thp = [sp[:, n, 0:T] for n in range(2)]
        oT = gates[:, 0:KD, :]
        orow = rows

        dense_order = []
        for name in ("q", "k", "v", "xb", "cg", "bg"):
            dense_order += [f"{name}{u}" for u in range(2)]
        dense_order += [f"gate{u}" for u in range(8)] + ["mod_late"] + [f"proj{j}" for j in range(KD)]
        dense_order += [f"wo{u}" for u in range(4)] + [f"moe{u}" for u in range(4)]
        for name in ("hf", "hq", "hi", "fq", "fk", "fv", "hg"):
            dense_order += [f"{name}{u}" for u in range(2)]
        dense_order += [f"gate_b{u}" for u in range(8)] + [f"proj_b{j}" for j in range(KD)]
        dense_order += [f"wo_b{u}" for u in range(4)] + [f"ffn{f}" for f in range(FFT)]
        dense_order += [f"down{u}" for u in range(4)] + [f"ple{j}" for j in range(KD)]

        def attention_order(steps, tag, bias):
            for n in range(HEADS + 3):
                names = []
                if n < HEADS:
                    names += [f"bias{n}"] * bias + [f"qk{tag}{n}"]
                if 0 <= n - 2 < HEADS:
                    names.append(f"pt{tag}{n - 2}")
                if 0 <= n - 3 < HEADS:
                    names.append(f"pv{tag}{n - 3}")
                steps.append(names)
            return steps

        att1 = attention_order([], "", False)
        att2 = attention_order([], "_b", True)
        small_order = ["params"] + [f"x{i}" for i in range(4)] + ["mod_early", "ms_norm1", "tq0", "tq1", "tk0", "tk1"]
        small_order += [n for step in att1 for n in step]
        small_order += ["ms_norm2", "logits"] + [f"h2r{i}" for i in range(4)] + ["rank"]
        n_block1 = len(small_order)
        small_order += ["ms_mix", "fox_f"]
        level_names = ["cross"] + [f"lev{m}" for m in LEVELS] + ["diag"]
        level_units = {n: ["cross"] if n == "cross" else [n + "a", n + "b"] for n in level_names}
        after2 = {}
        slots2 = ["fq0", "fq1", "fk0", "fk1", "fv0", "fv1", "hg0", "hg1", "hg1"]
        for n, at in zip(level_names, slots2):
            after2.setdefault(at, []).append(level_units[n])
        after2["fk0"].append(["tq_b0", "tq_b1"])
        after2["fv0"].append(["tk_b0", "tk_b1"])
        for n, names in enumerate(att2):
            after2.setdefault(f"gate_b{min(n, 7)}", []).append(names)
        after2["gate_b0"].insert(0, ["ho0", "ho1"])
        after2["gate_b1"].insert(0, ["ms_h0", "ms_h1"])
        for name in dense_order:
            for names in after2.get(name, []):
                small_order += names
        small_order += ["ms_ffn", "ms_ple", "pp", "o00", "o10", "o01", "o11"]

        dense_released = {f"moe{u}": (sem("x2_ready"), 2 * u + 2) for u in range(4)}
        for u in range(2):
            for name in ("q", "k", "v", "fq", "fk", "fv"):
                dense_released[f"{name}{u}"] = sem(f"{name}_rows"), u + 1
            for name, ready in (("xb", "xb_ready"), ("bg", "yb_ready"), ("hf", "hf_exp"), ("hi", "hi_ready")):
                dense_released[f"{name}{u}"] = sem(ready), u + 1
        for tag in ("", "_b"):
            for n in range(8):
                dense_released[f"gate{tag}{n}"] = sem(f"gates_ready{tag}"), n + 1
                dense_released[f"proj{tag}{n}"] = sem(f"merged_ready{tag}"), n + 1
        for u in range(4):
            for name, ready in (("wo", "x1_ready"), ("wo_b", "x3_ready"), ("down", "x4_ready")):
                dense_released[f"{name}{u}"] = sem(ready), 2 * u + 2
        for f in range(FFT):
            dense_released[f"ffn{f}"] = sem("act_ready"), f + 1
        small_released = {"params": (sem("pcol_ready"), 1), "pp": (sem("ppT_ready"), 1)}
        for i in range(4):
            small_released[f"x{i}"] = sem("xT_ready"), i + 1
            small_released[f"h2r{i}"] = sem("h2_rows_ready"), i + 1
        for n, name in enumerate(("o00", "o10", "o01", "o11")):
            small_released[name] = sem("out_ready"), n + 1
        for u in range(2):
            small_released[f"ho{u}"] = sem("ho_ready"), u + 1
            for tag in ("", "_b"):
                small_released[f"tq{tag}{u}"] = sem("qT_ready" + tag), u + 1
                small_released[f"tk{tag}{u}"] = sem("kT_ready" + tag), u + 1
        for h in range(HEADS):
            for tag, y in (("", "ya_ready"), ("_b", "yb_ready_b")):
                small_released[f"pt{tag}{h}"] = sem("pT_ready" + tag), h + 1
                small_released[f"pv{tag}{h}"] = sem(y), h + 1
        dense = Rotation(ps, 0, 4, dense_order, sem("dense_done"), [sem(f"dense_free{b}") for b in range(4)],
                         dense_released, [f"moe{u}" for u in range(4)])
        small = Rotation(ps, 4, 4, small_order, sem("small_done"), [sem(f"small_free{b}") for b in range(4)],
                         small_released)
        G, H, Y0, Y1 = (ps[:, 4 + b, :] for b in range(4))

        chunks = []
        chunk_of = {}

        def cols(w, at, n=COL):
            return w[:, at:at + n].rearrange("(k p) n -> p k n", p=P)

        def chunk(name, loads, released):
            chunk_of[name] = len(chunks)
            chunks.append((loads, released))

        def wide(slot):
            return ring[:, slot, :].rearrange("p (k n) -> p k n", k=KD)

        def tall(slot):
            return ring[:, slot, :].rearrange("p (k n) -> p k n", n=D)

        def after(unit):
            return dense.done, dense.done_at[unit]

        w_ada, w_in, w_in2 = A["w_ada"][0], A["w_in"][0], A["w_in_2"][0]

        def ada(n, released):
            chunk(f"ada{n}", [(lambda s: wide(s), cols(w_ada, n * COL))], released)

        for n in range(3):
            ada(n, (sem("mod_used"), n + 1))
        ada(3, (small.done, small.done_at["mod_early"]))
        IN1 = dict(q=0, k=1, v=2, xb=3, bg=4, cg=5)
        for name in ("q", "k", "v", "xb", "cg", "bg"):
            chunk(name, [(lambda s: wide(s), cols(w_in, IN1[name] * COL))], after(name + "1"))
        for n in range(4):
            chunk(f"gate{n}", [(lambda s: wide(s), cols(w_in, (6 + n) * COL))], after(f"gate{2 * n + 1}"))
        for n in range(4, 11):
            ada(n, (sem("mod_used"), n))
        ada(11, after("mod_late"))
        chunk("pa", [(lambda s: tall(s), A["w_pa"][0].rearrange("(k p) n -> p k n", p=P))], after(f"proj{KD - 1}"))
        chunk("pb", [(lambda s: tall(s), A["w_pb"][0].rearrange("(k p) n -> p k n", p=P))], after(f"proj{KD - 1}"))
        for n in range(2):
            chunk(f"wo{n}", [(lambda s: wide(s), cols(A["w_o"][0], n * COL))], after(f"wo{2 * n + 1}"))

        moe_first = len(chunks)
        moe_slot = [(moe_first + n) % SLOTS for n in range(6)]
        for n in range(PAIRS):
            for name, at in (("moe_w1_used", 2 * n + 1), ("moe_up_done", 2 * n + 1), ("moe_w1_used", 2 * n + 2),
                             ("moe_up_done", 2 * n + 2), ("moe_ys_done", 2 * n + 2), ("moe_ys_done", 2 * n + 2)):
                chunk(f"moe{len(chunks)}", None, (sem(name), at))
        block2_first = len(chunks)
        IN2 = dict(hq=0, hf=512, hi=1024, hg=1536, fq=2048, fk=2560, fv=3072)
        GATE2 = 3584 + HEADS
        for name in ("hf", "hq", "hi", "fq", "fk", "fv", "hg"):
            chunk(name, [(lambda s: wide(s), cols(w_in2, IN2[name]))], after(name + "1"))
        for n in range(4):
            chunk(f"gate_b{n}", [(lambda s: wide(s), cols(w_in2, GATE2 + n * COL))], after(f"gate_b{2 * n + 1}"))
        for name in ("a", "b"):
            chunk("branch_" + name, [(lambda s: tall(s), A[f"w_branch_{name}_2"][0].rearrange("(k p) n -> p k n", p=P))],
                  after(f"proj_b{KD - 1}"))
        for n in range(2):
            chunk(f"wo_b{n}", [(lambda s: wide(s), cols(A["w_out_2"][0], n * COL))], after(f"wo_b{2 * n + 1}"))
        wg, wu, wd = A["w_ffn_gate_2"][0], A["w_ffn_up_2"][0], A["w_ffn_down_2"][0]
        FULL = DFF // COL
        REST = DFF - FULL * COL
        for n in range(FULL):
            chunk(f"ffn_gate{n}", [(lambda s: wide(s), cols(wg, n * COL))], after(f"ffn{4 * n + 3}"))
            chunk(f"ffn_up{n}", [(lambda s: wide(s), cols(wu, n * COL))], after(f"ffn{4 * n + 3}"))
        chunk("ffn_rest", [(lambda s: wide(s)[:, :, 0:REST], cols(wg, FULL * COL, REST)),
                           (lambda s: wide(s)[:, :, REST:2 * REST], cols(wu, FULL * COL, REST))], after(f"ffn{FFT - 1}"))
        DOWN = []
        for n in range(0, FFT, 4):
            m = min(4, FFT - n)
            DOWN.append((n, m))
            chunk(f"down{n // 4}", [(lambda s, m=m: tall(s)[:, 0:m, :],
                                     wd[n * P:(n + m) * P, :].rearrange("(k p) n -> p k n", p=P))],
                  (sem("down_used"), n // 4 + 1) if n + m < FFT else after("down3"))
        for n in range(2):
            chunk(f"ple_gate{n}", [(lambda s: wide(s), cols(A["w_ple_gate_2"][0], n * COL))], after(f"ple{4 * n + 3}"))
        chunk("ple_proj", [(lambda s: tall(s)[:, 0:2, :], A["w_ple_proj_2"][0].rearrange("(k p) n -> p k n", p=P))],
              after(f"ple{KD - 1}"))

        landed, arrive_at = [0] * SLOTS, []
        for n, (loads, _) in enumerate(chunks):
            landed[n % SLOTS] += 16 * (1 if loads is None else len(loads))
            arrive_at.append(landed[n % SLOTS])
        chunk_in = [sem(f"chunk_in{s}") for s in range(SLOTS)]
        spare_in = [sem(f"spare_in{s}") for s in range(SLOTS)]

        def arrived(pe, name):
            n = chunk_of[name]
            pe.wait_ge(chunk_in[n % SLOTS], arrive_at[n])
            return n % SLOTS

        moe_in_base = [arrive_at[moe_first + n] for n in range(6)]
        expert_w = [A["w1"][0], A["w3"][0], A["w1"][0], A["w3"][0], A["w2"][0], A["w2"][0]]

        def expert_load(sp_, n, pair, signal):
            which = 0 if n in (0, 1, 4) else 1
            src = expert_w[n][bass.ds(2 * pair + which, 1)].rearrange("e (k p) n -> p (e k) n", p=P)
            view = tall(moe_slot[n]) if n >= 4 else wide(moe_slot[n])
            sp_.dma_start(view, src).then_inc(signal[moe_slot[n]], 16)

        block = ctx.enter_context(nc.Block())

        @block.sync
        def _(sp_):
            def load(n):
                if n >= SLOTS:
                    sp_.wait_ge(*chunks[n - SLOTS][1])
                for view, src in chunks[n][0]:
                    sp_.dma_start(view(n % SLOTS), src).then_inc(chunk_in[n % SLOTS], 16)

            sp_.dma_start(rows[:, :, :], A["x"][0].rearrange("(t p) d -> p t d", p=P)).then_inc(sem("x_in"), 16)
            for n in range(moe_first):
                load(n)
            for n in range(6):
                sp_.wait_ge(*chunks[moe_first + n - SLOTS][1])
                expert_load(sp_, n, 0, chunk_in)
            with sp_.Fori(1, PAIRS) as i:
                for n, (name, before_) in enumerate((("moe_w1_used", -1), ("moe_up_done", -1), ("moe_w1_used", 0),
                                                     ("moe_up_done", 0), ("moe_ys_done", 0), ("moe_ys_done", 0))):
                    sp_.wait_ge(sem(name), 2 * i + before_)
                    expert_load(sp_, n, i, chunk_in)
            for n in range(block2_first - SLOTS, block2_first):
                sp_.wait_ge(*chunks[n][1])
            sp_.wait_ge(sem("flag_ready"), 1)
            more = sp_.value_load(flag[0:1, 0:1], min_val=0, max_val=1)
            with sp_.If(more > 0):
                for n in range(6):
                    expert_load(sp_, n, 0, spare_in)
                with sp_.Fori(1, PAIRS * EXTRA_ROUNDS) as i:
                    e = sp_.snap(i % PAIRS)
                    for n, (name, before_) in enumerate((("spare_w1_used", -1), ("spare_up_done", -1),
                                                         ("spare_w1_used", 0), ("spare_up_done", 0),
                                                         ("spare_ys_done", 0), ("spare_ys_done", 0))):
                        sp_.wait_ge(sem(name), 2 * i + before_)
                        expert_load(sp_, n, e, spare_in)
                sp_.wait_ge(sem("spare_ys_done"), 2 * PAIRS * EXTRA_ROUNDS)
            for n in range(block2_first, len(chunks)):
                load(n)
            for n, (t, half) in enumerate(((0, 0), (1, 0), (0, 1), (1, 1))):
                sp_.wait_ge(sem("out_ready"), n + 1)
                sp_.dma_start(out[0, t * P:(t + 1) * P, half * 512:half * 512 + 512],
                              orow[:, t, half * 512:half * 512 + 512]).then_inc(sem("out_sent"), 16)
            sp_.wait_ge(sem("out_sent"), 64)

        @block.gpsimd
        def _(pool):
            pool.dma_start(cst[:, :], consts).then_inc(sem("cst_in"), 16)
            for name, n in PARAM_ROWS:
                a = A[name]
                flat = {2: "a (k p) -> (a k) p", 3: "a b (k p) -> (a b k) p"}[len(a.shape)]
                pool.dma_start(prow[PARAM_AT[name]:PARAM_AT[name] + n, :], a.rearrange(flat, p=P)).then_inc(sem("params_in"), 16)
            for n, name in enumerate(("g_q", "g_k", "fox_q_norm_g_2", "fox_k_norm_g_2")):
                pool.dma_start(gain[:, n, :], A[name].to_broadcast([P, DH])).then_inc(sem("gain_in"), 16)
            nc.gpsimd.memset(uT[:, :, 0:2], 0.0).then_inc(sem("pad_ready"), 1)
            pool.dma_start(br[:, 0:GROUPS], A["b_rg"].to_broadcast([P, GROUPS])).then_inc(sem("route_in"), 16)
            pool.dma_start(br[:, GROUPS:], A["b_re"].to_broadcast([P, EXPERTS])).then_inc(sem("route_in"), 16)
            pool.dma_start(wr[:, :, 0:GROUPS], A["w_rg"][0].rearrange("(k p) n -> p k n", p=P)).then_inc(sem("route_in"), 16)
            pool.dma_start(wr[:, :, GROUPS:], A["w_re"][0].rearrange("(k p) n -> p k n", p=P)).then_inc(sem("route_in"), 16)
            pool.dma_start(wfox[:, :, :], cols(w_in2, 3584, HEADS)).then_inc(sem("fox_in"), 16)
            pool.dma_start(fbias[:, :], A["fox_f_bias_2"].rearrange("a h -> h a")).then_inc(sem("fox_in"), 16)
            dense.ready(pool, f"proj{KD - 1}")
            nc.gpsimd.memset(scT, 0.0).then_inc(sem("scores_zeroed"), 1)
            for n in range(len(level_names) - 1):
                pool.wait_ge(sem("decay_ready"), n + 1)
                if n >= 2:
                    small.ready(pool, level_units[level_names[n - 2]][-1])
                nc.gpsimd.tensor_tensor(KE[n % 2], khT, E[n % 2], ALU.mult).then_inc(sem("ke_ready"), 1)
            dense.ready(pool, f"proj_b{KD - 1}")
            pool.dma_start(prows, A["p_2"][0, 0].rearrange("(t p) n -> p t n", p=P)).then_inc(sem("p_in"), 16)

        @block.tensor
        def _(pe):
            mm = nc.tensor.matmul

            def square_sums(name, ready, tiles, weight):
                o = small.claim(pe, name)[:, 0:T]
                for k in range(tiles):
                    pe.wait_ge(*ready(k))
                    last = mm(o, lhsT=weight, rhs=sq[:, k, :], start=k == 0, stop=k == tiles - 1)
                last.then_inc(small.done, 1)

            def token_rows(name, unit, slot, h_ready):
                o = dense.claim(pe, name)
                for k in range(KD):
                    pe.wait_ge(sem(h_ready), k + 1)
                    last = mm(o, lhsT=hT[:, k, unit * P:(unit + 1) * P], rhs=wide(slot)[:, k, :],
                              start=k == 0, stop=k == KD - 1)
                last.then_inc(dense.done, 1)

            def channel_tiles(name, unit, slot, h_ready, moving):
                o = dense.claim(pe, name)
                for j in range(2):
                    at = (2 * unit + j) * P
                    for k in range(KD):
                        pe.wait_ge(sem(h_ready), k + 1)
                        last = mm(o[:, j * T:(j + 1) * T], lhsT=wide(slot)[:, k, at:at + P], rhs=moving[:, k, :],
                                  start=k == 0, stop=k == KD - 1)
                last.then_inc(dense.done, 1)

            def modulation(o, first, n):
                for c in range(first, first + n):
                    slot = arrived(pe, f"ada{c}")
                    for j in range(COL // P):
                        at = (c - first) * (COL // P) + j
                        for k in range(KD):
                            last = mm(o[:, at:at + 1], lhsT=wide(slot)[:, k, j * P:(j + 1) * P], rhs=sc_c[:, 2, k:k + 1],
                                      start=k == 0, stop=k == KD - 1)
                    if c < first + n - 1:
                        last.then_inc(sem("mod_used"), 1)
                return last

            def head_transposes(name, row, ready):
                pe.wait_ge(sem(ready), 1)
                for u in range(2):
                    o = small.claim(pe, f"{name}{u}")
                    for j in range(2):
                        for t in range(TT):
                            c = 2 * u + j
                            last = nc.tensor.transpose(o[:, j * T + t * P:j * T + (t + 1) * P],
                                                       row[:, t, c * P:(c + 1) * P], ident)
                    last.then_inc(small.done, 1)

            def scores(tag, h):
                o = small.claim(pe, f"qk{tag}{h}")
                pe.wait_ge(sem(f"qT_ready{tag}"), h // 4 + 1)
                pe.wait_ge(sem(f"kT_ready{tag}"), h // 4 + 1)
                a = DH * (h % 2)
                mm(o[:, 0:P], lhsT=qT[a:a + DH, h // 2, 0:P], rhs=kT[a:a + DH, h // 2, 0:P], start=True, stop=True)
                mm(o[:, P:SC], lhsT=qT[a:a + DH, h // 2, P:T], rhs=kT[a:a + DH, h // 2, :], start=True,
                   stop=True).then_inc(small.done, 1)

            def probs_transposes(tag, h):
                o = small.claim(pe, f"pt{tag}{h}")
                pe.wait_ge(sem(f"probs_ready{tag}"), h + 1)
                for n in range(3):
                    last = nc.tensor.transpose(o[:, n * P:(n + 1) * P], sp[:, h % 4, n * P:(n + 1) * P], ident)
                last.then_inc(small.done, 1)

            def weighted_values(tag, h):
                o = small.claim(pe, f"pv{tag}{h}")
                pe.wait_ge(sem(f"pT_ready{tag}"), h + 1)
                a = DH * (h % 2)
                p = pT[:, h % 2, :]
                mm(o[a:a + DH, 0:P], lhsT=vrow[:, 0, h * DH:(h + 1) * DH], rhs=p[:, 0:P], start=True, stop=True)
                for t in range(TT):
                    last = mm(o[a:a + DH, P:T], lhsT=vrow[:, t, h * DH:(h + 1) * DH], rhs=p[:, (1 + t) * P:(2 + t) * P],
                              start=t == 0, stop=t == 1)
                last.then_inc(small.done, 1)

            def key_bias(h):
                o = small.claim(pe, f"bias{h}")
                pe.wait_ge(sem("fox_c_ready"), 1)
                mm(o[:, 0:T], lhsT=ident[0:HEADS, h:h + 1].to_broadcast([HEADS, P]), rhs=foxc[:, :], start=True,
                   stop=True).then_inc(small.done, 1)

            def attention_step(tag, names):
                for name in names:
                    h = int(name[-1])
                    if name.startswith("bias"):
                        key_bias(h)
                    elif name.startswith("qk"):
                        scores(tag, h)
                    elif name.startswith("pt"):
                        probs_transposes(tag, h)
                    else:
                        weighted_values(tag, h)

            def branch_products(tag, slot_a, slot_b, ready_a, ready_b):
                for j in range(KD):
                    o = dense.claim(pe, f"proj{tag}{j}")
                    for n, (slot, y) in enumerate(((slot_a, yaT), (slot_b, ybT))):
                        pe.wait_ge(*(ready_a, ready_b)[n])
                        for k in range(CT):
                            last = mm(o[:, n * T:(n + 1) * T], lhsT=tall(slot)[:, k, j * P:(j + 1) * P], rhs=y[:, k, :],
                                      start=k == 0, stop=k == CT - 1)
                    last.then_inc(dense.done, 1)

            pe.wait_ge(sem("cst_in"), 16)
            pe.wait_ge(sem("params_in"), 16 * len(PARAM_ROWS))
            o = small.claim(pe, "params")
            nc.tensor.transpose(o[:, 0:PARAM_N], prow[0:PARAM_N, :], ident[0:PARAM_N, 0:PARAM_N]).then_inc(small.done, 1)
            pe.wait_ge(sem("x_in"), 16)
            for i in range(4):
                o = small.claim(pe, f"x{i}")
                for kk in range(2):
                    for t in range(TT):
                        k = 2 * i + kk
                        last = nc.tensor.transpose(o[:, kk * T + t * P:kk * T + (t + 1) * P],
                                                   rows[:, t, k * P:(k + 1) * P], ident)
                last.then_inc(small.done, 1)
            pe.wait_ge(sem("silu_c_ready"), 1)
            modulation(small.claim(pe, "mod_early"), 0, 4).then_inc(small.done, 1)
            square_sums("ms_norm1", lambda k: (sem("sq_norm1"), k // 2 + 1), KD, mean_d)
            for name in ("q", "k", "v", "xb", "cg", "bg"):
                slot = arrived(pe, name)
                for u in range(2):
                    if name in "qkv":
                        token_rows(f"{name}{u}", u, slot, "h1_ready")
                    else:
                        channel_tiles(f"{name}{u}", u, slot, "h1_ready", hT)
                    if name == "v":
                        head_transposes(("tq", "tk")[u], (qrow, krow)[u], ("q_normed", "k_normed")[u])
                    if name in ("xb", "cg", "bg"):
                        n = 2 * ("xb", "cg", "bg").index(name) + u
                        attention_step("", att1[n])
            for u in range(8):
                if u % 2 == 0:
                    slot = arrived(pe, f"gate{u // 2}")
                channel_tiles(f"gate{u}", u % 2, slot, "h1_ready", hT)
                if 6 + u < len(att1):
                    attention_step("", att1[6 + u])
            modulation(dense.claim(pe, "mod_late"), 4, 8).then_inc(dense.done, 1)
            slots = arrived(pe, "pa"), arrived(pe, "pb")
            branch_products("", *slots, (sem("ya_ready"), HEADS), (sem("yb_ready"), 2))
            for u in range(4):
                if u % 2 == 0:
                    slot = arrived(pe, f"wo{u // 2}")
                channel_tiles(f"wo{u}", u % 2, slot, "merged_ready", merged)
            square_sums("ms_norm2", lambda k: (sem("sq_norm2"), k + 1), KD, mean_d)
            pe.wait_ge(sem("route_in"), 64)
            o = small.claim(pe, "logits")
            for t in range(TT):
                for k in range(KD):
                    pe.wait_ge(sem("h2_ready"), k + 1)
                    last = mm(o[:, t * 64:t * 64 + GROUPS + EXPERTS], lhsT=hT[:, k, t * P:(t + 1) * P], rhs=wr[:, k, :],
                              start=k == 0, stop=k == KD - 1)
            last.then_inc(small.done, 1)
            for i in range(4):
                o = small.claim(pe, f"h2r{i}")
                for j in range(4):
                    k = 4 * (i % 2) + j
                    last = nc.tensor.transpose(o[:, j * P:(j + 1) * P], hT[:, k, (i // 2) * P:(i // 2 + 1) * P], ident)
                last.then_inc(small.done, 1)
            o = small.claim(pe, "rank")
            pe.wait_ge(sem("chosen_ready"), 1)
            chosen = rt[:, 0, :, :]
            mm(o[:, 0:32], lhsT=before, rhs=chosen[:, 0, :], start=True, stop=True)
            mm(o[:, 32:64], lhsT=before, rhs=chosen[:, 1, :], start=True, stop=False)
            mm(o[:, 32:64], lhsT=ones, rhs=chosen[:, 0, :], start=False, stop=True)
            mm(o[:, 64:96], lhsT=ones, rhs=chosen[:, 0, :], start=True, stop=False)
            mm(o[:, 64:96], lhsT=ones, rhs=chosen[:, 1, :], start=False, stop=True).then_inc(small.done, 1)
            pe.wait_ge(sem("zeros_ready"), 1)
            for u in range(4):
                o = dense.claim(pe, f"moe{u}")
                mm(o, lhsT=ident, rhs=zeros, start=True, stop=True)
            for name in small_order[n_block1 - 4:n_block1]:
                pe.wait_ge(*small.released[name])
            pe.wait_ge(sem("h2_rows_ready"), 4)

            def gather(pre, e):
                S = (Sa, Sb)[e]
                for k in range(KD):
                    for t in range(TT):
                        last = mm(G[:, k * CAP:(k + 1) * CAP], lhsT=rows[:, t, k * P:(k + 1) * P], rhs=S[:, t, :],
                                  start=t == 0, stop=t == TT - 1)
                last.then_inc(sem(pre + "gather_done"), 1)

            def up(pre, e, i, signal, base):
                for n, w in enumerate((moe_slot[2 * e], moe_slot[2 * e + 1])):
                    pe.wait_ge(signal[w], base[2 * e + n] + 16 * i)
                    for f in range(FT):
                        for k in range(KD):
                            last = mm(H[:, n * T + f * CAP:n * T + (f + 1) * CAP], lhsT=wide(w)[:, k, f * P:(f + 1) * P],
                                      rhs=xs[e][:, k, :], start=k == 0, stop=k == KD - 1)
                    last.then_inc(sem(pre + ("w1_used", "up_done")[n]), 1)

            def pair_of_experts(pre, i, signal, base):
                pe.wait_ge(sem(pre + "sb_ready"), i + 1)
                pe.wait_ge(sem(pre + "xs_ready"), 2 * i + 1)
                gather(pre, 1)
                up(pre, 0, i, signal, base)
                pe.wait_ge(sem(pre + "sw_ready"), i + 1)
                for t in range(TT):
                    last = nc.tensor.transpose(Y1[:, t * P:(t + 1) * P], Sw[:, t, :], ident)
                last.then_inc(sem(pre + "st_done"), 1)
                pe.wait_ge(sem(pre + "sa_ready"), i + 2)
                pe.wait_ge(sem(pre + "xs_ready"), 2 * i + 2)
                gather(pre, 0)
                pe.wait_ge(sem(pre + "hid_ready"), 2 * i + 1)
                up(pre, 1, i, signal, base)
                pe.wait_ge(sem(pre + "hid_ready"), 2 * i + 2)
                for e in range(2):
                    pe.wait_ge(signal[moe_slot[4 + e]], base[4 + e] + 16 * i)
                for half, Y in enumerate((Y0, Y1)):
                    if half == 1:
                        pe.wait_ge(sem(pre + "st_ready"), i + 1)
                    for f in range(FT):
                        for e in range(2):
                            last = mm(Y[e * CAP:(e + 1) * CAP, :], lhsT=hid[e][:, f, :],
                                      rhs=tall(moe_slot[4 + e])[:, f, half * 512:half * 512 + 512],
                                      start=f == 0, stop=f == FT - 1)
                    last.then_inc(sem(pre + "ys_done"), 1)
                for half in range(2):
                    pe.wait_ge(sem(pre + f"ys{half}_ready"), i + 1)
                    for j in range(4 * half, 4 * half + 4):
                        sums = dense.bank(f"moe{j // 2}")
                        last = mm(sums[:, (j % 2) * T:(j % 2 + 1) * T], lhsT=ys[:, j * P:(j + 1) * P], rhs=ST,
                                  start=False, stop=True, skip_group_check=True)
                last.then_inc(sem(pre + "combined"), 1)

            def experts(pre, rounds, signal, base):
                pe.wait_ge(sem(pre + "sa_ready"), 1)
                gather(pre, 0)
                with pe.Fori(0, PAIRS * rounds) as i:
                    pair_of_experts(pre, i, signal, base)
                pe.wait_ge(sem(pre + "xs_ready"), 2 * PAIRS * rounds + 1)

            experts("moe_", 1, chunk_in, moe_in_base)
            pe.wait_ge(sem("flag_ready"), 1)
            more = pe.value_load(flag[0:1, 0:1], min_val=0, max_val=1)
            with pe.If(more > 0):
                experts("spare_", EXTRA_ROUNDS, spare_in, [16] * 6)

            square_sums("ms_mix", lambda k: (sem("sq_mix"), k + 1), KD, mean_d)

            def fox_gate_logits():
                o = small.claim(pe, "fox_f")
                pe.wait_ge(sem("fox_in"), 32)
                for k in range(KD):
                    last = mm(o[0:HEADS, 0:T], lhsT=wfox[:, k, :], rhs=hT[:, k, :], start=k == 0, stop=k == KD - 1)
                last.then_inc(small.done, 1)

            def level(name):
                n = level_names.index(name)
                if name != "diag":
                    pe.wait_ge(sem("qe_ready"), n + 1)
                    pe.wait_ge(sem("ke_ready"), n + 1)
                q, k = (qhT, khT) if name == "diag" else (QE[n % 2], KE[n % 2])
                if name == "cross":
                    o = small.claim(pe, "cross")
                    for h in range(HG):
                        last = mm(o[:, h * P:(h + 1) * P], lhsT=k[:, h, 0:P], rhs=q[:, h, P:T], start=True, stop=True)
                    last.then_inc(small.done, 1)
                    return
                for u, unit in enumerate(level_units[name]):
                    o = small.claim(pe, unit)
                    for j in range(4):
                        h, t = (4 * u + j) // TT, j % TT
                        last = mm(o[:, j * P:(j + 1) * P], lhsT=k[:, h, t * P:(t + 1) * P],
                                  rhs=q[:, h, t * P:(t + 1) * P], start=True, stop=True)
                    last.then_inc(small.done, 1)

            def hgrn_values():
                pe.wait_ge(*small.released["diagb"])
                for u in range(2):
                    o = small.claim(pe, f"ho{u}")
                    for j in range(2):
                        h = 2 * u + j
                        v = irow[:, :, h * P:(h + 1) * P]
                        mm(o[:, j * T:j * T + P], lhsT=v[:, 0, :], rhs=scT[:, 2 * h, :], start=True, stop=True)
                        mm(o[:, j * T + P:(j + 1) * T], lhsT=v[:, 0, :], rhs=scX[:, h, :], start=True, stop=False)
                        last = mm(o[:, j * T + P:(j + 1) * T], lhsT=v[:, 1, :], rhs=scT[:, 2 * h + 1, :],
                                  start=False, stop=True)
                    last.then_inc(small.done, 1)

            def hgrn_norm():
                for u in range(2):
                    o = small.claim(pe, f"ms_h{u}")
                    pe.wait_ge(sem("hsq_ready"), u + 1)
                    mm(o, lhsT=mean_v, rhs=hsq[:, 2 * u:2 * u + 2, :], start=True, stop=True).then_inc(small.done, 1)

            def between(name):
                for names in after2.get(name, []):
                    if names[0].startswith(("tq", "tk")):
                        which = names[0][1]
                        head_transposes(f"t{which}_b", qrow if which == "q" else krow, f"{which}_normed_b")
                    elif names[0] == "ho0":
                        hgrn_values()
                    elif names[0] == "ms_h0":
                        hgrn_norm()
                    elif names[0].startswith(("cross", "lev", "diag")):
                        level("cross" if names[0] == "cross" else names[0][:-1])
                    else:
                        attention_step("_b", names)

            for name in ("hf", "hq", "hi", "fq", "fk", "fv", "hg"):
                slot = arrived(pe, name)
                for u in range(2):
                    if name in ("hi", "fq", "fk", "fv"):
                        token_rows(f"{name}{u}", u, slot, "hm_ready")
                    else:
                        channel_tiles(f"{name}{u}", u, slot, "hm_ready", hT)
                    if name == "hf" and u == 0:
                        fox_gate_logits()
                    between(f"{name}{u}")
            for u in range(8):
                if u % 2 == 0:
                    slot = arrived(pe, f"gate_b{u // 2}")
                channel_tiles(f"gate_b{u}", u % 2, slot, "hm_ready", hT)
                between(f"gate_b{u}")
            slots = arrived(pe, "branch_a"), arrived(pe, "branch_b")
            branch_products("_b", *slots, (sem("ya_ready_b"), HG), (sem("yb_ready_b"), HEADS))
            for u in range(4):
                if u % 2 == 0:
                    slot = arrived(pe, f"wo_b{u // 2}")
                channel_tiles(f"wo_b{u}", u % 2, slot, "merged_ready_b", merged)
            square_sums("ms_ffn", lambda k: (sem("sq_ffn"), k + 1), KD, mean_d)
            for f in range(FFT):
                if f < 4 * FULL:
                    sg, su = arrived(pe, f"ffn_gate{f // 4}"), arrived(pe, f"ffn_up{f // 4}")
                    ag = au = (f % 4) * P
                else:
                    sg = su = arrived(pe, "ffn_rest")
                    ag = (f - 4 * FULL) * P
                    au = REST + ag
                o = dense.claim(pe, f"ffn{f}")
                for n, (slot, at) in enumerate(((sg, ag), (su, au))):
                    for k in range(KD):
                        pe.wait_ge(sem("hf_ready"), k + 1)
                        last = mm(o[:, n * T:(n + 1) * T], lhsT=wide(slot)[:, k, at:at + P], rhs=hT[:, k, :],
                                  start=k == 0, stop=k == KD - 1)
                last.then_inc(dense.done, 1)
            downs = [dense.claim(pe, f"down{u}") for u in range(4)]
            for c, (first, m) in enumerate(DOWN):
                slot = arrived(pe, f"down{c}")
                for f in range(first, first + m):
                    pe.wait_ge(sem("act_ready"), f + 1)
                    for j in range(KD):
                        last = mm(downs[j // 2][:, (j % 2) * T:(j % 2 + 1) * T],
                                  lhsT=tall(slot)[:, f - first, j * P:(j + 1) * P], rhs=act[:, f, :],
                                  start=f == 0 and j % 2 == 0, stop=f == FFT - 1, skip_group_check=True)
                        if f == FFT - 1 and j % 2 == 1:
                            last.then_inc(dense.done, 1)
                if first + m < FFT:
                    last.then_inc(sem("down_used"), 1)
            square_sums("ms_ple", lambda k: (sem("sq_ple"), k + 1), KD, mean_d)
            o = small.claim(pe, "pp")
            pe.wait_ge(sem("p_in"), 16)
            for k in range(2):
                for t in range(TT):
                    last = nc.tensor.transpose(o[:, k * T + t * P:k * T + (t + 1) * P], prows[:, t, k * P:(k + 1) * P], ident)
            last.then_inc(small.done, 1)

            def result_rows(half):
                for t in range(TT):
                    o = small.claim(pe, f"o{t}{half}")
                    for j in range(4):
                        pe.wait_ge(sem("o_ready"), 4 * half + j + 1)
                        last = nc.tensor.transpose(o[:, j * P:(j + 1) * P], oT[:, 4 * half + j, t * P:(t + 1) * P], ident)
                    last.then_inc(small.done, 1)

            sproj = None
            for j in range(KD):
                if j % 4 == 0:
                    slot = arrived(pe, f"ple_gate{j // 4}")
                o = dense.claim(pe, f"ple{j}")
                for k in range(KD):
                    pe.wait_ge(sem("hp_ready"), k + 1)
                    mm(o[:, 0:T], lhsT=wide(slot)[:, k, (j % 4) * P:(j % 4 + 1) * P], rhs=hT[:, k, :],
                       start=k == 0, stop=k == KD - 1)
                if sproj is None:
                    sproj = arrived(pe, "ple_proj")
                    pe.wait_ge(sem("ppT_ready"), 1)
                for k in range(2):
                    last = mm(o[:, T:2 * T], lhsT=tall(sproj)[:, k, j * P:(j + 1) * P], rhs=ppT[:, k, :],
                              start=k == 0, stop=k == 1)
                last.then_inc(dense.done, 1)
                if j == 5:
                    result_rows(0)
            result_rows(1)

        @block.scalar
        def _(act_):
            af = nc.scalar.activation

            def exps(tag, h):
                act_.wait_ge(sem(f"max_ready{tag}"), h + 1)
                for t, (a, b) in enumerate(((0, P), (P, SC))):
                    last = af(sp[:, h % 4, a:b], sp[:, h % 4, a:b], ACT.Exp, bias=aneg[:, h, t:t + 1], scale=SCALE,
                              accum_out=asum[:, h, t:t + 1])
                    last.then_inc(sem(f"exp_ready{tag}"), 1)

            def probs_out(tag, h):
                src = small.ready(act_, f"pt{tag}{h}")
                af(pT[:, h % 2, :], src[:, 0:SC], ACT.Copy).then_inc(sem(f"pT_ready{tag}"), 1)

            def values_out(tag, h, y, ready):
                src = small.ready(act_, f"pv{tag}{h}")
                a = DH * (h % 2)
                af(y[a:a + DH, h // 2, :], src[a:a + DH, 0:T], ACT.Copy).then_inc(sem(ready), 1)

            def attention_step(tag, names, y, ready):
                for name in names:
                    if name.startswith("qk"):
                        exps(tag, int(name[-1]))
                    elif name.startswith("pt"):
                        probs_out(tag, int(name[-1]))
                    elif name.startswith("pv"):
                        values_out(tag, int(name[-1]), y, ready)

            def copy_out(out_, banks, name, ready):
                af(out_, banks.ready(act_, name), ACT.Copy).then_inc(sem(ready), 1)

            def two_tiles(t, u):
                return t[:, 2 * u:2 * u + 2, :]

            src = small.ready(act_, "params")
            af(pcol[:, :], src[:, 0:PARAM_N], ACT.Copy).then_inc(sem("pcol_ready"), 1)
            act_.wait_ge(sem("pcol_ready"), 1)
            af(sc_c[:, 0, :], pc("c"), ACT.Tanh, scale=0.5).then_inc(sem("tanh_c_ready"), 1)
            for i in range(4):
                copy_out(two_tiles(xT, i), small, f"x{i}", "xT_ready")
                act_.wait_ge(sem("xT_ready"), i + 1)
                af(two_tiles(sq, i), two_tiles(xT, i), ACT.Square).then_inc(sem("sq_norm1"), 1)
            act_.wait_ge(sem("lb_sub_ready"), 1)
            af(lbt[:, 2:4, :], lbt[:, 0:2, :], ACT.Exp).then_inc(sem("lb_exp_ready"), 1)
            for k in range(KD):
                act_.wait_ge(sem("h1_scaled"), k + 1)
                af(hT[:, k, :], hT[:, k, :], ACT.Identity, bias=mod[:, k:k + 1]).then_inc(sem("h1_ready"), 1)
            for name, row in (("q", qrow), ("k", krow), ("v", vrow)):
                for u in range(2):
                    copy_out(row[:, u, :], dense, f"{name}{u}", f"{name}_rows")
                    if name == "v":
                        which, dst = (("tq", qT), ("tk", kT))[u]
                        for i in range(2):
                            copy_out(two_tiles(dst, i), small, f"{which}{i}", f"{which[1]}T_ready")
            for u in range(6):
                if u < 2:
                    copy_out(two_tiles(xbT, u), dense, f"xb{u}", "xb_ready")
                attention_step("", att1[u], yaT, "ya_ready")
            for u in range(8):
                src = dense.ready(act_, f"gate{u}")
                af(two_tiles(gates, u), src, ACT.Tanh, scale=0.5).then_inc(sem("gates_ready"), 1)
                if 6 + u < len(att1):
                    attention_step("", att1[6 + u], yaT, "ya_ready")
            for k in range(KD):
                act_.wait_ge(sem("x1_ready"), k + 1)
                af(sq[:, k, :], xT[:, k, :], ACT.Square).then_inc(sem("sq_norm2"), 1)
            for k in range(KD):
                act_.wait_ge(sem("h2_scaled"), k + 1)
                af(hT[:, k, :], hT[:, k, :], ACT.Identity, bias=mod[:, 3 * KD + k:3 * KD + k + 1]).then_inc(sem("h2_ready"), 1)
            for i in range(4):
                copy_out(rows[:, i // 2, (i % 2) * 512:(i % 2) * 512 + 512], small, f"h2r{i}", "h2_rows_ready")
            act_.wait_ge(sem("route_sub_ready"), 1)
            af(rt[:, 6, :, 0:GROUPS], rt[:, 7, :, 0:GROUPS], ACT.Exp).then_inc(sem("route_exp_ready"), 1)
            act_.wait_ge(sem("second_ready"), 1)
            af(r1[:, 6, :], r1[:, 5, :], ACT.Exp).then_inc(sem("second_exp_ready"), 1)

            def experts(pre, rounds):
                def tokens_out(e, done):
                    act_.wait_ge(sem(pre + "gather_done"), done)
                    af(xs[e], G.rearrange("p (k c) -> p k c", k=KD), ACT.Copy).then_inc(sem(pre + "xs_ready"), 1)

                def silu(e, done):
                    act_.wait_ge(sem(pre + "up_done"), done)
                    af(sil[e], H[:, 0:T], ACT.Silu).then_inc(sem(pre + "sil_ready"), 1)

                tokens_out(0, 1)
                with act_.Fori(0, PAIRS * rounds) as i:
                    tokens_out(1, 2 * i + 2)
                    silu(0, 2 * i + 1)
                    tokens_out(0, 2 * i + 3)
                    silu(1, 2 * i + 2)
                    act_.wait_ge(sem(pre + "ys_done"), 2 * i + 2)
                    af(ys[:, 512:1024], Y1, ACT.Copy).then_inc(sem(pre + "ys1_ready"), 1)

            experts("moe_", 1)
            act_.wait_ge(sem("flag_ready"), 1)
            more = act_.value_load(flag[0:1, 0:1], min_val=0, max_val=1)
            with act_.If(more > 0):
                experts("spare_", EXTRA_ROUNDS)
            for k in range(KD):
                act_.wait_ge(sem("x2_ready"), k + 1)
                af(sq[:, k, :], xT[:, k, :], ACT.Square).then_inc(sem("sq_mix"), 1)
            for u in range(2):
                src = dense.ready(act_, f"hf{u}")
                af(two_tiles(khT, u), src, ACT.Exp, scale=-1.0).then_inc(sem("hf_exp"), 1)
                if u == 0:
                    act_.wait_ge(sem("fox_abs_ready"), 1)
                    af(fl[:, 2, :], fl[:, 1, :], ACT.Exp, scale=-1.0).then_inc(sem("fox_exp_ready"), 1)
                    act_.wait_ge(sem("fox_exp_ready"), 1)
                    af(fl[:, 2, :], fl[:, 2, :], ACT.Ln, bias=1.0).then_inc(sem("fox_ln_ready"), 1)
            act_.wait_ge(sem("fg_ready"), 1)
            af(QE[0], QE[0], ACT.Ln).then_inc(sem("logf_ready"), 1)
            for u in range(2):
                src = dense.ready(act_, f"hq{u}")
                af(two_tiles(qhT, u), src, ACT.Tanh, scale=0.5).then_inc(sem("hq_tanh"), 1)
            for u in range(2):
                copy_out(irow[:, u, :], dense, f"hi{u}", "hi_ready")

            def decay(n):
                act_.wait_ge(sem("diff_ready"), n + 1)
                af(E[n % 2], E[n % 2], ACT.Exp).then_inc(sem("decay_ready"), 1)

            n_level = 0
            for name, row in (("fq", qrow), ("fk", krow), ("fv", vrow)):
                for u in range(2):
                    copy_out(row[:, u, :], dense, f"{name}{u}", f"{name}_rows")
                    decay(n_level)
                    n_level += 1
                    if (name, u) in (("fk", 0), ("fv", 0)):
                        which, dst = (("q", qT), ("k", kT))[name == "fv"]
                        for i in range(2):
                            copy_out(two_tiles(dst, i), small, f"t{which}_b{i}", f"{which}T_ready_b")
            for u in range(2):
                src = dense.ready(act_, f"hg{u}")
                af(two_tiles(sgT, u), src, ACT.Tanh, scale=0.5).then_inc(sem("hg_tanh"), 1)
                decay(n_level)
                n_level += 1
                if n_level == len(level_names) - 1:
                    break
            for u in range(8):
                src = dense.ready(act_, f"gate_b{u}")
                af(two_tiles(gates, u), src, ACT.Tanh, scale=0.5).then_inc(sem("gates_ready_b"), 1)
                if u == 0:
                    for v in range(2):
                        src = small.ready(act_, f"ho{v}")
                        af(two_tiles(hoT, v), src, ACT.Copy).then_inc(sem("ho_ready"), 1)
                        act_.wait_ge(sem("ho_ready"), v + 1)
                        af(two_tiles(hsq, v), two_tiles(hoT, v), ACT.Square).then_inc(sem("hsq_ready"), 1)
                steps = att2[u:u + 1] if u < 7 else att2[7:]
                for names in steps:
                    attention_step("_b", names, ybT, "yb_ready_b")
            for k in range(KD):
                act_.wait_ge(sem("x3_ready"), k + 1)
                af(sq[:, k, :], xT[:, k, :], ACT.Square).then_inc(sem("sq_ffn"), 1)
            for f in range(FFT):
                src = dense.ready(act_, f"ffn{f}")
                if f >= 2:
                    act_.wait_ge(sem("act_ready"), f - 1)
                af(fsil[:, f % 2, :], src[:, 0:T], ACT.Silu).then_inc(sem("fsil_ready"), 1)
            for k in range(KD):
                act_.wait_ge(sem("x4_ready"), k + 1)
                af(sq[:, k, :], xT[:, k, :], ACT.Square).then_inc(sem("sq_ple"), 1)
            copy_out(ppT, small, "pp", "ppT_ready")

            def result_out(n, t, half):
                copy_out(orow[:, t, half * 512:half * 512 + 512], small, f"o{t}{half}", "out_ready")

            for j in range(KD):
                src = dense.ready(act_, f"ple{j}")
                if j >= 2:
                    act_.wait_ge(sem("o_ready"), j - 1)
                af(thp[j % 2], src[:, 0:T], ACT.Tanh, scale=0.5).then_inc(sem("thp_ready"), 1)
                if j == 5:
                    result_out(0, 0, 0)
                    result_out(1, 1, 0)
            result_out(2, 0, 1)
            result_out(3, 1, 1)

        @block.vector
        def _(dve):
            v = nc.vector
            chain = [0]

            def link(ins):
                chain[0] += 1
                ins.then_inc(sem("dve_chain"), 1)
                dve.wait_ge(sem("dve_chain"), chain[0])

            def release(ins, banks, name):
                ins.then_inc(*banks.freed(name))
                dve.wait_ge(*banks.released[name])

            def inv_sqrt(y, x, a, b):
                link(v.tensor_scalar(a.bitcast(I32), x.bitcast(I32), 1, None, ALU.logical_shift_right))
                link(v.tensor_scalar(y.bitcast(I32), a.bitcast(I32), -1.0, float(0x5F3759DF), ALU.mult, ALU.add))
                for _ in range(3):
                    link(v.scalar_tensor_tensor(a, y, -0.5, x, ALU.mult, ALU.mult))
                    link(v.tensor_tensor(b, a, y, ALU.mult))
                    link(v.scalar_tensor_tensor(y, b, 1.5, y, ALU.add, ALU.mult))

            def inv_rms(name):
                src = small.ready(dve, name)
                release(v.tensor_scalar(nwt[:, 0, :], src[:, 0:T], EPS, None, ALU.add), small, name)
                inv_sqrt(rstd[:, :], nwt[:, 0, :], nwt[:, 1, :], nwt[:, 2, :])

            def scaled(scale, signal):
                for k in range(KD):
                    v.scalar_tensor_tensor(hT[:, k, :], xT[:, k, :], scale[:, k:k + 1], rstd[:, 0:T], ALU.mult,
                                           ALU.mult).then_inc(sem(signal), 1)

            def head_norm(row, n, rope, signal):
                r3 = row.rearrange("p t (h d) -> p (t h) d", d=DH)
                t3 = norm_tmp.rearrange("p (n d) -> p n d", d=DH)
                link(v.tensor_tensor(t3, r3, r3, ALU.mult))
                link(v.tensor_reduce(nstat[:, 0, :], t3, AX.X, ALU.add))
                link(v.tensor_scalar(nstat[:, 1, :], nstat[:, 0, :], 1.0 / DH, EPS, ALU.mult, ALU.add))
                inv_sqrt(nstat[:, 0, :], nstat[:, 1, :], nstat[:, 2, :], nstat[:, 3, :])
                link(v.tensor_tensor(t3, r3, nstat[:, 0, :].unsqueeze(2).to_broadcast([P, TT * HEADS, DH]), ALU.mult))
                last = v.tensor_tensor(r3, t3, gain[:, n, :].unsqueeze(1).to_broadcast([P, TT * HEADS, DH]), ALU.mult)
                if not rope:
                    last.then_inc(sem(signal), 1)
                    return
                link(last)
                r4 = row.rearrange("p t (h d) -> p t h d", d=DH)
                x1, x2 = r4[:, :, :, 0:HALF], r4[:, :, :, HALF:ROT]
                c4, s4 = (z.unsqueeze(2).to_broadcast([P, TT, HEADS, HALF]) for z in (cos, sin))
                t4 = [rtmp[:, i, :].rearrange("p (t h r) -> p t h r", t=TT, h=HEADS) for i in range(4)]
                for dst, a, b in ((0, x1, c4), (1, x2, s4), (2, x2, c4), (3, x1, s4)):
                    last = v.tensor_tensor(t4[dst], a, b, ALU.mult)
                    if dst < 3:
                        last.then_inc(sem("rope_parts"), 1)
                link(last)
                dve.wait_ge(sem("rope_parts"), 3 * (n + 1))
                link(v.tensor_tensor(x1, t4[0], t4[1], ALU.subtract))
                v.tensor_tensor(x2, t4[2], t4[3], ALU.add).then_inc(sem(signal), 1)

            def score_max(tag, h, bias):
                if h >= 4:
                    small.ready(dve, f"pt{tag}{h - 4}")
                mask = causal
                if bias:
                    b = small.ready(dve, f"bias{h}")
                    mask = fmask[:, :]
                    link(v.tensor_tensor(mask[:, 0:P], causal[:, 0:P], b[:, 0:P], ALU.add))
                    release(v.tensor_tensor(mask[:, P:SC], causal[:, P:SC], b[:, 0:T], ALU.add), small, f"bias{h}")
                src = small.ready(dve, f"qk{tag}{h}")
                for t, (a, b) in enumerate(((0, P), (P, SC))):
                    ins = v.tensor_tensor_reduce(out=sp[:, h % 4, a:b], in0=src[:, a:b], in1=mask[:, a:b], scale=1.0,
                                                 scalar=-3e38, op0=ALU.add, op1=ALU.max, accum_out=amax[:, h, t:t + 1])
                    if t == 0:
                        link(ins)
                    else:
                        release(ins, small, f"qk{tag}{h}")
                v.tensor_scalar(aneg[:, h, :], amax[:, h, :], -SCALE, None, ALU.mult).then_inc(sem(f"max_ready{tag}"), 1)

            def normalise(tag, h):
                dve.wait_ge(sem(f"exp_ready{tag}"), 2 * h + 2)
                link(v.reciprocal(ainv[:, h, :], asum[:, h, :]))
                link(v.tensor_scalar(sp[:, h % 4, 0:P], sp[:, h % 4, 0:P], ainv[:, h, 0:1], None, ALU.mult))
                v.tensor_scalar(sp[:, h % 4, P:SC], sp[:, h % 4, P:SC], ainv[:, h, 1:2], None,
                                ALU.mult).then_inc(sem(f"probs_ready{tag}"), 1)

            def two_tiles(t, u):
                return t[:, 2 * u:2 * u + 2, :]

            def pair(src):
                return src.rearrange("p (j t) -> p j t", t=T)

            def merge(tag):
                dve.wait_ge(sem(f"gates_ready{tag}"), 8)
                for j in range(KD):
                    src = dense.ready(dve, f"proj{tag}{j}")
                    v.scalar_tensor_tensor(gates[:, j, :], gates[:, j, :], 1.0, src[:, 0:T], ALU.add,
                                           ALU.mult).then_inc(sem("gate_a" + tag), 1)
                    link(v.scalar_tensor_tensor(gates[:, KD + j, :], gates[:, KD + j, :], 1.0, src[:, T:2 * T], ALU.add,
                                                ALU.mult))
                    dve.wait_ge(sem("gate_a" + tag), j + 1)
                    v.tensor_tensor(merged[:, j, :], gates[:, j, :], gates[:, KD + j, :],
                                    ALU.add).then_inc(sem(f"merged_ready{tag}"), 1)

            def residual(units, factor, ready):
                for u in range(4):
                    src = dense.bank(f"{units}{u}")
                    if units != "moe":
                        dense.ready(dve, f"{units}{u}")
                    for j in range(2):
                        k = 2 * u + j
                        v.scalar_tensor_tensor(xT[:, k, :], src[:, j * T:(j + 1) * T], factor(k), xT[:, k, :], ALU.mult,
                                               ALU.add).then_inc(sem(ready), 1)

            dve.wait_ge(sem("tanh_c_ready"), 1)
            link(v.scalar_tensor_tensor(sc_c[:, 1, :], sc_c[:, 0, :], 1.0, pc("c"), ALU.add, ALU.mult))
            v.tensor_scalar(sc_c[:, 2, :], sc_c[:, 1, :], 0.5, None, ALU.mult).then_inc(sem("silu_c_ready"), 1)
            link(v.tensor_tensor(lbt[:, 4, :], pc("hg_lb_logits_2", 0, HG), pc("hg_lb_logits_2", HG, HG), ALU.max))
            link(v.tensor_tensor(lbt[:, 0, :], pc("hg_lb_logits_2", 0, HG), lbt[:, 4, :], ALU.subtract))
            v.tensor_tensor(lbt[:, 1, :], pc("hg_lb_logits_2", HG, HG), lbt[:, 4, :], ALU.subtract).then_inc(sem("lb_sub_ready"), 1)
            dve.wait_ge(sem("lb_exp_ready"), 1)
            link(v.tensor_tensor(lbt[:, 5, :], lbt[:, 2, :], lbt[:, 3, :], ALU.add))
            link(v.reciprocal(lbt[:, 6, :], lbt[:, 5, :]))
            link(v.tensor_tensor(lbt[:, 7, :], lbt[:, 2, :], lbt[:, 6, :], ALU.mult))
            link(v.tensor_scalar(lbt[:, 4, :], lbt[:, 7, :], -1.0, 1.0, ALU.mult, ALU.add))
            link(v.tensor_scalar(oghalf[:, :], pc("hg_onorm_g_2"), 0.5, None, ALU.mult))
            src = small.ready(dve, "mod_early")
            release(v.tensor_tensor(mod[:, 0:2 * KD], src[:, 0:2 * KD], pc("b_ada", 0, 2 * KD), ALU.add), small, "mod_early")
            link(v.scalar_tensor_tensor(scale1[:, :], mod[:, KD:2 * KD], 1.0, pc("g_norm1"), ALU.add, ALU.mult))
            inv_rms("ms_norm1")
            scaled(scale1, "h1_scaled")
            dve.wait_ge(sem("gain_in"), 64)
            dve.wait_ge(sem("q_rows"), 2)
            head_norm(qrow, 0, True, "q_normed")
            dve.wait_ge(sem("k_rows"), 2)
            head_norm(krow, 1, True, "k_normed")
            dve.wait_ge(sem("pad_ready"), 1)

            def conv(c):
                w = lambda tap: pc("conv_w", tap * CT + c, 1)
                link(v.tensor_scalar(xbT[:, c, :], uT[:, c, 0:T], w(0), pc("conv_b", c, 1), ALU.mult, ALU.add))
                for tap in (1, 2):
                    link(v.scalar_tensor_tensor(xbT[:, c, :], uT[:, c, tap:tap + T], w(tap), xbT[:, c, :], ALU.mult, ALU.add))

            for n in range(HEADS + 1):
                if n in (2, 3):
                    u = n - 2
                    src = dense.ready(dve, f"cg{u}")
                    dve.wait_ge(sem("xb_ready"), u + 1)
                    release(v.tensor_tensor(uT[:, 2 * u:2 * u + 2, 2:T + 2], pair(src), two_tiles(xbT, u), ALU.mult), dense, f"cg{u}")
                if n in (4, 5):
                    u = n - 4
                    src = dense.ready(dve, f"bg{u}")
                    v.tensor_tensor(two_tiles(ybT, u), pair(src), two_tiles(xbT, u), ALU.mult).then_inc(sem("yb_ready"), 1)
                if n < HEADS:
                    score_max("", n, False)
                if n >= 1:
                    normalise("", n - 1)
                if n in (2, 3):
                    conv(2 * (n - 2))
                    conv(2 * (n - 2) + 1)
            src = dense.ready(dve, "mod_late")
            release(v.tensor_tensor(mod[:, 2 * KD:], src[:, 0:4 * KD], pc("b_ada", 2 * KD, 4 * KD), ALU.add), dense, "mod_late")
            link(v.scalar_tensor_tensor(scale2[:, :], mod[:, 4 * KD:5 * KD], 1.0, pc("g_norm2"), ALU.add, ALU.mult))
            link(v.tensor_scalar(ga1h[:, :], mod[:, 2 * KD:3 * KD], 0.5, None, ALU.mult))
            merge("")
            residual("wo", lambda k: ga1h[:, k:k + 1], "x1_ready")
            v.memset(zeros, 0.0).then_inc(sem("zeros_ready"), 1)
            inv_rms("ms_norm2")
            scaled(scale2, "h2_scaled")
            src = small.ready(dve, "logits")
            dve.wait_ge(sem("route_in"), 64)
            release(v.tensor_tensor(lg[:, :, :], src.rearrange("p (t n) -> p t n", n=64)[:, 0:TT, 0:GROUPS + EXPERTS],
                                 br[:, :].unsqueeze(1).to_broadcast([P, TT, GROUPS + EXPERTS]), ALU.add), small, "logits")
            index = cst[:, C_IOTA:C_IOTA + EXPERTS].unsqueeze(1)

            def wide_(a, n):
                return a.unsqueeze(2).to_broadcast([P, TT, n])

            def first_max(values, n, best, one_hot, tmp, least):
                link(v.tensor_reduce(best, values, AX.X, ALU.max))
                link(v.tensor_tensor(tmp, values, wide_(best, n), ALU.is_equal))
                link(v.scalar_tensor_tensor(tmp, tmp, -64.0, index[:, :, 0:n].to_broadcast([P, TT, n]), ALU.mult, ALU.add))
                link(v.tensor_reduce(least, tmp, AX.X, ALU.min))
                link(v.tensor_tensor(one_hot, tmp, wide_(least, n), ALU.is_equal))

            g, e = lg[:, :, 0:GROUPS], lg[:, :, GROUPS:]
            gsel = rt[:, 1, :, 0:GROUPS]
            first_max(g, GROUPS, r1[:, 0, :], gsel, rt[:, 2, :, 0:GROUPS], r1[:, 1, :])
            v.tensor_tensor(rt[:, 7, :, 0:GROUPS], g, wide_(r1[:, 0, :], GROUPS), ALU.subtract).then_inc(sem("route_sub_ready"), 1)
            link(v.tensor_scalar(rt[:, 2, :, 0:GROUPS], gsel, BIG, -BIG, ALU.mult, ALU.add))

            def by_group(a):
                return a.rearrange("p t (g n) -> p t g n", g=GROUPS)

            def per_group(a):
                return a.unsqueeze(3).to_broadcast([P, TT, GROUPS, PER_GROUP])

            link(v.tensor_tensor(by_group(rt[:, 3, :, :]), by_group(e), per_group(gsel), ALU.mult))
            link(v.tensor_tensor(by_group(rt[:, 4, :, :]), by_group(rt[:, 3, :, :]), per_group(rt[:, 2, :, 0:GROUPS]), ALU.add))
            first_max(rt[:, 4, :, :], EXPERTS, r1[:, 2, :], rt[:, 1, :, :], rt[:, 3, :, :], r1[:, 1, :])
            link(v.scalar_tensor_tensor(rt[:, 5, :, :], rt[:, 1, :, :], -2.0 * BIG, rt[:, 4, :, :], ALU.mult, ALU.add))
            first_max(rt[:, 5, :, :], EXPERTS, r1[:, 3, :], rt[:, 2, :, :], rt[:, 3, :, :], r1[:, 1, :])
            v.tensor_tensor(rt[:, 0, :, :], rt[:, 1, :, :], rt[:, 2, :, :], ALU.add).then_inc(sem("chosen_ready"), 1)
            v.tensor_tensor(r1[:, 5, :], r1[:, 3, :], r1[:, 2, :], ALU.subtract).then_inc(sem("second_ready"), 1)
            dve.wait_ge(sem("route_exp_ready"), 1)
            link(v.tensor_reduce(r1[:, 7, :], rt[:, 6, :, 0:GROUPS], AX.X, ALU.add))
            dve.wait_ge(sem("second_exp_ready"), 1)
            link(v.tensor_scalar(r1[:, 8, :], r1[:, 6, :], 1.0, None, ALU.add))
            link(v.tensor_tensor(r1[:, 9, :], r1[:, 7, :], r1[:, 8, :], ALU.mult))
            link(v.reciprocal(r1[:, 10, :], r1[:, 9, :]))
            link(v.tensor_tensor(r1[:, 11, :], r1[:, 10, :], r1[:, 6, :], ALU.mult))
            link(v.tensor_tensor(rt[:, 3, :, :], rt[:, 1, :, :], wide_(r1[:, 10, :], EXPERTS), ALU.mult))
            link(v.tensor_tensor(rt[:, 4, :, :], rt[:, 2, :, :], wide_(r1[:, 11, :], EXPERTS), ALU.mult))
            link(v.memset(wgt[:, :, :], 0.0))
            for r in range(1 + EXTRA_ROUNDS):
                link(v.tensor_tensor(wgt[:, :, r * EXPERTS:(r + 1) * EXPERTS], rt[:, 3, :, :], rt[:, 4, :, :], ALU.add))
            link(v.memset(rank[:, :, :], -1.0))
            src = small.ready(dve, "rank")
            link(v.scalar_tensor_tensor(rt[:, 3, :, :], src[:, 0:TT * EXPERTS].rearrange("p (t n) -> p t n", t=TT), 1.0,
                                        rt[:, 0, :, :], ALU.add, ALU.mult))
            release(v.tensor_reduce(flagf[:, 0:1], src[0:1, 64:96], AX.X, ALU.max), small, "rank")
            for r in range(1 + EXTRA_ROUNDS):
                link(v.tensor_scalar(rank[:, :, r * EXPERTS:(r + 1) * EXPERTS], rt[:, 3, :, :], -1.0 - CAP * r, None, ALU.add))
            v.tensor_scalar(flag[:, :], flagf[:, 0:1], float(CAP), None, ALU.is_gt).then_inc(sem("flag_ready"), 1)

            def experts(pre, first_round, rounds):
                col0 = first_round * EXPERTS

                def one_hot(dst, at, col, weighted=False):
                    for t in range(TT):
                        place = rank[:, t, bass.ds(col, 1)]
                        if weighted:
                            last = v.tensor_scalar(dst[:, t, at:at + CAP], iota, place, wgt[:, t, bass.ds(col, 1)],
                                                   ALU.is_equal, ALU.mult)
                        else:
                            last = v.tensor_scalar(dst[:, t, at:at + CAP], iota, place, None, ALU.is_equal)
                        if t < TT - 1:
                            last.then_inc(sem(pre + "one_hot_parts"), 1)
                    return last

                def hidden(e_, done):
                    dve.wait_ge(sem(pre + "sil_ready"), done)
                    v.tensor_tensor(hid[e_].rearrange("p f c -> p (f c)"), sil[e_], H[:, T:2 * T],
                                    ALU.mult).then_inc(sem(pre + "hid_ready"), 1)

                one_hot(Sa, 0, col0).then_inc(sem(pre + "sa_ready"), 1)
                one_hot(Sb, 0, col0 + 1).then_inc(sem(pre + "sb_ready"), 1)
                with dve.Fori(0, PAIRS * rounds) as i:
                    one_hot(Sw, 0, 2 * i + col0, True).then_inc(sem(pre + "one_hot_parts"), 1)
                    one_hot(Sw, CAP, 2 * i + col0 + 1, True).then_inc(sem(pre + "sw_ready"), 1)
                    hidden(0, 2 * i + 1)
                    one_hot(Sa, 0, 2 * i + col0 + 2).then_inc(sem(pre + "sa_ready"), 1)
                    dve.wait_ge(sem(pre + "st_done"), i + 1)
                    v.tensor_copy(ST, Y1[:, 0:T]).then_inc(sem(pre + "st_ready"), 1)
                    dve.wait_ge(sem(pre + "gather_done"), 2 * i + 2)
                    one_hot(Sb, 0, 2 * i + col0 + 3).then_inc(sem(pre + "sb_ready"), 1)
                    hidden(1, 2 * i + 2)
                    dve.wait_ge(sem(pre + "ys_done"), 2 * i + 1)
                    v.tensor_copy(ys[:, 0:512], Y0).then_inc(sem(pre + "ys0_ready"), 1)
                dve.wait_ge(sem(pre + "combined"), PAIRS * rounds)

            experts("moe_", 0, 1)
            more = dve.value_load(flag[0:1, 0:1], min_val=0, max_val=1)
            with dve.If(more > 0):
                experts("spare_", 1, EXTRA_ROUNDS)
            residual("moe", lambda k: mod[:, 5 * KD + k:5 * KD + k + 1], "x2_ready")
            inv_rms("ms_mix")
            scaled(pc("norm_mix_g_2"), "hm_ready")
            src = small.ready(dve, "fox_f")
            dve.wait_ge(sem("fox_in"), 32)
            release(v.tensor_scalar(fl[:, 0, :], src[0:HEADS, 0:T], fbias[:, 0:1], None, ALU.add), small, "fox_f")
            v.scalar_tensor_tensor(fl[:, 1, :], fl[:, 0, :], -1.0, fl[:, 0, :], ALU.mult, ALU.max).then_inc(sem("fox_abs_ready"), 1)
            link(v.tensor_scalar(fl[:, 0, :], fl[:, 0, :], 0.0, None, ALU.min))
            dve.wait_ge(sem("fox_ln_ready"), 1)
            link(v.tensor_tensor(fl[:, 1, :], fl[:, 0, :], fl[:, 2, :], ALU.subtract))
            link(v.tensor_tensor_scan(fl[:, 2, :], ones[0:HEADS, 0:1].to_broadcast([HEADS, T]), fl[:, 1, :], 0.0, ALU.mult, ALU.add))
            v.tensor_scalar(foxc[:, :], fl[:, 2, :], -1.0 / SCALE, None, ALU.mult).then_inc(sem("fox_c_ready"), 1)
            dve.wait_ge(sem("hf_exp"), 2)
            fg = QE[0]
            link(v.tensor_scalar(khT, khT, 1.0, None, ALU.add))
            link(v.reciprocal(fg, khT))
            for h in range(HG):
                last = v.tensor_scalar(fg[:, h, :], fg[:, h, :], lbt[:, 4, h:h + 1], lbt[:, 7, h:h + 1], ALU.mult, ALU.add)
                if h < HG - 1:
                    last.then_inc(sem("fg_parts"), 1)
            link(last)
            dve.wait_ge(sem("fg_parts"), HG - 1)
            v.tensor_scalar(khT, fg, -0.5, 0.5, ALU.mult, ALU.add).then_inc(sem("fg_ready"), 1)
            dve.wait_ge(sem("logf_ready"), 1)
            for h in range(HG):
                for t in range(TT):
                    last = v.tensor_tensor_scan(bT[:, h, t * P:(t + 1) * P], ones, fg[:, h, t * P:(t + 1) * P], 0.0,
                                                ALU.mult, ALU.add)
                    if (h, t) != (HG - 1, TT - 1):
                        last.then_inc(sem("scans"), 1)
            link(last)
            dve.wait_ge(sem("scans"), HG * TT - 1)
            for u in range(2):
                src = dense.ready(dve, f"hq{u}")
                dve.wait_ge(sem("hq_tanh"), u + 1)
                release(v.scalar_tensor_tensor(two_tiles(qhT, u), two_tiles(qhT, u), 1.0, pair(src), ALU.add, ALU.mult), dense, f"hq{u}")

            def differences(n):
                name = level_names[n]
                if n >= 2:
                    dve.wait_ge(sem("ke_ready"), n - 1)
                    dve.wait_ge(sem("qe_ready"), n - 1)
                if name == "cross":
                    b, d = bT, E[n % 2]
                    v.tensor_tensor(d[:, :, 0:P], b[:, :, P - 1:P].to_broadcast([P, HG, P]), b[:, :, 0:P],
                                    ALU.subtract).then_inc(sem("left_parts"), 1)
                    last = v.tensor_copy(d[:, :, P:T], b[:, :, P:T])
                else:
                    m = int(name[3:])
                    b, d = (z.rearrange("p h (n two m) -> p (h n) two m", two=2, m=m) for z in (bT, E[n % 2]))
                    mid = b[:, :, 0, m - 1:m].to_broadcast([P, HG * T // (2 * m), m])
                    v.tensor_tensor(d[:, :, 0, :], mid, b[:, :, 0, :], ALU.subtract).then_inc(sem("left_parts"), 1)
                    last = v.tensor_tensor(d[:, :, 1, :], b[:, :, 1, :], mid, ALU.subtract)
                dve.wait_ge(sem("left_parts"), n + 1)
                last.then_inc(sem("diff_ready"), 1)

            def decayed_queries(n):
                dve.wait_ge(sem("decay_ready"), n + 1)
                if n >= 2:
                    small.ready(dve, level_units[level_names[n - 2]][-1])
                v.tensor_tensor(QE[n % 2], qhT, E[n % 2], ALU.mult).then_inc(sem("qe_ready"), 1)

            def scores_out(n):
                name = level_names[n]
                if name == "cross":
                    src = small.ready(dve, "cross")
                    release(v.tensor_copy(scX.rearrange("p h t -> p (h t)"), src), small, "cross")
                    return
                at = C_IDENT if name == "diag" else C_LEVEL + (n - 1) * P
                mask = cst[:, at:at + P].bitcast(I32).unsqueeze(1).to_broadcast([P, 4, P])
                for u, unit in enumerate(level_units[name]):
                    src = small.ready(dve, unit)
                    release(v.copy_predicated(scT[:, 4 * u:4 * u + 4, :], mask, src.rearrange("p (n t) -> p n t", t=P)), small, unit)

            dve.wait_ge(sem("scores_zeroed"), 1)
            n_levels = len(level_names)
            for step in range(n_levels + 1):
                if step < n_levels - 1:
                    differences(step)
                if 1 <= step < n_levels:
                    decayed_queries(step - 1)
                if step >= 2:
                    scores_out(step - 2)
                if step == 2:
                    dve.wait_ge(sem("fq_rows"), 2)
                    head_norm(qrow, 2, False, "q_normed_b")
                if step == 4:
                    dve.wait_ge(sem("fk_rows"), 2)
                    head_norm(krow, 3, False, "k_normed_b")
            scores_out(n_levels - 1)
            for u in range(2):
                src = dense.ready(dve, f"hg{u}")
                dve.wait_ge(sem("hg_tanh"), u + 1)
                release(v.scalar_tensor_tensor(two_tiles(sgT, u), two_tiles(sgT, u), 1.0, pair(src), ALU.add, ALU.mult), dense, f"hg{u}")

            def hgrn_out():
                for h in range(HG):
                    u, j = divmod(h, 2)
                    src = small.ready(dve, f"ms_h{u}")
                    ins = v.tensor_scalar(nwt[:, 0, :], src[:, j * T:(j + 1) * T], EPS, None, ALU.add)
                    if j == 0:
                        link(ins)
                    else:
                        release(ins, small, f"ms_h{u}")
                    inv_sqrt(rstd[:, :], nwt[:, 0, :], nwt[:, 1, :], nwt[:, 2, :])
                    dve.wait_ge(sem("ho_ready"), u + 1)
                    link(v.scalar_tensor_tensor(hoT[:, h, :], hoT[:, h, :], oghalf[:, 0:1], rstd[:, :], ALU.mult, ALU.mult))
                    v.tensor_tensor(yaT[:, h, :], hoT[:, h, :], sgT[:, h, :], ALU.mult).then_inc(sem("ya_ready_b"), 1)

            for n in range(HEADS + 1):
                if n < HEADS:
                    score_max("_b", n, True)
                if n >= 1:
                    normalise("_b", n - 1)
                if n == 1:
                    hgrn_out()
            merge("_b")
            residual("wo_b", lambda k: 0.5, "x3_ready")
            inv_rms("ms_ffn")
            scaled(pc("norm_ffn_g_2"), "hf_ready")
            for f in range(FFT):
                src = dense.bank(f"ffn{f}")
                dve.wait_ge(sem("fsil_ready"), f + 1)
                v.tensor_tensor(act[:, f, :], fsil[:, f % 2, :], src[:, T:2 * T], ALU.mult).then_inc(sem("act_ready"), 1)
            residual("down", lambda k: 1.0, "x4_ready")
            inv_rms("ms_ple")
            scaled(pc("norm_ple_g_2"), "hp_ready")
            for j in range(KD):
                dve.wait_ge(sem("thp_ready"), j + 1)
                src = dense.ready(dve, f"ple{j}")
                release(v.scalar_tensor_tensor(oT[:, j, :], thp[j % 2], 1.0, src[:, T:2 * T], ALU.add, ALU.mult), dense, f"ple{j}")
                v.scalar_tensor_tensor(oT[:, j, :], oT[:, j, :], 0.5, xT[:, j, :], ALU.mult, ALU.add).then_inc(sem("o_ready"), 1)


_INS = ["x", "c", "w_ada", "b_ada", "g_norm1", "g_norm2", "w_in", "g_q", "g_k", "conv_w", "conv_b", "w_pa", "w_pb",
        "w_o", "w_rg", "b_rg", "w_re", "b_re", "w1", "w3", "w2", "p_2", "norm_mix_g_2", "w_in_2", "hg_lb_logits_2",
        "hg_onorm_g_2", "fox_f_bias_2", "fox_q_norm_g_2", "fox_k_norm_g_2", "w_branch_a_2", "w_branch_b_2", "w_out_2",
        "norm_ffn_g_2", "w_ffn_gate_2", "w_ffn_up_2", "w_ffn_down_2", "norm_ple_g_2", "w_ple_gate_2", "w_ple_proj_2"]


def kernel(**inputs):
    import concourse.bacc as _bacc
    from concourse.bass_utils import run_bass_kernel_spmd as _run

    nc = _bacc.Bacc("TRN2", target_bir_lowering=False, num_devices=1)
    arrays, args = {}, {}
    for name in _INS:
        a = np.ascontiguousarray(inputs[name])
        arrays[f"in_{name}"] = a
        args[name] = nc.dram_tensor(f"in_{name}", a.shape, mybir.dt.from_np(a.dtype), kind="ExternalInput").ap()
    arrays["constants"] = constant_table()
    consts = nc.dram_tensor("constants", (P, C_ALL), F32, kind="ExternalInput").ap()
    out = nc.dram_tensor("out", (1, T, D), F32, kind="ExternalOutput").ap()
    two_blocks(nc, args, consts, out)
    r = _run(nc, [arrays], core_ids=[0])
    return r.results[0]["out"]
```

```python
from contextlib import ExitStack

import concourse.bass as bass
from concourse import mybir
import numpy as np

F32 = mybir.dt.float32
I32 = mybir.dt.int32
ALU = mybir.AluOpType
ACT = mybir.ActivationFunctionType
AX = mybir.AxisListType

P = 128
D = 1024
KD = D // P
T = 256
TT = T // P
HEADS = 8
DH = 64
ROT = DH // 4
HALF = ROT // 2
CW = 512
CT = CW // P
GROUPS = 4
PER_GROUP = 8
EXPERTS = GROUPS * PER_GROUP
PAIRS = EXPERTS // 2
ADA = 12
ADA_EARLY = 4
FE = 512
FT = FE // P
CAP = 64
EXTRA_ROUNDS = T // CAP - 1
DFF = 2816
FFT = DFF // P
PLE = 256
HG = 4
EPS = 1e-6
SCALE = DH ** -0.5
BIG = 1e30
COL = 512
SLOTS = 6
SLOT = KD * COL
LEVELS = [64, 32, 16, 8, 4, 2, 1]
SC = 3 * P

C_IDENT = 0
C_MEAN_D = C_IDENT + P
C_MEAN_V = C_MEAN_D + P
C_ONES = C_MEAN_V + P
C_CAUSAL = C_ONES + P
C_BEFORE = C_CAUSAL + SC
C_LEVEL = C_BEFORE + P
C_IOTA = C_LEVEL + len(LEVELS) * P
C_COS = C_IOTA + CAP
C_SIN = C_COS + TT * HALF
C_ALL = C_SIN + TT * HALF

PARAM_ROWS = [("c", KD), ("b_ada", 6 * KD), ("g_norm1", KD), ("g_norm2", KD), ("conv_w", 3 * CT), ("conv_b", CT),
              ("norm_mix_g_2", KD), ("hg_lb_logits_2", 2 * HG), ("hg_onorm_g_2", 1), ("norm_ffn_g_2", KD),
              ("norm_ple_g_2", KD)]
PARAM_AT = {}
PARAM_N = 0
for _name, _rows in PARAM_ROWS:
    PARAM_AT[_name] = PARAM_N
    PARAM_N += _rows


def constant_table():
    c = np.zeros((P, C_ALL), np.float32)
    i = np.arange(P)
    c[:, C_IDENT:C_IDENT + P] = np.eye(P)
    c[:, C_MEAN_D:C_MEAN_D + P] = 1.0 / D
    c[:, C_MEAN_V:C_MEAN_V + P] = 1.0 / P
    c[:, C_ONES:C_ONES + P] = 1.0
    causal = np.where(i[None, :] <= i[:, None], 0.0, -BIG)
    c[:, C_CAUSAL:C_CAUSAL + P] = causal
    c[:, C_CAUSAL + 2 * P:C_CAUSAL + 3 * P] = causal
    c[:, C_BEFORE:C_BEFORE + P] = i[:, None] < i[None, :]
    for n, m in enumerate(LEVELS):
        same = i[:, None] // (2 * m) == i[None, :] // (2 * m)
        c[:, C_LEVEL + n * P:C_LEVEL + (n + 1) * P] = same & (i[:, None] % (2 * m) < m) & (i[None, :] % (2 * m) >= m)
    c[:, C_IOTA:C_IOTA + CAP] = np.arange(CAP)
    freq = np.float32(500000.0) ** (-np.arange(0, ROT, 2, dtype=np.float32) / np.float32(ROT))
    angle = np.arange(T, dtype=np.float32)[:, None] * freq[None, :]
    for table, at in ((np.cos(angle), C_COS), (np.sin(angle), C_SIN)):
        c[:, at:at + TT * HALF] = table.reshape(TT, P, HALF).transpose(1, 0, 2).reshape(P, TT * HALF)
    return c


class Rotation:

    def __init__(self, psum, first, count, order, done, free, released, uncounted=()):
        self.psum, self.first, self.count, self.done, self.free = psum, first, count, done, free
        self.index = {name: n for n, name in enumerate(order)}
        assert len(self.index) == len(order)
        self.order, self.claimed = order, 0
        self.done_at, self.released = {}, {}
        freed, done_n = [0] * count, 0
        for n, name in enumerate(order):
            done_n += name not in uncounted
            self.done_at[name] = done_n
            if name in released:
                self.released[name] = released[name]
            else:
                freed[n % count] += 1
                self.released[name] = free[n % count], freed[n % count]

    def bank(self, name):
        return self.psum[:, self.first + self.index[name] % self.count, :]

    def claim(self, pe, name):
        assert self.index[name] == self.claimed, (name, self.order[self.claimed])
        self.claimed += 1
        if self.index[name] >= self.count:
            pe.wait_ge(*self.released[self.order[self.index[name] - self.count]])
        return self.bank(name)

    def ready(self, engine, name):
        engine.wait_ge(self.done, self.done_at[name])
        return self.bank(name)

    def freed(self, name):
        assert self.released[name][0] is self.free[self.index[name] % self.count]
        return self.released[name][0], 1


def two_blocks(nc, A, consts, out):
    with ExitStack() as ctx:
        def sb(name, shape, dt=F32):
            return ctx.enter_context(nc.sbuf_tensor(name, shape, dt))

        sems = {}

        def sem(name):
            if name not in sems:
                sems[name] = ctx.enter_context(nc.semaphore(name))
            return sems[name]

        ps = ctx.enter_context(nc.psum_tensor("ps", [P, 8, 512], F32))
        ring = sb("ring", [P, SLOTS, SLOT])
        cst = sb("cst", [P, C_ALL])
        prow = sb("prow", [P, P])
        pcol = sb("pcol", [P, PARAM_N])
        xT = sb("xT", [P, KD, T])
        hT = sb("hT", [P, KD, T])
        sq = sb("sq", [P, KD, T])
        rows = sb("rows", [P, TT, D])
        arena = sb("arena", [P, 24 * T])
        uT = sb("uT", [P, CT, T + 2])
        ybT = sb("ybT", [P, CT, T])
        yaT = sb("yaT", [P, CT, T])
        gates = sb("gates", [P, 2 * KD, T])
        sp = sb("sp", [P, 4, SC])
        pT = sb("pT", [P, 2, SC])
        wr = sb("wr", [P, KD, GROUPS + EXPERTS])
        wfox = sb("wfox", [P, KD, HEADS])
        br = sb("br", [P, GROUPS + EXPERTS])
        gain = sb("gain", [P, 4, DH])
        fbias = sb("fbias", [HEADS, 1])
        rstd = sb("rstd", [P, T])
        nwt = sq[:, 4:7, :]
        sc_c = sb("sc_c", [P, 3, KD])
        mod = sb("mod", [P, 6 * KD])
        scale1 = sb("scale1", [P, KD])
        scale2 = sb("scale2", [P, KD])
        ga1h = sb("ga1h", [P, KD])
        oghalf = sb("oghalf", [P, 1])
        lbt = sb("lbt", [P, 8, HG])
        nstat = sb("nstat", [P, 4, TT * HEADS])
        amax = sb("amax", [P, HEADS, 2])
        aneg = sb("aneg", [P, HEADS, 2])
        asum = sb("asum", [P, HEADS, 2])
        ainv = sb("ainv", [P, HEADS, 2])
        lg = sb("lg", [P, TT, GROUPS + EXPERTS])
        r1 = sb("r1", [P, 12, TT])
        rank = sb("rank", [P, TT, (1 + EXTRA_ROUNDS) * EXPERTS + 2])
        wgt = sb("wgt", [P, TT, (1 + EXTRA_ROUNDS) * EXPERTS + 2])
        flagf = sb("flagf", [1, 2])
        flag = sb("flag", [1, 1], I32)
        foxc = sb("foxc", [HEADS, T])

        ident = cst[:, C_IDENT:C_IDENT + P]
        mean_d = cst[:, C_MEAN_D:C_MEAN_D + P]
        mean_v = cst[:, C_MEAN_V:C_MEAN_V + P]
        ones = cst[:, C_ONES:C_ONES + P]
        causal = cst[:, C_CAUSAL:C_CAUSAL + SC]
        before = cst[:, C_BEFORE:C_BEFORE + P]
        iota = cst[:, C_IOTA:C_IOTA + CAP]
        cos = cst[:, C_COS:C_COS + TT * HALF].rearrange("p (t r) -> p t r", t=TT)
        sin = cst[:, C_SIN:C_SIN + TT * HALF].rearrange("p (t r) -> p t r", t=TT)

        def pc(name, at=0, n=None):
            a = PARAM_AT[name] + at
            return pcol[:, a:a + (dict(PARAM_ROWS)[name] if n is None else n)]

        def part(at, tiles):
            return arena[:, at * T:(at + tiles) * T]

        qrow = part(0, 4).rearrange("p (t c) -> p t c", t=TT)
        krow = part(4, 4).rearrange("p (t c) -> p t c", t=TT)
        vrow = part(8, 4).rearrange("p (t c) -> p t c", t=TT)
        qT = part(12, 4).rearrange("p (c t) -> p c t", t=T)
        kT = part(16, 4).rearrange("p (c t) -> p c t", t=T)
        xbT = part(20, 4).rearrange("p (c t) -> p c t", t=T)
        sp_flat = sp[:, :, :].rearrange("p a b -> p (a b)")
        norm_tmp = sp_flat[:, 0:2 * CW]
        rtmp = sp_flat[:, 2 * CW:].rearrange("p (n r) -> p n r", n=4)
        fl = sp_flat[0:HEADS, 0:3 * T].rearrange("p (n t) -> p n t", n=3)
        merged = gates[:, 0:KD, :]
        S = part(0, 1).rearrange("p (t c) -> p t c", t=TT)
        Sw = part(1, 1).rearrange("p (t c) -> p t c", t=TT)
        ST = part(2, 1)
        xs = part(4, 4).rearrange("p (k c) -> p k c", k=KD)
        sil = part(8, 2)
        hid = part(10, 2)
        hidT = part(12, 2).rearrange("p (f c) -> p f c", f=FT)
        ys = part(14, 4)
        zeros = part(18, 2)
        khT = xbT
        bT = uT[:, :, :].rearrange("p c t -> p (c t)")[:, 0:HG * T].rearrange("p (h t) -> p h t", h=HG)
        qhT = rows[:, 0, :].rearrange("p (h t) -> p h t", h=HG)
        irow = rows[:, 1, :].rearrange("p (t c) -> p t c", t=TT)
        E = [sq[:, 4 * n:4 * n + 4, :] for n in range(2)]
        QE = [gates[:, 4 * n:4 * n + 4, :] for n in range(2)]
        KE = [gates[:, 8 + 4 * n:12 + 4 * n, :] for n in range(2)]
        hoT = khT
        hsq = E[0]
        sgT = yaT
        scT = ybT[:, :, :].rearrange("p c t -> p (c t)").rearrange("p (n t) -> p n t", t=P)
        scX = pT[:, :, :].rearrange("p a b -> p (a b)")[:, 0:HG * P].rearrange("p (h t) -> p h t", t=P)
        fmask = rows[:, 0, 0:SC]
        rt = uT[:, :, :].rearrange("p c t -> p (c t)")[:, 0:8 * TT * EXPERTS].rearrange("p (n t e) -> p n t e", t=TT, e=EXPERTS)
        act = arena[:, 0:FFT * T].rearrange("p (f t) -> p f t", t=T)
        fsil = sp[:, 0:2, 0:T]
        prows = yaT[:, 0:2, :]
        ppT = ybT[:, 0:2, :]
        thp = [sp[:, n, 0:T] for n in range(2)]
        oT = gates[:, 0:KD, :]
        orow = rows

        dense_order = []
        for name in ("q", "k", "v", "xb", "cg", "bg"):
            dense_order += [f"{name}{u}" for u in range(2)]
        dense_order += [f"gate{u}" for u in range(8)] + [f"proj{j}" for j in range(KD)]
        dense_order += [f"wo{u}" for u in range(4)] + [f"moe{u}" for u in range(4)]
        for name in ("hf", "hq", "hi", "fq", "fk", "fv", "hg"):
            dense_order += [f"{name}{u}" for u in range(2)]
        dense_order += [f"gate_b{u}" for u in range(8)] + [f"proj_b{j}" for j in range(KD)]
        dense_order += [f"wo_b{u}" for u in range(4)] + [f"ffn{f}" for f in range(FFT)]
        dense_order += [f"down{u}" for u in range(4)] + [f"ple{j}" for j in range(KD)]

        def attention_order(steps, tag, bias):
            for n in range(HEADS + 3):
                names = []
                if n < HEADS:
                    names += [f"bias{n}"] * bias + [f"qk{tag}{n}"]
                if 0 <= n - 2 < HEADS:
                    names.append(f"pt{tag}{n - 2}")
                if 0 <= n - 3 < HEADS:
                    names.append(f"pv{tag}{n - 3}")
                steps.append(names)
            return steps

        att1 = attention_order([], "", False)
        att2 = attention_order([], "_b", True)
        small_order = ["params"] + [f"x{i}" for i in range(4)] + ["ms_norm1"] + [f"ada{c}" for c in range(ADA_EARLY)]
        ada_after = {4: "k1", 5: "v0", 6: "v1", 7: "xb0", 8: "xb1", 9: "cg0", 10: "gate0", 11: "gate1"}
        ada_at = {name: c for c, name in ada_after.items()}
        after1 = {"v0": ["tq0", "tq1"], "v1": ["tk0", "tk1"]}
        for n, names in enumerate(att1):
            after1.setdefault(f"{('xb', 'cg', 'bg')[n // 2]}{n % 2}" if n < 6 else f"gate{n - 6}", []).extend(names)
        for name in dense_order:
            small_order += after1.get(name, []) + ([f"ada{ada_at[name]}"] if name in ada_at else [])
        small_order += ["ms_norm2", "logits"] + [f"h2r{i}" for i in range(4)] + ["rank"]
        n_block1 = len(small_order)
        small_order += ["ms_mix", "fox_f"]
        level_names = ["cross"] + [f"lev{m}" for m in LEVELS] + ["diag"]
        level_units = {n: ["cross"] if n == "cross" else [n + "a", n + "b"] for n in level_names}
        after2 = {}
        slots2 = ["fq0", "fq1", "fk0", "fk1", "fv0", "fv1", "hg0", "hg1", "hg1"]
        for n, at in zip(level_names, slots2):
            after2.setdefault(at, []).append(level_units[n])
        after2["fk0"].append(["tq_b0", "tq_b1"])
        after2["fv0"].append(["tk_b0", "tk_b1"])
        for n, names in enumerate(att2):
            after2.setdefault(f"gate_b{min(n, 7)}", []).append(names)
        after2["gate_b0"].insert(0, ["ho0", "ho1"])
        after2["gate_b1"].insert(0, ["ms_h0", "ms_h1"])
        for name in dense_order:
            for names in after2.get(name, []):
                small_order += names
        small_order += ["ms_ffn", "ms_ple", "pp", "o00", "o10", "o01", "o11"]

        dense_released = {f"moe{u}": (sem("x2_ready"), 2 * u + 2) for u in range(4)}
        for u in range(2):
            for name in ("q", "k", "v", "fq", "fk", "fv"):
                dense_released[f"{name}{u}"] = sem(f"{name}_rows"), u + 1
            for name, ready in (("xb", "xb_ready"), ("bg", "yb_ready"), ("hf", "hf_exp"), ("hi", "hi_ready")):
                dense_released[f"{name}{u}"] = sem(ready), u + 1
        for tag in ("", "_b"):
            for n in range(8):
                dense_released[f"gate{tag}{n}"] = sem(f"gates_ready{tag}"), n + 1
                dense_released[f"proj{tag}{n}"] = sem(f"merged_ready{tag}"), n + 1
        for u in range(4):
            for name, ready in (("wo", "x1_ready"), ("wo_b", "x3_ready"), ("down", "x4_ready")):
                dense_released[f"{name}{u}"] = sem(ready), 2 * u + 2
        for f in range(FFT):
            dense_released[f"ffn{f}"] = sem("act_ready"), f + 1
        small_released = {"params": (sem("pcol_ready"), 1), "pp": (sem("ppT_ready"), 1)}
        for i in range(4):
            small_released[f"x{i}"] = sem("xT_ready"), i + 1
            small_released[f"h2r{i}"] = sem("h2_rows_ready"), i + 1
        for n, name in enumerate(("o00", "o10", "o01", "o11")):
            small_released[name] = sem("out_ready"), n + 1
        for u in range(2):
            small_released[f"ho{u}"] = sem("ho_ready"), u + 1
            for tag in ("", "_b"):
                small_released[f"tq{tag}{u}"] = sem("qT_ready" + tag), u + 1
                small_released[f"tk{tag}{u}"] = sem("kT_ready" + tag), u + 1
        for c in range(ADA):
            small_released[f"ada{c}"] = sem("mod_raw"), c + 1
        for h in range(HEADS):
            for tag, y in (("", "ya_ready"), ("_b", "yb_ready_b")):
                small_released[f"pt{tag}{h}"] = sem("pT_ready" + tag), h + 1
                small_released[f"pv{tag}{h}"] = sem(y), h + 1
        dense = Rotation(ps, 0, 4, dense_order, sem("dense_done"), [sem(f"dense_free{b}") for b in range(4)],
                         dense_released, [f"moe{u}" for u in range(4)])
        small = Rotation(ps, 4, 4, small_order, sem("small_done"), [sem(f"small_free{b}") for b in range(4)],
                         small_released)
        GA, GB, HA, HB = (ps[:, 4 + b, :] for b in range(4))

        chunks = []
        chunk_of = {}

        def cols(w, at, n=COL):
            return w[:, at:at + n].rearrange("(k p) n -> p k n", p=P)

        def chunk(name, loads, released):
            chunk_of[name] = len(chunks)
            chunks.append((loads, released))

        def wide(slot):
            return ring[:, slot, :].rearrange("p (k n) -> p k n", k=KD)

        def tall(slot):
            return ring[:, slot, :].rearrange("p (k n) -> p k n", n=D)

        def after(unit):
            return dense.done, dense.done_at[unit]

        w_ada, w_in, w_in2 = A["w_ada"][0], A["w_in"][0], A["w_in_2"][0]

        def ada(n):
            chunk(f"ada{n}", [(lambda s: wide(s), cols(w_ada, n * COL))], (sem("ada_sums"), n + 1))

        IN1 = dict(q=0, k=1, v=2, xb=3, bg=4, cg=5, gate0=6, gate1=7, gate2=8, gate3=9)
        for n in range(ADA_EARLY):
            ada(n)
        for name, later in (("q", ()), ("k", (4, 5)), ("v", (6,)), ("xb", (7,)), ("cg", (8,)), ("bg", (9,)),
                            ("gate0", (10,)), ("gate1", (11,)), ("gate2", ()), ("gate3", ())):
            last_unit = f"gate{2 * int(name[4]) + 1}" if name.startswith("gate") else name + "1"
            chunk(name, [(lambda s: wide(s), cols(w_in, IN1[name] * COL))], after(last_unit))
            for n in later:
                ada(n)
        chunk("pa", [(lambda s: tall(s), A["w_pa"][0].rearrange("(k p) n -> p k n", p=P))], after(f"proj{KD - 1}"))
        chunk("pb", [(lambda s: tall(s), A["w_pb"][0].rearrange("(k p) n -> p k n", p=P))], after(f"proj{KD - 1}"))
        for n in range(2):
            chunk(f"wo{n}", [(lambda s: wide(s), cols(A["w_o"][0], n * COL))], after(f"wo{2 * n + 1}"))

        moe_first = len(chunks)
        moe_slot = [(moe_first + n) % SLOTS for n in range(6)]
        MOE_USED = ("w1_used", "w1_used", "w3_used", "w3_used", "ys1_done", "ys1_done")
        for n in range(PAIRS):
            for name in MOE_USED:
                chunk(f"moe{len(chunks)}", None, (sem("moe_" + name), n + 1))
        block2_first = len(chunks)
        IN2 = dict(hq=0, hf=512, hi=1024, hg=1536, fq=2048, fk=2560, fv=3072)
        GATE2 = 3584 + HEADS
        for name in ("hf", "hq", "hi", "fq", "fk", "fv", "hg"):
            chunk(name, [(lambda s: wide(s), cols(w_in2, IN2[name]))], after(name + "1"))
        for n in range(4):
            chunk(f"gate_b{n}", [(lambda s: wide(s), cols(w_in2, GATE2 + n * COL))], after(f"gate_b{2 * n + 1}"))
        for name in ("a", "b"):
            chunk("branch_" + name, [(lambda s: tall(s), A[f"w_branch_{name}_2"][0].rearrange("(k p) n -> p k n", p=P))],
                  after(f"proj_b{KD - 1}"))
        for n in range(2):
            chunk(f"wo_b{n}", [(lambda s: wide(s), cols(A["w_out_2"][0], n * COL))], after(f"wo_b{2 * n + 1}"))
        wg, wu, wd = A["w_ffn_gate_2"][0], A["w_ffn_up_2"][0], A["w_ffn_down_2"][0]
        FULL = DFF // COL
        REST = DFF - FULL * COL
        for n in range(FULL):
            chunk(f"ffn_gate{n}", [(lambda s: wide(s), cols(wg, n * COL))], after(f"ffn{4 * n + 3}"))
            chunk(f"ffn_up{n}", [(lambda s: wide(s), cols(wu, n * COL))], after(f"ffn{4 * n + 3}"))
        chunk("ffn_rest", [(lambda s: wide(s)[:, :, 0:REST], cols(wg, FULL * COL, REST)),
                           (lambda s: wide(s)[:, :, REST:2 * REST], cols(wu, FULL * COL, REST))], after(f"ffn{FFT - 1}"))
        DOWN = []
        for n in range(0, FFT, 4):
            m = min(4, FFT - n)
            DOWN.append((n, m))
            chunk(f"down{n // 4}", [(lambda s, m=m: tall(s)[:, 0:m, :],
                                     wd[n * P:(n + m) * P, :].rearrange("(k p) n -> p k n", p=P))],
                  (sem("down_used"), n // 4 + 1) if n + m < FFT else after("down3"))
        for n in range(2):
            chunk(f"ple_gate{n}", [(lambda s: wide(s), cols(A["w_ple_gate_2"][0], n * COL))], after(f"ple{4 * n + 3}"))
        chunk("ple_proj", [(lambda s: tall(s)[:, 0:2, :], A["w_ple_proj_2"][0].rearrange("(k p) n -> p k n", p=P))],
              after(f"ple{KD - 1}"))

        landed, arrive_at = [0] * SLOTS, []
        for n, (loads, _) in enumerate(chunks):
            landed[n % SLOTS] += 16 * (1 if loads is None else len(loads))
            arrive_at.append(landed[n % SLOTS])
        chunk_in = [sem(f"chunk_in{s}") for s in range(SLOTS)]
        spare_in = [sem(f"spare_in{s}") for s in range(SLOTS)]

        def arrived(pe, name):
            n = chunk_of[name]
            pe.wait_ge(chunk_in[n % SLOTS], arrive_at[n])
            return n % SLOTS

        def ada_acc(c):
            a = 2 * KD - 4 + 2 * (c % 2)
            return gates[:, a:a + 2, :].rearrange("p k t -> p (k t)")

        moe_in_base = [arrive_at[moe_first + n] for n in range(6)]
        expert_w = [A[name][0] for name in ("w1", "w1", "w3", "w3", "w2", "w2")]

        def expert_load(sp_, n, pair, signal):
            src = expert_w[n][bass.ds(2 * pair + n % 2, 1)].rearrange("e (k p) n -> p (e k) n", p=P)
            view = tall(moe_slot[n]) if n >= 4 else wide(moe_slot[n])
            sp_.dma_start(view, src).then_inc(signal[moe_slot[n]], 16)

        block = ctx.enter_context(nc.Block())

        @block.sync
        def _(sp_):
            def load(n):
                if n >= SLOTS:
                    sp_.wait_ge(*chunks[n - SLOTS][1])
                for view, src in chunks[n][0]:
                    sp_.dma_start(view(n % SLOTS), src).then_inc(chunk_in[n % SLOTS], 16)

            sp_.dma_start(rows[:, :, :], A["x"][0].rearrange("(t p) d -> p t d", p=P)).then_inc(sem("x_in"), 16)
            sp_.dma_start(cst[:, :], consts).then_inc(sem("cst_in"), 16)
            sp_.wait_ge(sem("params_in"), 16 * len(PARAM_ROWS))
            for n in range(moe_first):
                load(n)
            for n in range(6):
                sp_.wait_ge(*chunks[moe_first + n - SLOTS][1])
                expert_load(sp_, n, 0, chunk_in)
            with sp_.Fori(1, PAIRS) as i:
                for n, name in enumerate(MOE_USED):
                    sp_.wait_ge(sem("moe_" + name), i)
                    expert_load(sp_, n, i, chunk_in)
            for n in range(block2_first - SLOTS, block2_first):
                sp_.wait_ge(*chunks[n][1])
            sp_.wait_ge(sem("flag_ready"), 1)
            more = sp_.value_load(flag[0:1, 0:1], min_val=0, max_val=1)
            with sp_.If(more > 0):
                for n in range(6):
                    expert_load(sp_, n, 0, spare_in)
                with sp_.Fori(1, PAIRS * EXTRA_ROUNDS) as i:
                    e = sp_.snap(i % PAIRS)
                    for n, name in enumerate(MOE_USED):
                        sp_.wait_ge(sem("moe_" + name), i + PAIRS)
                        expert_load(sp_, n, e, spare_in)
                sp_.wait_ge(sem("moe_ys1_done"), PAIRS + PAIRS * EXTRA_ROUNDS)
            for n in range(block2_first, len(chunks)):
                load(n)
            for n, (t, half) in enumerate(((0, 0), (1, 0), (0, 1), (1, 1))):
                sp_.wait_ge(sem("out_ready"), n + 1)
                sp_.dma_start(out[0, t * P:(t + 1) * P, half * 512:half * 512 + 512],
                              orow[:, t, half * 512:half * 512 + 512]).then_inc(sem("out_sent"), 16)
            sp_.wait_ge(sem("out_sent"), 64)

        @block.gpsimd
        def _(pool):
            nc.gpsimd.memset(uT[:, :, 0:2], 0.0).then_inc(sem("pad_ready"), 1)
            pool.dma_start(br[:, 0:GROUPS], A["b_rg"].to_broadcast([P, GROUPS])).then_inc(sem("route_in"), 16)
            pool.dma_start(br[:, GROUPS:], A["b_re"].to_broadcast([P, EXPERTS])).then_inc(sem("route_in"), 16)
            pool.dma_start(wr[:, :, 0:GROUPS], A["w_rg"][0].rearrange("(k p) n -> p k n", p=P)).then_inc(sem("route_in"), 16)
            pool.dma_start(wr[:, :, GROUPS:], A["w_re"][0].rearrange("(k p) n -> p k n", p=P)).then_inc(sem("route_in"), 16)
            pool.dma_start(wfox[:, :, :], cols(w_in2, 3584, HEADS)).then_inc(sem("fox_in"), 16)
            pool.dma_start(fbias[:, :], A["fox_f_bias_2"].rearrange("a h -> h a")).then_inc(sem("fox_in"), 16)
            dense.ready(pool, f"proj{KD - 1}")
            nc.gpsimd.memset(scT, 0.0).then_inc(sem("scores_zeroed"), 1)
            for n in range(len(level_names) - 1):
                pool.wait_ge(sem("decay_ready"), n + 1)
                if n >= 2:
                    small.ready(pool, level_units[level_names[n - 2]][-1])
                nc.gpsimd.tensor_tensor(KE[n % 2], khT, E[n % 2], ALU.mult).then_inc(sem("ke_ready"), 1)
            dense.ready(pool, f"proj_b{KD - 1}")
            pool.dma_start(prows, A["p_2"][0, 0].rearrange("(t p) n -> p t n", p=P)).then_inc(sem("p_in"), 16)

        @block.tensor
        def _(pe):
            mm = nc.tensor.matmul

            def square_sums(name, ready, tiles, weight):
                o = small.claim(pe, name)[:, 0:T]
                for k in range(tiles):
                    pe.wait_ge(*ready(k))
                    last = mm(o, lhsT=weight, rhs=sq[:, k, :], start=k == 0, stop=k == tiles - 1)
                last.then_inc(small.done, 1)

            def token_rows(name, unit, slot, h_ready):
                o = dense.claim(pe, name)
                for k in range(KD):
                    pe.wait_ge(sem(h_ready), k + 1)
                    last = mm(o, lhsT=hT[:, k, unit * P:(unit + 1) * P], rhs=wide(slot)[:, k, :],
                              start=k == 0, stop=k == KD - 1)
                last.then_inc(dense.done, 1)

            def channel_tiles(name, unit, slot, h_ready, moving):
                o = dense.claim(pe, name)
                for j in range(2):
                    at = (2 * unit + j) * P
                    for k in range(KD):
                        pe.wait_ge(sem(h_ready), k + 1)
                        last = mm(o[:, j * T:(j + 1) * T], lhsT=wide(slot)[:, k, at:at + P], rhs=moving[:, k, :],
                                  start=k == 0, stop=k == KD - 1)
                last.then_inc(dense.done, 1)

            def modulation(c):
                o = small.claim(pe, f"ada{c}")
                pe.wait_ge(sem("ada_sums"), c + 1)
                for j in range(COL // P):
                    last = mm(o[:, j:j + 1], lhsT=ada_acc(c)[:, j * P:(j + 1) * P], rhs=ones[:, 0:1], start=True, stop=True)
                last.then_inc(small.done, 1)

            def head_transposes(name, row, ready):
                pe.wait_ge(sem(ready), 1)
                for u in range(2):
                    o = small.claim(pe, f"{name}{u}")
                    for j in range(2):
                        for t in range(TT):
                            c = 2 * u + j
                            last = nc.tensor.transpose(o[:, j * T + t * P:j * T + (t + 1) * P],
                                                       row[:, t, c * P:(c + 1) * P], ident)
                    last.then_inc(small.done, 1)

            def scores(tag, h):
                o = small.claim(pe, f"qk{tag}{h}")
                pe.wait_ge(sem(f"qT_ready{tag}"), h // 4 + 1)
                pe.wait_ge(sem(f"kT_ready{tag}"), h // 4 + 1)
                a = DH * (h % 2)
                mm(o[:, 0:P], lhsT=qT[a:a + DH, h // 2, 0:P], rhs=kT[a:a + DH, h // 2, 0:P], start=True, stop=True)
                mm(o[:, P:SC], lhsT=qT[a:a + DH, h // 2, P:T], rhs=kT[a:a + DH, h // 2, :], start=True,
                   stop=True).then_inc(small.done, 1)

            def probs_transposes(tag, h):
                o = small.claim(pe, f"pt{tag}{h}")
                pe.wait_ge(sem(f"probs_ready{tag}"), h + 1)
                for n in range(3):
                    last = nc.tensor.transpose(o[:, n * P:(n + 1) * P], sp[:, h % 4, n * P:(n + 1) * P], ident)
                last.then_inc(small.done, 1)

            def weighted_values(tag, h):
                o = small.claim(pe, f"pv{tag}{h}")
                pe.wait_ge(sem(f"pT_ready{tag}"), h + 1)
                a = DH * (h % 2)
                p = pT[:, h % 2, :]
                mm(o[a:a + DH, 0:P], lhsT=vrow[:, 0, h * DH:(h + 1) * DH], rhs=p[:, 0:P], start=True, stop=True)
                for t in range(TT):
                    last = mm(o[a:a + DH, P:T], lhsT=vrow[:, t, h * DH:(h + 1) * DH], rhs=p[:, (1 + t) * P:(2 + t) * P],
                              start=t == 0, stop=t == 1)
                last.then_inc(small.done, 1)

            def key_bias(h):
                o = small.claim(pe, f"bias{h}")
                pe.wait_ge(sem("fox_c_ready"), 1)
                mm(o[:, 0:T], lhsT=ident[0:HEADS, h:h + 1].to_broadcast([HEADS, P]), rhs=foxc[:, :], start=True,
                   stop=True).then_inc(small.done, 1)

            def attention_step(tag, names):
                for name in names:
                    h = int(name[-1])
                    if name.startswith("bias"):
                        key_bias(h)
                    elif name.startswith("qk"):
                        scores(tag, h)
                    elif name.startswith("pt"):
                        probs_transposes(tag, h)
                    else:
                        weighted_values(tag, h)

            def branch_products(tag, slot_a, slot_b, ready_a, ready_b):
                for j in range(KD):
                    o = dense.claim(pe, f"proj{tag}{j}")
                    for n, (slot, y) in enumerate(((slot_a, yaT), (slot_b, ybT))):
                        pe.wait_ge(*(ready_a, ready_b)[n])
                        for k in range(CT):
                            last = mm(o[:, n * T:(n + 1) * T], lhsT=tall(slot)[:, k, j * P:(j + 1) * P], rhs=y[:, k, :],
                                      start=k == 0, stop=k == CT - 1)
                    last.then_inc(dense.done, 1)

            pe.wait_ge(sem("cst_in"), 16)
            pe.wait_ge(sem("params_in"), 16 * len(PARAM_ROWS))
            o = small.claim(pe, "params")
            nc.tensor.transpose(o[:, 0:PARAM_N], prow[0:PARAM_N, :], ident[0:PARAM_N, 0:PARAM_N]).then_inc(small.done, 1)
            pe.wait_ge(sem("x_in"), 16)
            for i in range(4):
                o = small.claim(pe, f"x{i}")
                for kk in range(2):
                    for t in range(TT):
                        k = 2 * i + kk
                        last = nc.tensor.transpose(o[:, kk * T + t * P:kk * T + (t + 1) * P],
                                                   rows[:, t, k * P:(k + 1) * P], ident)
                last.then_inc(small.done, 1)
            square_sums("ms_norm1", lambda k: (sem("sq_norm1"), k // 2 + 1), KD, mean_d)
            for c in range(ADA_EARLY):
                modulation(c)
            for name in ("q", "k", "v", "xb", "cg", "bg"):
                slot = arrived(pe, name)
                for u in range(2):
                    if name in "qkv":
                        token_rows(f"{name}{u}", u, slot, "h1_ready")
                    else:
                        channel_tiles(f"{name}{u}", u, slot, "h1_ready", hT)
                    if name == "v":
                        head_transposes(("tq", "tk")[u], (qrow, krow)[u], ("q_normed", "k_normed")[u])
                    if name in ("xb", "cg", "bg"):
                        n = 2 * ("xb", "cg", "bg").index(name) + u
                        attention_step("", att1[n])
                    if f"{name}{u}" in ada_at:
                        modulation(ada_at[f"{name}{u}"])
            for u in range(8):
                if u % 2 == 0:
                    slot = arrived(pe, f"gate{u // 2}")
                channel_tiles(f"gate{u}", u % 2, slot, "h1_ready", hT)
                if 6 + u < len(att1):
                    attention_step("", att1[6 + u])
                if f"gate{u}" in ada_at:
                    modulation(ada_at[f"gate{u}"])
            slots = arrived(pe, "pa"), arrived(pe, "pb")
            branch_products("", *slots, (sem("ya_ready"), HEADS), (sem("yb_ready"), 2))
            for u in range(4):
                if u % 2 == 0:
                    slot = arrived(pe, f"wo{u // 2}")
                channel_tiles(f"wo{u}", u % 2, slot, "merged_ready", merged)
            square_sums("ms_norm2", lambda k: (sem("sq_norm2"), k + 1), KD, mean_d)
            pe.wait_ge(sem("route_in"), 64)
            o = small.claim(pe, "logits")
            for t in range(TT):
                for k in range(KD):
                    pe.wait_ge(sem("h2_ready"), k + 1)
                    last = mm(o[:, t * 64:t * 64 + GROUPS + EXPERTS], lhsT=hT[:, k, t * P:(t + 1) * P], rhs=wr[:, k, :],
                              start=k == 0, stop=k == KD - 1)
            last.then_inc(small.done, 1)
            for i in range(4):
                o = small.claim(pe, f"h2r{i}")
                for j in range(4):
                    k = 4 * (i % 2) + j
                    last = nc.tensor.transpose(o[:, j * P:(j + 1) * P], hT[:, k, (i // 2) * P:(i // 2 + 1) * P], ident)
                last.then_inc(small.done, 1)
            o = small.claim(pe, "rank")
            pe.wait_ge(sem("chosen_ready"), 1)
            chosen = rt[:, 0, :, :]
            mm(o[:, 0:32], lhsT=before, rhs=chosen[:, 0, :], start=True, stop=True)
            mm(o[:, 32:64], lhsT=before, rhs=chosen[:, 1, :], start=True, stop=False)
            mm(o[:, 32:64], lhsT=ones, rhs=chosen[:, 0, :], start=False, stop=True)
            mm(o[:, 64:96], lhsT=ones, rhs=chosen[:, 0, :], start=True, stop=False)
            mm(o[:, 64:96], lhsT=ones, rhs=chosen[:, 1, :], start=False, stop=True).then_inc(small.done, 1)
            pe.wait_ge(sem("zeros_ready"), 1)
            for u in range(4):
                o = dense.claim(pe, f"moe{u}")
                mm(o, lhsT=ident, rhs=zeros, start=True, stop=True)
            for name in small_order[n_block1 - 4:n_block1]:
                pe.wait_ge(*small.released[name])
            pe.wait_ge(sem("h2_rows_ready"), 4)

            def gather():
                for n, G in enumerate((GA, GB)):
                    for j in range(4):
                        k = 4 * n + j
                        for t in range(TT):
                            last = mm(G[:, j * P:(j + 1) * P], lhsT=rows[:, t, k * P:(k + 1) * P], rhs=S[:, t, :],
                                      start=t == 0, stop=t == TT - 1)
                    last.then_inc(sem(f"moe_gather{n}_done"), 1)

            def slots_of(e):
                return slice(e * CAP, (e + 1) * CAP)

            def up(n, H, i, signal, base):
                for e in range(2):
                    pe.wait_ge(signal[moe_slot[2 * n + e]], base[2 * n + e] + 16 * i)
                for k in range(KD):
                    for e in range(2):
                        last = mm(H[slots_of(e), :], lhsT=xs[:, k, slots_of(e)], rhs=wide(moe_slot[2 * n + e])[:, k, :],
                                  start=k == 0, stop=k == KD - 1)
                last.then_inc(sem(("moe_w1_used", "moe_w3_used")[n]), 1)

            def pair_of_experts(i, done, ahead, signal, base):
                for n in range(2):
                    pe.wait_ge(sem(f"moe_xs{n}_ready"), i + ahead + 1)
                up(0, HA, i, signal, base)
                up(1, HB, i, signal, base)
                pe.wait_ge(sem("moe_s_ready"), 4 * i + 4 * ahead + 8)
                gather()
                pe.wait_ge(sem("moe_xs0_ready"), i + ahead + 2)
                pe.wait_ge(sem("moe_hid_ready"), i + done + 1)
                for f in range(FT):
                    last = nc.tensor.transpose(GA[:, f * P:(f + 1) * P], hid[:, f * P:(f + 1) * P], ident)
                last.then_inc(sem("moe_hidT_done"), 1)
                pe.wait_ge(sem("moe_xs1_ready"), i + ahead + 2)
                pe.wait_ge(sem("moe_sw_ready"), 4 * i + 4 * done + 4)
                for t in range(TT):
                    last = nc.tensor.transpose(GB[:, t * P:(t + 1) * P], Sw[:, t, :], ident)
                last.then_inc(sem("moe_st_done"), 1)
                for e in range(2):
                    pe.wait_ge(signal[moe_slot[4 + e]], base[4 + e] + 16 * i)
                pe.wait_ge(sem("moe_hidT_ready"), i + done + 1)
                for half, Y in enumerate((HA, HB)):
                    for f in range(FT):
                        for e in range(2):
                            last = mm(Y[slots_of(e), :], lhsT=hidT[:, f, slots_of(e)],
                                      rhs=tall(moe_slot[4 + e])[:, f, half * 512:half * 512 + 512],
                                      start=f == 0, stop=f == FT - 1)
                    last.then_inc(sem(f"moe_ys{half}_done"), 1)
                pe.wait_ge(sem("moe_st_ready"), i + done + 1)
                for half in range(2):
                    pe.wait_ge(sem(f"moe_ys{half}_ready"), i + done + 1)
                    for j in range(4 * half, 4 * half + 4):
                        sums = dense.bank(f"moe{j // 2}")
                        last = mm(sums[:, (j % 2) * T:(j % 2 + 1) * T], lhsT=ys[:, j * P:(j + 1) * P], rhs=ST,
                                  start=False, stop=True, skip_group_check=True)
                last.then_inc(sem("moe_combined"), 1)

            def experts(rounds, done, ahead, signal, base):
                pe.wait_ge(sem("moe_s_ready"), 4 * ahead + 4)
                gather()
                with pe.Fori(0, PAIRS * rounds) as i:
                    pair_of_experts(i, done, ahead, signal, base)
                for n in range(2):
                    pe.wait_ge(sem(f"moe_xs{n}_ready"), PAIRS * rounds + ahead + 1)

            experts(1, 0, 0, chunk_in, moe_in_base)
            pe.wait_ge(sem("flag_ready"), 1)
            more = pe.value_load(flag[0:1, 0:1], min_val=0, max_val=1)
            with pe.If(more > 0):
                experts(EXTRA_ROUNDS, PAIRS, PAIRS + 1, spare_in, [16] * 6)

            square_sums("ms_mix", lambda k: (sem("sq_mix"), k + 1), KD, mean_d)

            def fox_gate_logits():
                o = small.claim(pe, "fox_f")
                pe.wait_ge(sem("fox_in"), 32)
                for k in range(KD):
                    last = mm(o[0:HEADS, 0:T], lhsT=wfox[:, k, :], rhs=hT[:, k, :], start=k == 0, stop=k == KD - 1)
                last.then_inc(small.done, 1)

            def level(name):
                n = level_names.index(name)
                if name != "diag":
                    pe.wait_ge(sem("qe_ready"), n + 1)
                    pe.wait_ge(sem("ke_ready"), n + 1)
                q, k = (qhT, khT) if name == "diag" else (QE[n % 2], KE[n % 2])
                if name == "cross":
                    o = small.claim(pe, "cross")
                    for h in range(HG):
                        last = mm(o[:, h * P:(h + 1) * P], lhsT=k[:, h, 0:P], rhs=q[:, h, P:T], start=True, stop=True)
                    last.then_inc(small.done, 1)
                    return
                for u, unit in enumerate(level_units[name]):
                    o = small.claim(pe, unit)
                    for j in range(4):
                        h, t = (4 * u + j) // TT, j % TT
                        last = mm(o[:, j * P:(j + 1) * P], lhsT=k[:, h, t * P:(t + 1) * P],
                                  rhs=q[:, h, t * P:(t + 1) * P], start=True, stop=True)
                    last.then_inc(small.done, 1)

            def hgrn_values():
                pe.wait_ge(*small.released["diagb"])
                for u in range(2):
                    o = small.claim(pe, f"ho{u}")
                    for j in range(2):
                        h = 2 * u + j
                        v = irow[:, :, h * P:(h + 1) * P]
                        mm(o[:, j * T:j * T + P], lhsT=v[:, 0, :], rhs=scT[:, 2 * h, :], start=True, stop=True)
                        mm(o[:, j * T + P:(j + 1) * T], lhsT=v[:, 0, :], rhs=scX[:, h, :], start=True, stop=False)
                        last = mm(o[:, j * T + P:(j + 1) * T], lhsT=v[:, 1, :], rhs=scT[:, 2 * h + 1, :],
                                  start=False, stop=True)
                    last.then_inc(small.done, 1)

            def hgrn_norm():
                for u in range(2):
                    o = small.claim(pe, f"ms_h{u}")
                    pe.wait_ge(sem("hsq_ready"), u + 1)
                    mm(o, lhsT=mean_v, rhs=hsq[:, 2 * u:2 * u + 2, :], start=True, stop=True).then_inc(small.done, 1)

            def between(name):
                for names in after2.get(name, []):
                    if names[0].startswith(("tq", "tk")):
                        which = names[0][1]
                        head_transposes(f"t{which}_b", qrow if which == "q" else krow, f"{which}_normed_b")
                    elif names[0] == "ho0":
                        hgrn_values()
                    elif names[0] == "ms_h0":
                        hgrn_norm()
                    elif names[0].startswith(("cross", "lev", "diag")):
                        level("cross" if names[0] == "cross" else names[0][:-1])
                    else:
                        attention_step("_b", names)

            for name in ("hf", "hq", "hi", "fq", "fk", "fv", "hg"):
                slot = arrived(pe, name)
                for u in range(2):
                    if name in ("hi", "fq", "fk", "fv"):
                        token_rows(f"{name}{u}", u, slot, "hm_ready")
                    else:
                        channel_tiles(f"{name}{u}", u, slot, "hm_ready", hT)
                    if name == "hf" and u == 0:
                        fox_gate_logits()
                    between(f"{name}{u}")
            for u in range(8):
                if u % 2 == 0:
                    slot = arrived(pe, f"gate_b{u // 2}")
                channel_tiles(f"gate_b{u}", u % 2, slot, "hm_ready", hT)
                between(f"gate_b{u}")
            slots = arrived(pe, "branch_a"), arrived(pe, "branch_b")
            branch_products("_b", *slots, (sem("ya_ready_b"), HG), (sem("yb_ready_b"), HEADS))
            for u in range(4):
                if u % 2 == 0:
                    slot = arrived(pe, f"wo_b{u // 2}")
                channel_tiles(f"wo_b{u}", u % 2, slot, "merged_ready_b", merged)
            square_sums("ms_ffn", lambda k: (sem("sq_ffn"), k + 1), KD, mean_d)
            for f in range(FFT):
                if f < 4 * FULL:
                    sg, su = arrived(pe, f"ffn_gate{f // 4}"), arrived(pe, f"ffn_up{f // 4}")
                    ag = au = (f % 4) * P
                else:
                    sg = su = arrived(pe, "ffn_rest")
                    ag = (f - 4 * FULL) * P
                    au = REST + ag
                o = dense.claim(pe, f"ffn{f}")
                for n, (slot, at) in enumerate(((sg, ag), (su, au))):
                    for k in range(KD):
                        pe.wait_ge(sem("hf_ready"), k + 1)
                        last = mm(o[:, n * T:(n + 1) * T], lhsT=wide(slot)[:, k, at:at + P], rhs=hT[:, k, :],
                                  start=k == 0, stop=k == KD - 1)
                last.then_inc(dense.done, 1)
            downs = [dense.claim(pe, f"down{u}") for u in range(4)]
            for c, (first, m) in enumerate(DOWN):
                slot = arrived(pe, f"down{c}")
                for f in range(first, first + m):
                    pe.wait_ge(sem("act_ready"), f + 1)
                    for j in range(KD):
                        last = mm(downs[j // 2][:, (j % 2) * T:(j % 2 + 1) * T],
                                  lhsT=tall(slot)[:, f - first, j * P:(j + 1) * P], rhs=act[:, f, :],
                                  start=f == 0 and j % 2 == 0, stop=f == FFT - 1, skip_group_check=True)
                        if f == FFT - 1 and j % 2 == 1:
                            last.then_inc(dense.done, 1)
                if first + m < FFT:
                    last.then_inc(sem("down_used"), 1)
            square_sums("ms_ple", lambda k: (sem("sq_ple"), k + 1), KD, mean_d)
            o = small.claim(pe, "pp")
            pe.wait_ge(sem("p_in"), 16)
            for k in range(2):
                for t in range(TT):
                    last = nc.tensor.transpose(o[:, k * T + t * P:k * T + (t + 1) * P], prows[:, t, k * P:(k + 1) * P], ident)
            last.then_inc(small.done, 1)

            def result_rows(half):
                for t in range(TT):
                    o = small.claim(pe, f"o{t}{half}")
                    for j in range(4):
                        pe.wait_ge(sem("o_ready"), 4 * half + j + 1)
                        last = nc.tensor.transpose(o[:, j * P:(j + 1) * P], oT[:, 4 * half + j, t * P:(t + 1) * P], ident)
                    last.then_inc(small.done, 1)

            sproj = None
            for j in range(KD):
                if j % 4 == 0:
                    slot = arrived(pe, f"ple_gate{j // 4}")
                o = dense.claim(pe, f"ple{j}")
                for k in range(KD):
                    pe.wait_ge(sem("hp_ready"), k + 1)
                    mm(o[:, 0:T], lhsT=wide(slot)[:, k, (j % 4) * P:(j % 4 + 1) * P], rhs=hT[:, k, :],
                       start=k == 0, stop=k == KD - 1)
                if sproj is None:
                    sproj = arrived(pe, "ple_proj")
                    pe.wait_ge(sem("ppT_ready"), 1)
                for k in range(2):
                    last = mm(o[:, T:2 * T], lhsT=tall(sproj)[:, k, j * P:(j + 1) * P], rhs=ppT[:, k, :],
                              start=k == 0, stop=k == 1)
                last.then_inc(dense.done, 1)
                if j == 5:
                    result_rows(0)
            result_rows(1)

        @block.scalar
        def _(act_):
            af = nc.scalar.activation

            for name, n in PARAM_ROWS:
                a = A[name]
                flat = {2: "a (k p) -> (a k) p", 3: "a b (k p) -> (a b k) p"}[len(a.shape)]
                act_.dma_start(prow[PARAM_AT[name]:PARAM_AT[name] + n, :], a.rearrange(flat, p=P)).then_inc(sem("params_in"), 16)
            for n, name in enumerate(("g_q", "g_k", "fox_q_norm_g_2", "fox_k_norm_g_2")):
                act_.dma_start(gain[:, n, :], A[name].to_broadcast([P, DH])).then_inc(sem("gain_in"), 16)

            def exps(tag, h):
                act_.wait_ge(sem(f"max_ready{tag}"), h + 1)
                for t, (a, b) in enumerate(((0, P), (P, SC))):
                    last = af(sp[:, h % 4, a:b], sp[:, h % 4, a:b], ACT.Exp, bias=aneg[:, h, t:t + 1], scale=SCALE,
                              accum_out=asum[:, h, t:t + 1])
                    last.then_inc(sem(f"exp_ready{tag}"), 1)

            def probs_out(tag, h):
                src = small.ready(act_, f"pt{tag}{h}")
                af(pT[:, h % 2, :], src[:, 0:SC], ACT.Copy).then_inc(sem(f"pT_ready{tag}"), 1)

            def values_out(tag, h, y, ready):
                src = small.ready(act_, f"pv{tag}{h}")
                a = DH * (h % 2)
                af(y[a:a + DH, h // 2, :], src[a:a + DH, 0:T], ACT.Copy).then_inc(sem(ready), 1)

            def attention_step(tag, names, y, ready):
                for name in names:
                    if name.startswith("qk"):
                        exps(tag, int(name[-1]))
                    elif name.startswith("pt"):
                        probs_out(tag, int(name[-1]))
                    elif name.startswith("pv"):
                        values_out(tag, int(name[-1]), y, ready)

            def copy_out(out_, banks, name, ready):
                af(out_, banks.ready(act_, name), ACT.Copy).then_inc(sem(ready), 1)

            def two_tiles(t, u):
                return t[:, 2 * u:2 * u + 2, :]

            src = small.ready(act_, "params")
            af(pcol[:, :], src[:, 0:PARAM_N], ACT.Copy).then_inc(sem("pcol_ready"), 1)
            act_.wait_ge(sem("pcol_ready"), 1)
            af(sc_c[:, 0, :], pc("c"), ACT.Tanh, scale=0.5).then_inc(sem("tanh_c_ready"), 1)
            for i in range(4):
                copy_out(two_tiles(xT, i), small, f"x{i}", "xT_ready")
                act_.wait_ge(sem("xT_ready"), i + 1)
                af(two_tiles(sq, i), two_tiles(xT, i), ACT.Square).then_inc(sem("sq_norm1"), 1)
            act_.wait_ge(sem("lb_sub_ready"), 1)
            af(lbt[:, 2:4, :], lbt[:, 0:2, :], ACT.Exp).then_inc(sem("lb_exp_ready"), 1)

            def modulation_out(c):
                src = small.ready(act_, f"ada{c}")
                n = COL // P
                af(mod[:, c * n:(c + 1) * n], src[:, 0:n], ACT.Copy).then_inc(sem("mod_raw"), 1)

            def modulation_after(unit):
                if unit in ada_at:
                    modulation_out(ada_at[unit])

            for c in range(ADA_EARLY):
                modulation_out(c)
            for k in range(KD):
                act_.wait_ge(sem("h1_scaled"), k + 1)
                af(hT[:, k, :], hT[:, k, :], ACT.Identity, bias=mod[:, k:k + 1]).then_inc(sem("h1_ready"), 1)
            for name, row in (("q", qrow), ("k", krow), ("v", vrow)):
                for u in range(2):
                    copy_out(row[:, u, :], dense, f"{name}{u}", f"{name}_rows")
                    if name == "v":
                        which, dst = (("tq", qT), ("tk", kT))[u]
                        for i in range(2):
                            copy_out(two_tiles(dst, i), small, f"{which}{i}", f"{which[1]}T_ready")
                    modulation_after(f"{name}{u}")
            for u in range(6):
                if u < 2:
                    copy_out(two_tiles(xbT, u), dense, f"xb{u}", "xb_ready")
                attention_step("", att1[u], yaT, "ya_ready")
                modulation_after(f"{('xb', 'cg', 'bg')[u // 2]}{u % 2}")
            for u in range(8):
                src = dense.ready(act_, f"gate{u}")
                af(two_tiles(gates, u), src, ACT.Tanh, scale=0.5).then_inc(sem("gates_ready"), 1)
                if 6 + u < len(att1):
                    attention_step("", att1[6 + u], yaT, "ya_ready")
                modulation_after(f"gate{u}")
            for k in range(KD):
                act_.wait_ge(sem("x1_ready"), k + 1)
                af(sq[:, k, :], xT[:, k, :], ACT.Square).then_inc(sem("sq_norm2"), 1)
            for k in range(KD):
                act_.wait_ge(sem("h2_scaled"), k + 1)
                af(hT[:, k, :], hT[:, k, :], ACT.Identity, bias=mod[:, 3 * KD + k:3 * KD + k + 1]).then_inc(sem("h2_ready"), 1)
            for i in range(4):
                copy_out(rows[:, i // 2, (i % 2) * 512:(i % 2) * 512 + 512], small, f"h2r{i}", "h2_rows_ready")
            act_.wait_ge(sem("route_sub_ready"), 1)
            af(rt[:, 6, :, 0:GROUPS], rt[:, 7, :, 0:GROUPS], ACT.Exp).then_inc(sem("route_exp_ready"), 1)
            act_.wait_ge(sem("second_ready"), 1)
            af(r1[:, 6, :], r1[:, 5, :], ACT.Exp).then_inc(sem("second_exp_ready"), 1)

            def experts(rounds, done, ahead):
                def tokens_out(count):
                    act_.wait_ge(sem("moe_gather0_done"), count)
                    af(xs[:, 0:4, :], GA.rearrange("p (k c) -> p k c", c=P), ACT.Copy).then_inc(sem("moe_xs0_ready"), 1)

                tokens_out(ahead + 1)
                with act_.Fori(0, PAIRS * rounds) as i:
                    act_.wait_ge(sem("moe_w1_used"), i + done + 1)
                    af(sil, HA, ACT.Silu).then_inc(sem("moe_sil_ready"), 1)
                    tokens_out(i + ahead + 2)
                    act_.wait_ge(sem("moe_hidT_done"), i + done + 1)
                    af(hidT, GA.rearrange("p (f c) -> p f c", c=P), ACT.Copy).then_inc(sem("moe_hidT_ready"), 1)
                    act_.wait_ge(sem("moe_ys0_done"), i + done + 1)
                    af(ys[:, 0:512], HA, ACT.Copy).then_inc(sem("moe_ys0_ready"), 1)

            experts(1, 0, 0)
            act_.wait_ge(sem("flag_ready"), 1)
            more = act_.value_load(flag[0:1, 0:1], min_val=0, max_val=1)
            with act_.If(more > 0):
                experts(EXTRA_ROUNDS, PAIRS, PAIRS + 1)
            for k in range(KD):
                act_.wait_ge(sem("x2_ready"), k + 1)
                af(sq[:, k, :], xT[:, k, :], ACT.Square).then_inc(sem("sq_mix"), 1)
            for u in range(2):
                src = dense.ready(act_, f"hf{u}")
                af(two_tiles(khT, u), src, ACT.Exp, scale=-1.0).then_inc(sem("hf_exp"), 1)
                if u == 0:
                    act_.wait_ge(sem("fox_abs_ready"), 1)
                    af(fl[:, 2, :], fl[:, 1, :], ACT.Exp, scale=-1.0).then_inc(sem("fox_exp_ready"), 1)
                    act_.wait_ge(sem("fox_exp_ready"), 1)
                    af(fl[:, 2, :], fl[:, 2, :], ACT.Ln, bias=1.0).then_inc(sem("fox_ln_ready"), 1)
            act_.wait_ge(sem("fg_ready"), 1)
            af(QE[0], QE[0], ACT.Ln).then_inc(sem("logf_ready"), 1)
            for u in range(2):
                src = dense.ready(act_, f"hq{u}")
                af(two_tiles(qhT, u), src, ACT.Tanh, scale=0.5).then_inc(sem("hq_tanh"), 1)
            for u in range(2):
                copy_out(irow[:, u, :], dense, f"hi{u}", "hi_ready")

            def decay(n):
                act_.wait_ge(sem("diff_ready"), n + 1)
                af(E[n % 2], E[n % 2], ACT.Exp).then_inc(sem("decay_ready"), 1)

            n_level = 0
            for name, row in (("fq", qrow), ("fk", krow), ("fv", vrow)):
                for u in range(2):
                    copy_out(row[:, u, :], dense, f"{name}{u}", f"{name}_rows")
                    decay(n_level)
                    n_level += 1
                    if (name, u) in (("fk", 0), ("fv", 0)):
                        which, dst = (("q", qT), ("k", kT))[name == "fv"]
                        for i in range(2):
                            copy_out(two_tiles(dst, i), small, f"t{which}_b{i}", f"{which}T_ready_b")
            for u in range(2):
                src = dense.ready(act_, f"hg{u}")
                af(two_tiles(sgT, u), src, ACT.Tanh, scale=0.5).then_inc(sem("hg_tanh"), 1)
                decay(n_level)
                n_level += 1
                if n_level == len(level_names) - 1:
                    break
            for u in range(8):
                src = dense.ready(act_, f"gate_b{u}")
                af(two_tiles(gates, u), src, ACT.Tanh, scale=0.5).then_inc(sem("gates_ready_b"), 1)
                if u == 0:
                    for v in range(2):
                        src = small.ready(act_, f"ho{v}")
                        af(two_tiles(hoT, v), src, ACT.Copy).then_inc(sem("ho_ready"), 1)
                        act_.wait_ge(sem("ho_ready"), v + 1)
                        af(two_tiles(hsq, v), two_tiles(hoT, v), ACT.Square).then_inc(sem("hsq_ready"), 1)
                steps = att2[u:u + 1] if u < 7 else att2[7:]
                for names in steps:
                    attention_step("_b", names, ybT, "yb_ready_b")
            for k in range(KD):
                act_.wait_ge(sem("x3_ready"), k + 1)
                af(sq[:, k, :], xT[:, k, :], ACT.Square).then_inc(sem("sq_ffn"), 1)
            for f in range(FFT):
                src = dense.ready(act_, f"ffn{f}")
                if f >= 2:
                    act_.wait_ge(sem("act_ready"), f - 1)
                af(fsil[:, f % 2, :], src[:, 0:T], ACT.Silu).then_inc(sem("fsil_ready"), 1)
            for k in range(KD):
                act_.wait_ge(sem("x4_ready"), k + 1)
                af(sq[:, k, :], xT[:, k, :], ACT.Square).then_inc(sem("sq_ple"), 1)
            copy_out(ppT, small, "pp", "ppT_ready")

            def result_out(n, t, half):
                copy_out(orow[:, t, half * 512:half * 512 + 512], small, f"o{t}{half}", "out_ready")

            for j in range(KD):
                src = dense.ready(act_, f"ple{j}")
                if j >= 2:
                    act_.wait_ge(sem("o_ready"), j - 1)
                af(thp[j % 2], src[:, 0:T], ACT.Tanh, scale=0.5).then_inc(sem("thp_ready"), 1)
                if j == 5:
                    result_out(0, 0, 0)
                    result_out(1, 1, 0)
            result_out(2, 0, 1)
            result_out(3, 1, 1)

        @block.vector
        def _(dve):
            v = nc.vector
            chain = [0]

            def link(ins):
                chain[0] += 1
                ins.then_inc(sem("dve_chain"), 1)
                dve.wait_ge(sem("dve_chain"), chain[0])

            def release(ins, banks, name):
                ins.then_inc(*banks.freed(name))
                dve.wait_ge(*banks.released[name])

            def inv_sqrt(y, x, a, b):
                link(v.tensor_scalar(a.bitcast(I32), x.bitcast(I32), 1, None, ALU.logical_shift_right))
                link(v.tensor_scalar(y.bitcast(I32), a.bitcast(I32), -1.0, float(0x5F3759DF), ALU.mult, ALU.add))
                for _ in range(3):
                    link(v.scalar_tensor_tensor(a, y, -0.5, x, ALU.mult, ALU.mult))
                    link(v.tensor_tensor(b, a, y, ALU.mult))
                    link(v.scalar_tensor_tensor(y, b, 1.5, y, ALU.add, ALU.mult))

            def inv_rms(name):
                src = small.ready(dve, name)
                release(v.tensor_scalar(nwt[:, 0, :], src[:, 0:T], EPS, None, ALU.add), small, name)
                inv_sqrt(rstd[:, :], nwt[:, 0, :], nwt[:, 1, :], nwt[:, 2, :])

            def scaled(scale, signal):
                for k in range(KD):
                    v.scalar_tensor_tensor(hT[:, k, :], xT[:, k, :], scale[:, k:k + 1], rstd[:, 0:T], ALU.mult,
                                           ALU.mult).then_inc(sem(signal), 1)

            def head_norm(row, n, rope, signal):
                r3 = row.rearrange("p t (h d) -> p (t h) d", d=DH)
                t3 = norm_tmp.rearrange("p (n d) -> p n d", d=DH)
                link(v.tensor_tensor(t3, r3, r3, ALU.mult))
                link(v.tensor_reduce(nstat[:, 0, :], t3, AX.X, ALU.add))
                link(v.tensor_scalar(nstat[:, 1, :], nstat[:, 0, :], 1.0 / DH, EPS, ALU.mult, ALU.add))
                inv_sqrt(nstat[:, 0, :], nstat[:, 1, :], nstat[:, 2, :], nstat[:, 3, :])
                link(v.tensor_tensor(t3, r3, nstat[:, 0, :].unsqueeze(2).to_broadcast([P, TT * HEADS, DH]), ALU.mult))
                last = v.tensor_tensor(r3, t3, gain[:, n, :].unsqueeze(1).to_broadcast([P, TT * HEADS, DH]), ALU.mult)
                if not rope:
                    last.then_inc(sem(signal), 1)
                    return
                link(last)
                r4 = row.rearrange("p t (h d) -> p t h d", d=DH)
                x1, x2 = r4[:, :, :, 0:HALF], r4[:, :, :, HALF:ROT]
                c4, s4 = (z.unsqueeze(2).to_broadcast([P, TT, HEADS, HALF]) for z in (cos, sin))
                t4 = [rtmp[:, i, :].rearrange("p (t h r) -> p t h r", t=TT, h=HEADS) for i in range(4)]
                for dst, a, b in ((0, x1, c4), (1, x2, s4), (2, x2, c4), (3, x1, s4)):
                    last = v.tensor_tensor(t4[dst], a, b, ALU.mult)
                    if dst < 3:
                        last.then_inc(sem("rope_parts"), 1)
                link(last)
                dve.wait_ge(sem("rope_parts"), 3 * (n + 1))
                link(v.tensor_tensor(x1, t4[0], t4[1], ALU.subtract))
                v.tensor_tensor(x2, t4[2], t4[3], ALU.add).then_inc(sem(signal), 1)

            def score_max(tag, h, bias):
                if h >= 4:
                    small.ready(dve, f"pt{tag}{h - 4}")
                mask = causal
                if bias:
                    b = small.ready(dve, f"bias{h}")
                    mask = fmask[:, :]
                    link(v.tensor_tensor(mask[:, 0:P], causal[:, 0:P], b[:, 0:P], ALU.add))
                    release(v.tensor_tensor(mask[:, P:SC], causal[:, P:SC], b[:, 0:T], ALU.add), small, f"bias{h}")
                src = small.ready(dve, f"qk{tag}{h}")
                for t, (a, b) in enumerate(((0, P), (P, SC))):
                    ins = v.tensor_tensor_reduce(out=sp[:, h % 4, a:b], in0=src[:, a:b], in1=mask[:, a:b], scale=1.0,
                                                 scalar=-3e38, op0=ALU.add, op1=ALU.max, accum_out=amax[:, h, t:t + 1])
                    if t == 0:
                        link(ins)
                    else:
                        release(ins, small, f"qk{tag}{h}")
                v.tensor_scalar(aneg[:, h, :], amax[:, h, :], -SCALE, None, ALU.mult).then_inc(sem(f"max_ready{tag}"), 1)

            def normalise(tag, h):
                dve.wait_ge(sem(f"exp_ready{tag}"), 2 * h + 2)
                link(v.reciprocal(ainv[:, h, :], asum[:, h, :]))
                link(v.tensor_scalar(sp[:, h % 4, 0:P], sp[:, h % 4, 0:P], ainv[:, h, 0:1], None, ALU.mult))
                v.tensor_scalar(sp[:, h % 4, P:SC], sp[:, h % 4, P:SC], ainv[:, h, 1:2], None,
                                ALU.mult).then_inc(sem(f"probs_ready{tag}"), 1)

            def two_tiles(t, u):
                return t[:, 2 * u:2 * u + 2, :]

            def pair(src):
                return src.rearrange("p (j t) -> p j t", t=T)

            def merge(tag):
                dve.wait_ge(sem(f"gates_ready{tag}"), 8)
                for j in range(KD):
                    src = dense.ready(dve, f"proj{tag}{j}")
                    v.scalar_tensor_tensor(gates[:, j, :], gates[:, j, :], 1.0, src[:, 0:T], ALU.add,
                                           ALU.mult).then_inc(sem("gate_a" + tag), 1)
                    link(v.scalar_tensor_tensor(gates[:, KD + j, :], gates[:, KD + j, :], 1.0, src[:, T:2 * T], ALU.add,
                                                ALU.mult))
                    dve.wait_ge(sem("gate_a" + tag), j + 1)
                    v.tensor_tensor(merged[:, j, :], gates[:, j, :], gates[:, KD + j, :],
                                    ALU.add).then_inc(sem(f"merged_ready{tag}"), 1)

            def residual(units, factor, ready):
                for u in range(4):
                    src = dense.bank(f"{units}{u}")
                    if units != "moe":
                        dense.ready(dve, f"{units}{u}")
                    for j in range(2):
                        k = 2 * u + j
                        v.scalar_tensor_tensor(xT[:, k, :], src[:, j * T:(j + 1) * T], factor(k), xT[:, k, :], ALU.mult,
                                               ALU.add).then_inc(sem(ready), 1)

            dve.wait_ge(sem("tanh_c_ready"), 1)
            link(v.scalar_tensor_tensor(sc_c[:, 1, :], sc_c[:, 0, :], 1.0, pc("c"), ALU.add, ALU.mult))
            link(v.tensor_scalar(sc_c[:, 2, :], sc_c[:, 1, :], 0.5, None, ALU.mult))
            link(v.tensor_tensor(lbt[:, 4, :], pc("hg_lb_logits_2", 0, HG), pc("hg_lb_logits_2", HG, HG), ALU.max))
            link(v.tensor_tensor(lbt[:, 0, :], pc("hg_lb_logits_2", 0, HG), lbt[:, 4, :], ALU.subtract))
            v.tensor_tensor(lbt[:, 1, :], pc("hg_lb_logits_2", HG, HG), lbt[:, 4, :], ALU.subtract).then_inc(sem("lb_sub_ready"), 1)
            dve.wait_ge(sem("lb_exp_ready"), 1)
            link(v.tensor_tensor(lbt[:, 5, :], lbt[:, 2, :], lbt[:, 3, :], ALU.add))
            link(v.reciprocal(lbt[:, 6, :], lbt[:, 5, :]))
            link(v.tensor_tensor(lbt[:, 7, :], lbt[:, 2, :], lbt[:, 6, :], ALU.mult))
            link(v.tensor_scalar(lbt[:, 4, :], lbt[:, 7, :], -1.0, 1.0, ALU.mult, ALU.add))
            link(v.tensor_scalar(oghalf[:, :], pc("hg_onorm_g_2"), 0.5, None, ALU.mult))
            inv_rms("ms_norm1")

            def modulation(c):
                slot = chunk_of[f"ada{c}"] % SLOTS
                dve.wait_ge(chunk_in[slot], arrive_at[chunk_of[f"ada{c}"]])
                if c >= 2:
                    small.ready(dve, f"ada{c - 2}")
                acc, w = ada_acc(c), wide(slot)
                link(v.tensor_scalar(acc, w[:, 0, :], sc_c[:, 2, 0:1], None, ALU.mult))
                for k in range(1, KD):
                    last = v.scalar_tensor_tensor(acc, w[:, k, :], sc_c[:, 2, k:k + 1], acc, ALU.mult, ALU.add)
                    if k < KD - 1:
                        link(last)
                last.then_inc(sem("ada_sums"), 1)

            for c in range(ADA_EARLY):
                modulation(c)
            dve.wait_ge(sem("mod_raw"), ADA_EARLY)
            link(v.tensor_tensor(mod[:, 0:2 * KD], mod[:, 0:2 * KD], pc("b_ada", 0, 2 * KD), ALU.add))
            link(v.scalar_tensor_tensor(scale1[:, :], mod[:, KD:2 * KD], 1.0, pc("g_norm1"), ALU.add, ALU.mult))
            scaled(scale1, "h1_scaled")
            modulation(4)
            modulation(5)
            dve.wait_ge(sem("gain_in"), 64)
            dve.wait_ge(sem("q_rows"), 2)
            head_norm(qrow, 0, True, "q_normed")
            modulation(6)
            dve.wait_ge(sem("k_rows"), 2)
            head_norm(krow, 1, True, "k_normed")
            modulation(7)
            dve.wait_ge(sem("pad_ready"), 1)

            def conv(c):
                w = lambda tap: pc("conv_w", tap * CT + c, 1)
                link(v.tensor_scalar(xbT[:, c, :], uT[:, c, 0:T], w(0), pc("conv_b", c, 1), ALU.mult, ALU.add))
                for tap in (1, 2):
                    link(v.scalar_tensor_tensor(xbT[:, c, :], uT[:, c, tap:tap + T], w(tap), xbT[:, c, :], ALU.mult, ALU.add))

            for n in range(HEADS + 1):
                if n in (2, 3):
                    u = n - 2
                    src = dense.ready(dve, f"cg{u}")
                    dve.wait_ge(sem("xb_ready"), u + 1)
                    release(v.tensor_tensor(uT[:, 2 * u:2 * u + 2, 2:T + 2], pair(src), two_tiles(xbT, u), ALU.mult), dense, f"cg{u}")
                if n in (4, 5):
                    u = n - 4
                    src = dense.ready(dve, f"bg{u}")
                    v.tensor_tensor(two_tiles(ybT, u), pair(src), two_tiles(xbT, u), ALU.mult).then_inc(sem("yb_ready"), 1)
                if n < HEADS:
                    score_max("", n, False)
                if n >= 1:
                    normalise("", n - 1)
                if n in (2, 3):
                    conv(2 * (n - 2))
                    conv(2 * (n - 2) + 1)
                if n in (0, 1, 4, 5):
                    modulation({0: 8, 1: 9, 4: 10, 5: 11}[n])
            dve.wait_ge(sem("mod_raw"), ADA)
            link(v.tensor_tensor(mod[:, 2 * KD:], mod[:, 2 * KD:], pc("b_ada", 2 * KD, 4 * KD), ALU.add))
            link(v.scalar_tensor_tensor(scale2[:, :], mod[:, 4 * KD:5 * KD], 1.0, pc("g_norm2"), ALU.add, ALU.mult))
            link(v.tensor_scalar(ga1h[:, :], mod[:, 2 * KD:3 * KD], 0.5, None, ALU.mult))
            merge("")
            residual("wo", lambda k: ga1h[:, k:k + 1], "x1_ready")
            v.memset(zeros, 0.0).then_inc(sem("zeros_ready"), 1)
            inv_rms("ms_norm2")
            scaled(scale2, "h2_scaled")
            src = small.ready(dve, "logits")
            dve.wait_ge(sem("route_in"), 64)
            release(v.tensor_tensor(lg[:, :, :], src.rearrange("p (t n) -> p t n", n=64)[:, 0:TT, 0:GROUPS + EXPERTS],
                                 br[:, :].unsqueeze(1).to_broadcast([P, TT, GROUPS + EXPERTS]), ALU.add), small, "logits")
            index = cst[:, C_IOTA:C_IOTA + EXPERTS].unsqueeze(1)

            def wide_(a, n):
                return a.unsqueeze(2).to_broadcast([P, TT, n])

            def first_max(values, n, best, one_hot, tmp, least):
                link(v.tensor_reduce(best, values, AX.X, ALU.max))
                link(v.tensor_tensor(tmp, values, wide_(best, n), ALU.is_equal))
                link(v.scalar_tensor_tensor(tmp, tmp, -64.0, index[:, :, 0:n].to_broadcast([P, TT, n]), ALU.mult, ALU.add))
                link(v.tensor_reduce(least, tmp, AX.X, ALU.min))
                link(v.tensor_tensor(one_hot, tmp, wide_(least, n), ALU.is_equal))

            g, e = lg[:, :, 0:GROUPS], lg[:, :, GROUPS:]
            gsel = rt[:, 1, :, 0:GROUPS]
            first_max(g, GROUPS, r1[:, 0, :], gsel, rt[:, 2, :, 0:GROUPS], r1[:, 1, :])
            v.tensor_tensor(rt[:, 7, :, 0:GROUPS], g, wide_(r1[:, 0, :], GROUPS), ALU.subtract).then_inc(sem("route_sub_ready"), 1)
            link(v.tensor_scalar(rt[:, 2, :, 0:GROUPS], gsel, BIG, -BIG, ALU.mult, ALU.add))

            def by_group(a):
                return a.rearrange("p t (g n) -> p t g n", g=GROUPS)

            def per_group(a):
                return a.unsqueeze(3).to_broadcast([P, TT, GROUPS, PER_GROUP])

            link(v.tensor_tensor(by_group(rt[:, 3, :, :]), by_group(e), per_group(gsel), ALU.mult))
            link(v.tensor_tensor(by_group(rt[:, 4, :, :]), by_group(rt[:, 3, :, :]), per_group(rt[:, 2, :, 0:GROUPS]), ALU.add))
            first_max(rt[:, 4, :, :], EXPERTS, r1[:, 2, :], rt[:, 1, :, :], rt[:, 3, :, :], r1[:, 1, :])
            link(v.scalar_tensor_tensor(rt[:, 5, :, :], rt[:, 1, :, :], -2.0 * BIG, rt[:, 4, :, :], ALU.mult, ALU.add))
            first_max(rt[:, 5, :, :], EXPERTS, r1[:, 3, :], rt[:, 2, :, :], rt[:, 3, :, :], r1[:, 1, :])
            v.tensor_tensor(rt[:, 0, :, :], rt[:, 1, :, :], rt[:, 2, :, :], ALU.add).then_inc(sem("chosen_ready"), 1)
            v.tensor_tensor(r1[:, 5, :], r1[:, 3, :], r1[:, 2, :], ALU.subtract).then_inc(sem("second_ready"), 1)
            dve.wait_ge(sem("route_exp_ready"), 1)
            link(v.tensor_reduce(r1[:, 7, :], rt[:, 6, :, 0:GROUPS], AX.X, ALU.add))
            dve.wait_ge(sem("second_exp_ready"), 1)
            link(v.tensor_scalar(r1[:, 8, :], r1[:, 6, :], 1.0, None, ALU.add))
            link(v.tensor_tensor(r1[:, 9, :], r1[:, 7, :], r1[:, 8, :], ALU.mult))
            link(v.reciprocal(r1[:, 10, :], r1[:, 9, :]))
            link(v.tensor_tensor(r1[:, 11, :], r1[:, 10, :], r1[:, 6, :], ALU.mult))
            link(v.tensor_tensor(rt[:, 3, :, :], rt[:, 1, :, :], wide_(r1[:, 10, :], EXPERTS), ALU.mult))
            link(v.tensor_tensor(rt[:, 4, :, :], rt[:, 2, :, :], wide_(r1[:, 11, :], EXPERTS), ALU.mult))
            link(v.memset(wgt[:, :, :], 0.0))
            for r in range(1 + EXTRA_ROUNDS):
                link(v.tensor_tensor(wgt[:, :, r * EXPERTS:(r + 1) * EXPERTS], rt[:, 3, :, :], rt[:, 4, :, :], ALU.add))
            link(v.memset(rank[:, :, :], -1.0))
            src = small.ready(dve, "rank")
            link(v.scalar_tensor_tensor(rt[:, 3, :, :], src[:, 0:TT * EXPERTS].rearrange("p (t n) -> p t n", t=TT), 1.0,
                                        rt[:, 0, :, :], ALU.add, ALU.mult))
            release(v.tensor_reduce(flagf[:, 0:1], src[0:1, 64:96], AX.X, ALU.max), small, "rank")
            for r in range(1 + EXTRA_ROUNDS):
                link(v.tensor_scalar(rank[:, :, r * EXPERTS:(r + 1) * EXPERTS], rt[:, 3, :, :], -1.0 - CAP * r, None, ALU.add))
            v.tensor_scalar(flag[:, :], flagf[:, 0:1], float(CAP), None, ALU.is_gt).then_inc(sem("flag_ready"), 1)

            def experts(first_round, rounds, done, ahead):
                col0 = first_round * EXPERTS

                def one_hot(dst, col, signal, weighted=False):
                    for e_ in range(2):
                        for t in range(TT):
                            place = rank[:, t, bass.ds(col + e_, 1)]
                            into = dst[:, t, e_ * CAP:(e_ + 1) * CAP]
                            if weighted:
                                last = v.tensor_scalar(into, iota, place, wgt[:, t, bass.ds(col + e_, 1)], ALU.is_equal, ALU.mult)
                            else:
                                last = v.tensor_scalar(into, iota, place, None, ALU.is_equal)
                            last.then_inc(sem("moe_" + signal), 1)

                def tokens_out(count):
                    dve.wait_ge(sem("moe_gather1_done"), count)
                    v.tensor_copy(xs[:, 4:8, :], GB.rearrange("p (k c) -> p k c", c=P)).then_inc(sem("moe_xs1_ready"), 1)

                one_hot(S, col0, "s_ready")
                tokens_out(ahead + 1)
                with dve.Fori(0, PAIRS * rounds) as i:
                    one_hot(S, 2 * i + col0 + 2, "s_ready")
                    one_hot(Sw, 2 * i + col0, "sw_ready", True)
                    dve.wait_ge(sem("moe_sil_ready"), i + done + 1)
                    dve.wait_ge(sem("moe_w3_used"), i + done + 1)
                    v.tensor_tensor(hid, sil, HB, ALU.mult).then_inc(sem("moe_hid_ready"), 1)
                    tokens_out(i + ahead + 2)
                    dve.wait_ge(sem("moe_st_done"), i + done + 1)
                    v.tensor_copy(ST, GB[:, 0:T]).then_inc(sem("moe_st_ready"), 1)
                    dve.wait_ge(sem("moe_ys1_done"), i + done + 1)
                    v.tensor_copy(ys[:, 512:1024], HB).then_inc(sem("moe_ys1_ready"), 1)
                dve.wait_ge(sem("moe_combined"), PAIRS * rounds + done)

            experts(0, 1, 0, 0)
            more = dve.value_load(flag[0:1, 0:1], min_val=0, max_val=1)
            with dve.If(more > 0):
                experts(1, EXTRA_ROUNDS, PAIRS, PAIRS + 1)
            residual("moe", lambda k: mod[:, 5 * KD + k:5 * KD + k + 1], "x2_ready")
            inv_rms("ms_mix")
            scaled(pc("norm_mix_g_2"), "hm_ready")
            src = small.ready(dve, "fox_f")
            dve.wait_ge(sem("fox_in"), 32)
            release(v.tensor_scalar(fl[:, 0, :], src[0:HEADS, 0:T], fbias[:, 0:1], None, ALU.add), small, "fox_f")
            v.scalar_tensor_tensor(fl[:, 1, :], fl[:, 0, :], -1.0, fl[:, 0, :], ALU.mult, ALU.max).then_inc(sem("fox_abs_ready"), 1)
            link(v.tensor_scalar(fl[:, 0, :], fl[:, 0, :], 0.0, None, ALU.min))
            dve.wait_ge(sem("fox_ln_ready"), 1)
            link(v.tensor_tensor(fl[:, 1, :], fl[:, 0, :], fl[:, 2, :], ALU.subtract))
            link(v.tensor_tensor_scan(fl[:, 2, :], ones[0:HEADS, 0:1].to_broadcast([HEADS, T]), fl[:, 1, :], 0.0, ALU.mult, ALU.add))
            v.tensor_scalar(foxc[:, :], fl[:, 2, :], -1.0 / SCALE, None, ALU.mult).then_inc(sem("fox_c_ready"), 1)
            dve.wait_ge(sem("hf_exp"), 2)
            fg = QE[0]
            link(v.tensor_scalar(khT, khT, 1.0, None, ALU.add))
            link(v.reciprocal(fg, khT))
            for h in range(HG):
                last = v.tensor_scalar(fg[:, h, :], fg[:, h, :], lbt[:, 4, h:h + 1], lbt[:, 7, h:h + 1], ALU.mult, ALU.add)
                if h < HG - 1:
                    last.then_inc(sem("fg_parts"), 1)
            link(last)
            dve.wait_ge(sem("fg_parts"), HG - 1)
            v.tensor_scalar(khT, fg, -0.5, 0.5, ALU.mult, ALU.add).then_inc(sem("fg_ready"), 1)
            dve.wait_ge(sem("logf_ready"), 1)
            for h in range(HG):
                for t in range(TT):
                    last = v.tensor_tensor_scan(bT[:, h, t * P:(t + 1) * P], ones, fg[:, h, t * P:(t + 1) * P], 0.0,
                                                ALU.mult, ALU.add)
                    if (h, t) != (HG - 1, TT - 1):
                        last.then_inc(sem("scans"), 1)
            link(last)
            dve.wait_ge(sem("scans"), HG * TT - 1)
            for u in range(2):
                src = dense.ready(dve, f"hq{u}")
                dve.wait_ge(sem("hq_tanh"), u + 1)
                release(v.scalar_tensor_tensor(two_tiles(qhT, u), two_tiles(qhT, u), 1.0, pair(src), ALU.add, ALU.mult), dense, f"hq{u}")

            def differences(n):
                name = level_names[n]
                if n >= 2:
                    dve.wait_ge(sem("ke_ready"), n - 1)
                    dve.wait_ge(sem("qe_ready"), n - 1)
                if name == "cross":
                    b, d = bT, E[n % 2]
                    v.tensor_tensor(d[:, :, 0:P], b[:, :, P - 1:P].to_broadcast([P, HG, P]), b[:, :, 0:P],
                                    ALU.subtract).then_inc(sem("left_parts"), 1)
                    last = v.tensor_copy(d[:, :, P:T], b[:, :, P:T])
                else:
                    m = int(name[3:])
                    b, d = (z.rearrange("p h (n two m) -> p (h n) two m", two=2, m=m) for z in (bT, E[n % 2]))
                    mid = b[:, :, 0, m - 1:m].to_broadcast([P, HG * T // (2 * m), m])
                    v.tensor_tensor(d[:, :, 0, :], mid, b[:, :, 0, :], ALU.subtract).then_inc(sem("left_parts"), 1)
                    last = v.tensor_tensor(d[:, :, 1, :], b[:, :, 1, :], mid, ALU.subtract)
                dve.wait_ge(sem("left_parts"), n + 1)
                last.then_inc(sem("diff_ready"), 1)

            def decayed_queries(n):
                dve.wait_ge(sem("decay_ready"), n + 1)
                if n >= 2:
                    small.ready(dve, level_units[level_names[n - 2]][-1])
                v.tensor_tensor(QE[n % 2], qhT, E[n % 2], ALU.mult).then_inc(sem("qe_ready"), 1)

            def scores_out(n):
                name = level_names[n]
                if name == "cross":
                    src = small.ready(dve, "cross")
                    release(v.tensor_copy(scX.rearrange("p h t -> p (h t)"), src), small, "cross")
                    return
                at = C_IDENT if name == "diag" else C_LEVEL + (n - 1) * P
                mask = cst[:, at:at + P].bitcast(I32).unsqueeze(1).to_broadcast([P, 4, P])
                for u, unit in enumerate(level_units[name]):
                    src = small.ready(dve, unit)
                    release(v.copy_predicated(scT[:, 4 * u:4 * u + 4, :], mask, src.rearrange("p (n t) -> p n t", t=P)), small, unit)

            dve.wait_ge(sem("scores_zeroed"), 1)
            n_levels = len(level_names)
            for step in range(n_levels + 1):
                if step < n_levels - 1:
                    differences(step)
                if 1 <= step < n_levels:
                    decayed_queries(step - 1)
                if step >= 2:
                    scores_out(step - 2)
                if step == 2:
                    dve.wait_ge(sem("fq_rows"), 2)
                    head_norm(qrow, 2, False, "q_normed_b")
                if step == 4:
                    dve.wait_ge(sem("fk_rows"), 2)
                    head_norm(krow, 3, False, "k_normed_b")
            scores_out(n_levels - 1)
            for u in range(2):
                src = dense.ready(dve, f"hg{u}")
                dve.wait_ge(sem("hg_tanh"), u + 1)
                release(v.scalar_tensor_tensor(two_tiles(sgT, u), two_tiles(sgT, u), 1.0, pair(src), ALU.add, ALU.mult), dense, f"hg{u}")

            def hgrn_out():
                for h in range(HG):
                    u, j = divmod(h, 2)
                    src = small.ready(dve, f"ms_h{u}")
                    ins = v.tensor_scalar(nwt[:, 0, :], src[:, j * T:(j + 1) * T], EPS, None, ALU.add)
                    if j == 0:
                        link(ins)
                    else:
                        release(ins, small, f"ms_h{u}")
                    inv_sqrt(rstd[:, :], nwt[:, 0, :], nwt[:, 1, :], nwt[:, 2, :])
                    dve.wait_ge(sem("ho_ready"), u + 1)
                    link(v.scalar_tensor_tensor(hoT[:, h, :], hoT[:, h, :], oghalf[:, 0:1], rstd[:, :], ALU.mult, ALU.mult))
                    v.tensor_tensor(yaT[:, h, :], hoT[:, h, :], sgT[:, h, :], ALU.mult).then_inc(sem("ya_ready_b"), 1)

            for n in range(HEADS + 1):
                if n < HEADS:
                    score_max("_b", n, True)
                if n >= 1:
                    normalise("_b", n - 1)
                if n == 1:
                    hgrn_out()
            merge("_b")
            residual("wo_b", lambda k: 0.5, "x3_ready")
            inv_rms("ms_ffn")
            scaled(pc("norm_ffn_g_2"), "hf_ready")
            for f in range(FFT):
                src = dense.bank(f"ffn{f}")
                dve.wait_ge(sem("fsil_ready"), f + 1)
                v.tensor_tensor(act[:, f, :], fsil[:, f % 2, :], src[:, T:2 * T], ALU.mult).then_inc(sem("act_ready"), 1)
            residual("down", lambda k: 1.0, "x4_ready")
            inv_rms("ms_ple")
            scaled(pc("norm_ple_g_2"), "hp_ready")
            for j in range(KD):
                dve.wait_ge(sem("thp_ready"), j + 1)
                src = dense.ready(dve, f"ple{j}")
                release(v.scalar_tensor_tensor(oT[:, j, :], thp[j % 2], 1.0, src[:, T:2 * T], ALU.add, ALU.mult), dense, f"ple{j}")
                v.scalar_tensor_tensor(oT[:, j, :], oT[:, j, :], 0.5, xT[:, j, :], ALU.mult, ALU.add).then_inc(sem("o_ready"), 1)


_INS = ["x", "c", "w_ada", "b_ada", "g_norm1", "g_norm2", "w_in", "g_q", "g_k", "conv_w", "conv_b", "w_pa", "w_pb",
        "w_o", "w_rg", "b_rg", "w_re", "b_re", "w1", "w3", "w2", "p_2", "norm_mix_g_2", "w_in_2", "hg_lb_logits_2",
        "hg_onorm_g_2", "fox_f_bias_2", "fox_q_norm_g_2", "fox_k_norm_g_2", "w_branch_a_2", "w_branch_b_2", "w_out_2",
        "norm_ffn_g_2", "w_ffn_gate_2", "w_ffn_up_2", "w_ffn_down_2", "norm_ple_g_2", "w_ple_gate_2", "w_ple_proj_2"]


def kernel(**inputs):
    import concourse.bacc as _bacc
    from concourse.bass_utils import run_bass_kernel_spmd as _run

    nc = _bacc.Bacc("TRN2", target_bir_lowering=False, num_devices=1)
    arrays, args = {}, {}
    for name in _INS:
        a = np.ascontiguousarray(inputs[name])
        arrays[f"in_{name}"] = a
        args[name] = nc.dram_tensor(f"in_{name}", a.shape, mybir.dt.from_np(a.dtype), kind="ExternalInput").ap()
    arrays["constants"] = constant_table()
    consts = nc.dram_tensor("constants", (P, C_ALL), F32, kind="ExternalInput").ap()
    out = nc.dram_tensor("out", (1, T, D), F32, kind="ExternalOutput").ap()
    two_blocks(nc, args, consts, out)
    r = _run(nc, [arrays], core_ids=[0])
    return r.results[0]["out"]
```

```python
from contextlib import ExitStack

import concourse.bass as bass
from concourse import mybir
import numpy as np

F32 = mybir.dt.float32
I32 = mybir.dt.int32
BF16 = mybir.dt.bfloat16
F32R = mybir.dt.float32r
ALU = mybir.AluOpType
ACT = mybir.ActivationFunctionType
AX = mybir.AxisListType

P = 128
D = 1024
KD = D // P
T = 256
TT = T // P
HEADS = 8
DH = 64
ROT = DH // 4
HALF = ROT // 2
CW = 512
CT = CW // P
GROUPS = 4
PER_GROUP = 8
EXPERTS = GROUPS * PER_GROUP
PAIRS = EXPERTS // 2
ADA = 12
ADA_EARLY = 4
FE = 512
FT = FE // P
CAP = 64
EXTRA_ROUNDS = T // CAP - 1
DFF = 2816
FFT = DFF // P
PLE = 256
HG = 4
EPS = 1e-6
SCALE = DH ** -0.5
BIG = 1e30
COL = 512
SLOTS = 6
SLOT = KD * COL
LEVELS = [64, 32, 16, 8, 4, 2, 1]
SC = 3 * P

C_IDENT = 0
C_MEAN_D = C_IDENT + P
C_MEAN_V = C_MEAN_D + P
C_ONES = C_MEAN_V + P
C_CAUSAL = C_ONES + P
C_BEFORE = C_CAUSAL + SC
C_LEVEL = C_BEFORE + P
C_IOTA = C_LEVEL + len(LEVELS) * P
C_COS = C_IOTA + CAP
C_SIN = C_COS + TT * HALF
C_ALL = C_SIN + TT * HALF

PARAM_ROWS = [("c", KD), ("b_ada", 6 * KD), ("g_norm1", KD), ("g_norm2", KD), ("conv_w", 3 * CT), ("conv_b", CT),
              ("norm_mix_g_2", KD), ("hg_lb_logits_2", 2 * HG), ("hg_onorm_g_2", 1), ("norm_ffn_g_2", KD),
              ("norm_ple_g_2", KD)]
PARAM_AT = {}
PARAM_N = 0
for _name, _rows in PARAM_ROWS:
    PARAM_AT[_name] = PARAM_N
    PARAM_N += _rows


def constant_table():
    c = np.zeros((P, C_ALL), np.float32)
    i = np.arange(P)
    c[:, C_IDENT:C_IDENT + P] = np.eye(P)
    c[:, C_MEAN_D:C_MEAN_D + P] = 1.0 / D
    c[:, C_MEAN_V:C_MEAN_V + P] = 1.0 / P
    c[:, C_ONES:C_ONES + P] = 1.0
    causal = np.where(i[None, :] <= i[:, None], 0.0, -BIG)
    c[:, C_CAUSAL:C_CAUSAL + P] = causal
    c[:, C_CAUSAL + 2 * P:C_CAUSAL + 3 * P] = causal
    c[:, C_BEFORE:C_BEFORE + P] = i[:, None] < i[None, :]
    for n, m in enumerate(LEVELS):
        same = i[:, None] // (2 * m) == i[None, :] // (2 * m)
        c[:, C_LEVEL + n * P:C_LEVEL + (n + 1) * P] = same & (i[:, None] % (2 * m) < m) & (i[None, :] % (2 * m) >= m)
    c[:, C_IOTA:C_IOTA + CAP] = np.arange(CAP)
    freq = np.float32(500000.0) ** (-np.arange(0, ROT, 2, dtype=np.float32) / np.float32(ROT))
    angle = np.arange(T, dtype=np.float32)[:, None] * freq[None, :]
    for table, at in ((np.cos(angle), C_COS), (np.sin(angle), C_SIN)):
        c[:, at:at + TT * HALF] = table.reshape(TT, P, HALF).transpose(1, 0, 2).reshape(P, TT * HALF)
    return c


class Rotation:

    def __init__(self, psum, first, count, order, done, free, released, uncounted=()):
        self.psum, self.first, self.count, self.done, self.free = psum, first, count, done, free
        self.index = {name: n for n, name in enumerate(order)}
        assert len(self.index) == len(order)
        self.order, self.claimed = order, 0
        self.done_at, self.released = {}, {}
        freed, done_n = [0] * count, 0
        for n, name in enumerate(order):
            done_n += name not in uncounted
            self.done_at[name] = done_n
            if name in released:
                self.released[name] = released[name]
            else:
                freed[n % count] += 1
                self.released[name] = free[n % count], freed[n % count]

    def bank(self, name):
        return self.psum[:, self.first + self.index[name] % self.count, :]

    def claim(self, pe, name):
        assert self.index[name] == self.claimed, (name, self.order[self.claimed])
        self.claimed += 1
        if self.index[name] >= self.count:
            pe.wait_ge(*self.released[self.order[self.index[name] - self.count]])
        return self.bank(name)

    def ready(self, engine, name):
        engine.wait_ge(self.done, self.done_at[name])
        return self.bank(name)

    def freed(self, name):
        assert self.released[name][0] is self.free[self.index[name] % self.count]
        return self.released[name][0], 1


def two_blocks(nc, A, consts, out):
    with ExitStack() as ctx:
        layout = []
        first_view = ExitStack()

        def sb(name, shape, dt=F32):
            layout.append((name, shape, dt))
            return first_view.enter_context(nc.sbuf_tensor(name, shape, dt))

        sems = {}

        def sem(name):
            if name not in sems:
                sems[name] = ctx.enter_context(nc.semaphore(name))
            return sems[name]

        ps = ctx.enter_context(nc.psum_tensor("ps", [P, 8, 512], F32))
        ring = sb("ring", [P, SLOTS, SLOT])
        cst = sb("cst", [P, C_ALL])
        prow = sb("prow", [P, P])
        pcol = sb("pcol", [P, PARAM_N])
        xT = sb("xT", [P, KD, T])
        hT = sb("hT", [P, KD, T])
        sq = sb("sq", [P, KD, T])
        rows = sb("rows", [P, TT, D])
        arena = sb("arena", [P, 24 * T])
        uT = sb("uT", [P, CT, T + 2])
        ybT = sb("ybT", [P, CT, T])
        yaT = sb("yaT", [P, CT, T])
        gates = sb("gates", [P, 2 * KD, T])
        sp = sb("sp", [P, 4, SC])
        pT = sb("pT", [P, 2, SC])
        wr = sb("wr", [P, KD, GROUPS + EXPERTS])
        wfox = sb("wfox", [P, KD, HEADS])
        br = sb("br", [P, GROUPS + EXPERTS])
        gain = sb("gain", [P, 4, DH])
        fbias = sb("fbias", [HEADS, 1])
        nrm = sb("nrm", [P, 4, TT * HG])
        sc_c = sb("sc_c", [P, 3, KD])
        mod = sb("mod", [P, 6 * KD])
        scale1 = sb("scale1", [P, KD])
        scale2 = sb("scale2", [P, KD])
        ga1h = sb("ga1h", [P, KD])
        oghalf = sb("oghalf", [P, 1])
        lbt = sb("lbt", [P, 8, HG])
        nstat = sb("nstat", [P, 4, TT * HEADS])
        amax = sb("amax", [P, HEADS, 2])
        aneg = sb("aneg", [P, HEADS, 2])
        asum = sb("asum", [P, HEADS, 2])
        ainv = sb("ainv", [P, HEADS, 2])
        lg = sb("lg", [P, TT, GROUPS + EXPERTS])
        r1 = sb("r1", [P, 12, TT])
        rank = sb("rank", [P, TT, (1 + EXTRA_ROUNDS) * EXPERTS + 2])
        wgt = sb("wgt", [P, TT, (1 + EXTRA_ROUNDS) * EXPERTS + 2])
        flagf = sb("flagf", [1, 2])
        flag = sb("flag", [1, 1], I32)
        foxc = sb("foxc", [HEADS, T])

        first_view.close()
        twin = {name: ctx.enter_context(nc.sbuf_tensor(name + "_r", shape, F32R if dt == F32 else dt))
                for name, shape, dt in layout}

        ident = cst[:, C_IDENT:C_IDENT + P]
        mean_d = cst[:, C_MEAN_D:C_MEAN_D + P]
        mean_v = cst[:, C_MEAN_V:C_MEAN_V + P]
        ones = cst[:, C_ONES:C_ONES + P]
        causal = cst[:, C_CAUSAL:C_CAUSAL + SC]
        before = cst[:, C_BEFORE:C_BEFORE + P]
        iota = cst[:, C_IOTA:C_IOTA + CAP]
        cos = cst[:, C_COS:C_COS + TT * HALF].rearrange("p (t r) -> p t r", t=TT)
        sin = cst[:, C_SIN:C_SIN + TT * HALF].rearrange("p (t r) -> p t r", t=TT)

        def pc(name, at=0, n=None):
            a = PARAM_AT[name] + at
            return pcol[:, a:a + (dict(PARAM_ROWS)[name] if n is None else n)]

        def part(at, tiles):
            return arena[:, at * T:(at + tiles) * T]

        qrow = part(0, 4).rearrange("p (t c) -> p t c", t=TT)
        krow = part(4, 4).rearrange("p (t c) -> p t c", t=TT)
        vrow = part(8, 4).rearrange("p (t c) -> p t c", t=TT)
        qT = part(12, 4).rearrange("p (c t) -> p c t", t=T)
        kT = part(16, 4).rearrange("p (c t) -> p c t", t=T)
        xbT = part(20, 4).rearrange("p (c t) -> p c t", t=T)
        sp_flat = sp[:, :, :].rearrange("p a b -> p (a b)")
        norm_tmp = sp_flat[:, 0:2 * CW]
        rtmp = sp_flat[:, 2 * CW:].rearrange("p (n r) -> p n r", n=4)
        fl = sp_flat[0:HEADS, 0:3 * T].rearrange("p (n t) -> p n t", n=3)
        merged = gates[:, 0:KD, :]
        S = part(0, 1).rearrange("p (t c) -> p t c", t=TT)
        Sw = part(1, 1).rearrange("p (t c) -> p t c", t=TT)
        ST = part(2, 1)
        xs = part(4, 4).rearrange("p (k c) -> p k c", k=KD)
        sil = part(8, 2)
        hid = part(10, 2)
        hidT = part(12, 2).rearrange("p (f c) -> p f c", f=FT)
        ys = part(14, 4)
        zeros = part(18, 2)
        khT = xbT
        bT = uT[:, :, :].rearrange("p c t -> p (c t)")[:, 0:HG * T].rearrange("p (h t) -> p h t", h=HG)
        qhT = rows[:, 0, :].rearrange("p (h t) -> p h t", h=HG)
        irow = rows[:, 1, :].rearrange("p (t c) -> p t c", t=TT)
        E = [sq[:, 4 * n:4 * n + 4, :] for n in range(2)]
        QE = [gates[:, 4 * n:4 * n + 4, :] for n in range(2)]
        KE = [gates[:, 8 + 4 * n:12 + 4 * n, :] for n in range(2)]
        hoT = khT
        hsq = E[0]
        sgT = yaT
        scT = ybT[:, :, :].rearrange("p c t -> p (c t)").rearrange("p (n t) -> p n t", t=P)
        scX = pT[:, :, :].rearrange("p a b -> p (a b)")[:, 0:HG * P].rearrange("p (h t) -> p h t", t=P)
        fmask = rows[:, 0, 0:SC]
        rt = uT[:, :, :].rearrange("p c t -> p (c t)")[:, 0:8 * TT * EXPERTS].rearrange("p (n t e) -> p n t e", t=TT, e=EXPERTS)
        act = arena[:, 0:FFT * T].rearrange("p (f t) -> p f t", t=T)
        fsil = sp[:, 0:2, 0:T]
        prows = yaT[:, 0:2, :]
        ppT = ybT[:, 0:2, :]
        thp = [sp[:, n, 0:T] for n in range(2)]
        oT = gates[:, 0:KD, :]
        HALF_SLOT = SLOT // 2
        gates_flat = twin["gates"][:, :, :].rearrange("p k t -> p (k t)")
        lead_w = [[twin["rows"][:, :, :].rearrange("p t d -> p (t d)"), gates_flat[:, HALF_SLOT:]],
                  [gates_flat[:, 0:HALF_SLOT], twin["sq"][:, :, :].rearrange("p k t -> p (k t)")]]
        uT_flat = twin["uT"][:, :, :].rearrange("p c t -> p (c t)")
        lead_h = [uT_flat[:, k * T:(k + 1) * T] for k in range(4)] + [y[:, k, :] for y in (twin["yaT"], twin["ybT"]) for k in (2, 3)]
        pT_flat = twin["pT"][:, :, :].rearrange("p a b -> p (a b)")
        lead_act = [twin["sp"][:, n, 0:T] for n in (2, 3)] + [pT_flat[:, n * T:(n + 1) * T] for n in range(2)]
        orow = rows
        rest_w = twin["ring"]
        rest_h = twin["hT"]
        rest_act = twin["arena"][:, 0:FFT * T].rearrange("p (f t) -> p f t", t=T)

        dense_order = []
        for name in ("q", "k", "v", "xb", "cg", "bg"):
            dense_order += [f"{name}{u}" for u in range(2)]
        dense_order += [f"gate{u}" for u in range(8)] + [f"proj{j}" for j in range(KD)]
        dense_order += [f"wo{u}" for u in range(4)] + [f"moe{u}" for u in range(4)]
        for name in ("hf", "hq", "hi", "fq", "fk", "fv", "hg"):
            dense_order += [f"{name}{u}" for u in range(2)]
        dense_order += [f"gate_b{u}" for u in range(8)] + [f"proj_b{j}" for j in range(KD)]
        dense_order += [f"wo_b{u}" for u in range(4)] + [f"ffn{f}" for f in range(FFT)]
        dense_order += [f"down{u}" for u in range(4)] + [f"ple{j}" for j in range(KD)]

        def attention_order(steps, tag, bias):
            for n in range(HEADS + 3):
                names = []
                if n < HEADS:
                    names += [f"bias{n}"] * bias + [f"qk{tag}{n}"]
                if 0 <= n - 2 < HEADS:
                    names.append(f"pt{tag}{n - 2}")
                if 0 <= n - 3 < HEADS:
                    names.append(f"pv{tag}{n - 3}")
                steps.append(names)
            return steps

        att1 = attention_order([], "", False)
        att2 = attention_order([], "_b", True)
        small_order = ["params"] + [f"x{i}" for i in range(4)] + ["ms_norm1"] + [f"ada{c}" for c in range(ADA_EARLY)]
        small_order += ["rs_norm1"]
        ada_after = {4: "k1", 5: "v0", 6: "v1", 7: "xb0", 8: "xb1", 9: "cg0", 10: "gate0", 11: "gate1"}
        ada_at = {name: c for c, name in ada_after.items()}
        after1 = {"v0": ["tq0", "tq1"], "v1": ["tk0", "tk1"]}
        for n, names in enumerate(att1):
            after1.setdefault(f"{('xb', 'cg', 'bg')[n // 2]}{n % 2}" if n < 6 else f"gate{n - 6}", []).extend(names)
        for name in dense_order:
            small_order += after1.get(name, []) + ([f"ada{ada_at[name]}"] if name in ada_at else [])
        small_order += ["ms_norm2", "rs_norm2", "logits"] + [f"h2r{i}" for i in range(4)] + ["rank"]
        n_block1 = len(small_order)
        small_order += ["ms_mix", "rs_mix", "fox_f"]
        level_names = ["cross"] + [f"lev{m}" for m in LEVELS] + ["diag"]
        level_units = {n: ["cross"] if n == "cross" else [n + "a", n + "b"] for n in level_names}
        after2 = {}
        slots2 = ["fq0", "fq1", "fk0", "fk1", "fv0", "fv1", "hg0", "hg1", "hg1"]
        for n, at in zip(level_names, slots2):
            after2.setdefault(at, []).append(level_units[n])
        after2["fk0"].append(["tq_b0", "tq_b1"])
        after2["fv0"].append(["tk_b0", "tk_b1"])
        for n, names in enumerate(att2):
            after2.setdefault(f"gate_b{min(n, 7)}", []).append(names)
        after2["gate_b0"].insert(0, ["ho0", "ho1"])
        after2["gate_b1"].insert(0, ["ms_h"])
        after2["gate_b2"].insert(0, ["rs_h0", "rs_h1"])
        for name in dense_order:
            for names in after2.get(name, []):
                small_order += names
        small_order += ["ms_ffn", "rs_ffn", "ms_ple", "rs_ple", "pp", "o00", "o10", "o01", "o11"]

        dense_released = {f"moe{u}": (sem("x2_ready"), 2 * u + 2) for u in range(4)}
        for u in range(2):
            for name in ("q", "k", "v", "fq", "fk", "fv"):
                dense_released[f"{name}{u}"] = sem(f"{name}_rows"), u + 1
            for name, ready in (("xb", "xb_ready"), ("bg", "yb_ready"), ("hf", "hf_exp"), ("hi", "hi_ready")):
                dense_released[f"{name}{u}"] = sem(ready), u + 1
        for tag in ("", "_b"):
            for n in range(8):
                dense_released[f"gate{tag}{n}"] = sem(f"gates_ready{tag}"), n + 1
                dense_released[f"proj{tag}{n}"] = sem(f"merged_ready{tag}"), n + 1
        for u in range(4):
            for name, ready in (("wo", "x1_ready"), ("wo_b", "x3_ready"), ("down", "x4_ready")):
                dense_released[f"{name}{u}"] = sem(ready), 2 * u + 2
        for f in range(FFT):
            dense_released[f"ffn{f}"] = sem("act_ready"), f + 1
        small_released = {"params": (sem("pcol_ready"), 1), "pp": (sem("ppT_ready"), 1)}
        for i in range(4):
            small_released[f"x{i}"] = sem("xT_ready"), i + 1
            small_released[f"h2r{i}"] = sem("h2_rows_ready"), i + 1
        for n, name in enumerate(("o00", "o10", "o01", "o11")):
            small_released[name] = sem("out_ready"), n + 1
        for u in range(2):
            small_released[f"ho{u}"] = sem("ho_ready"), u + 1
            for tag in ("", "_b"):
                small_released[f"tq{tag}{u}"] = sem("qT_ready" + tag), u + 1
                small_released[f"tk{tag}{u}"] = sem("kT_ready" + tag), u + 1
        for name, ready in (("norm1", "h1_scaled"), ("norm2", "h2_scaled"), ("mix", "hm_ready"), ("ffn", "hf_ready"),
                            ("ple", "hp_ready")):
            small_released["rs_" + name] = sem(ready), KD
        for c in range(ADA):
            small_released[f"ada{c}"] = sem("mod_raw"), c + 1
        for h in range(HEADS):
            for tag, y in (("", "ya_ready"), ("_b", "yb_ready_b")):
                small_released[f"pt{tag}{h}"] = sem("pT_ready" + tag), h + 1
                small_released[f"pv{tag}{h}"] = sem(y), h + 1
        dense = Rotation(ps, 0, 4, dense_order, sem("dense_done"), [sem(f"dense_free{b}") for b in range(4)],
                         dense_released, [f"moe{u}" for u in range(4)])
        small = Rotation(ps, 4, 4, small_order, sem("small_done"), [sem(f"small_free{b}") for b in range(4)],
                         small_released)
        GA, GB, HA, HB = (ps[:, 4 + b, :] for b in range(4))

        chunks = []
        chunk_of = {}

        def cols(w, at, n=COL):
            return w[:, at:at + n].rearrange("(k p) n -> p k n", p=P)

        def chunk(name, loads, released):
            chunk_of[name] = len(chunks)
            chunks.append((loads, released))

        def wide(slot):
            return ring[:, slot, :].rearrange("p (k n) -> p k n", k=KD)

        def tall(slot):
            return ring[:, slot, :].rearrange("p (k n) -> p k n", n=D)

        def after(unit):
            return dense.done, dense.done_at[unit]

        w_ada, w_in, w_in2 = A["w_ada"][0], A["w_in"][0], A["w_in_2"][0]

        def ada(n):
            chunk(f"ada{n}", [(lambda s: wide(s), cols(w_ada, n * COL))], (sem("ada_sums"), n + 1))

        IN1 = dict(q=0, k=1, v=2, xb=3, bg=4, cg=5, gate0=6, gate1=7, gate2=8, gate3=9)
        for n in range(ADA_EARLY):
            ada(n)
        for name, later in (("q", ()), ("k", (4, 5)), ("v", (6,)), ("xb", (7,)), ("cg", (8,)), ("bg", (9,)),
                            ("gate0", (10,)), ("gate1", (11,)), ("gate2", ()), ("gate3", ())):
            last_unit = f"gate{2 * int(name[4]) + 1}" if name.startswith("gate") else name + "1"
            chunk(name, [(lambda s: wide(s), cols(w_in, IN1[name] * COL))], after(last_unit))
            for n in later:
                ada(n)
        chunk("pa", [(lambda s: tall(s), A["w_pa"][0].rearrange("(k p) n -> p k n", p=P))], after(f"proj{KD - 1}"))
        chunk("pb", [(lambda s: tall(s), A["w_pb"][0].rearrange("(k p) n -> p k n", p=P))], after(f"proj{KD - 1}"))
        for n in range(2):
            chunk(f"wo{n}", [(lambda s: wide(s), cols(A["w_o"][0], n * COL))], after(f"wo{2 * n + 1}"))

        moe_first = len(chunks)
        moe_slot = [(moe_first + n) % SLOTS for n in range(6)]
        MOE_USED = ("w1_used", "w1_used", "w3_used", "w3_used", "ys1_done", "ys1_done")
        for n in range(PAIRS):
            for name in MOE_USED:
                chunk(f"moe{len(chunks)}", None, (sem("moe_" + name), n + 1))
        block2_first = len(chunks)
        IN2 = dict(hq=0, hf=512, hi=1024, hg=1536, fq=2048, fk=2560, fv=3072)
        GATE2 = 3584 + HEADS
        for name in ("hf", "hq", "hi", "fq", "fk", "fv", "hg"):
            chunk(name, [(lambda s: wide(s), cols(w_in2, IN2[name]))], after(name + "1"))
        for n in range(4):
            chunk(f"gate_b{n}", [(lambda s: wide(s), cols(w_in2, GATE2 + n * COL))], after(f"gate_b{2 * n + 1}"))
        for name in ("a", "b"):
            chunk("branch_" + name, [(lambda s: tall(s), A[f"w_branch_{name}_2"][0].rearrange("(k p) n -> p k n", p=P))],
                  after(f"proj_b{KD - 1}"))
        for n in range(2):
            chunk(f"wo_b{n}", [(lambda s: wide(s), cols(A["w_out_2"][0], n * COL))], after(f"wo_b{2 * n + 1}"))
        wg, wu, wd = A["w_ffn_gate_2"][0], A["w_ffn_up_2"][0], A["w_ffn_down_2"][0]
        FC = COL // 2
        FFN_CHUNKS = DFF // FC
        for n in range(FFN_CHUNKS):
            chunk(f"ffn{n}", [(lambda s: wide(s)[:, :, 0:FC], cols(wg, n * FC, FC)),
                              (lambda s: wide(s)[:, :, FC:COL], cols(wu, n * FC, FC))], after(f"ffn{2 * n + 1}"))
        DOWN = []
        for n in range(0, FFT, 4):
            m = min(4, FFT - n)
            DOWN.append((n, m))
            chunk(f"down{n // 4}", [(lambda s, m=m: tall(s)[:, 0:m, :],
                                     wd[n * P:(n + m) * P, :].rearrange("(k p) n -> p k n", p=P))],
                  (sem("down_tiles"), n + m) if n + m < FFT else after("down3"))
        split_chunks = [f"ffn{n}" for n in range(FFN_CHUNKS)] + [f"down{n}" for n in range(len(DOWN))]
        for n in range(2):
            chunk(f"ple_gate{n}", [(lambda s: wide(s), cols(A["w_ple_gate_2"][0], n * COL))], after(f"ple{4 * n + 3}"))
        chunk("ple_proj", [(lambda s: tall(s)[:, 0:2, :], A["w_ple_proj_2"][0].rearrange("(k p) n -> p k n", p=P))],
              after(f"ple{KD - 1}"))

        landed, arrive_at = [0] * SLOTS, []
        for n, (loads, _) in enumerate(chunks):
            landed[n % SLOTS] += 16 * (1 if loads is None else len(loads))
            arrive_at.append(landed[n % SLOTS])
        chunk_in = [sem(f"chunk_in{s}") for s in range(SLOTS)]
        spare_in = [sem(f"spare_in{s}") for s in range(SLOTS)]

        def arrived(pe, name):
            n = chunk_of[name]
            pe.wait_ge(chunk_in[n % SLOTS], arrive_at[n])
            return n % SLOTS

        def ada_acc(c):
            a = 2 * KD - 4 + 2 * (c % 2)
            return gates[:, a:a + 2, :].rearrange("p k t -> p (k t)")

        def halves(m):
            slot = chunk_of[split_chunks[m]] % SLOTS
            last = DOWN[-1][1] * D if m == len(split_chunks) - 1 else SLOT
            out = []
            for n in range(2):
                a, b = n * HALF_SLOT, min((n + 1) * HALF_SLOT, last)
                if a < b:
                    out.append((ring[:, slot, a:b], rest_w[:, slot, a:b], lead_w[m % 2][n][:, 0:b - a]))
            return out

        def lead_at(m, at):
            return lead_w[m % 2][at // HALF_SLOT][:, at % HALF_SLOT:at % HALF_SLOT + P]

        def rest_at(m, at):
            return rest_w[:, chunk_of[split_chunks[m]] % SLOTS, at:at + P]

        lead_done = [0]
        for m in range(len(split_chunks)):
            lead_done.append(lead_done[-1] + len(halves(m)))
        rest_pool = [0]
        for m in range(len(split_chunks)):
            rest_pool.append(rest_pool[-1] + len(halves(m)) - 1)

        moe_in_base = [arrive_at[moe_first + n] for n in range(6)]
        expert_w = [A[name][0] for name in ("w1", "w1", "w3", "w3", "w2", "w2")]

        def expert_load(sp_, n, pair, signal):
            src = expert_w[n][bass.ds(2 * pair + n % 2, 1)].rearrange("e (k p) n -> p (e k) n", p=P)
            view = tall(moe_slot[n]) if n >= 4 else wide(moe_slot[n])
            sp_.dma_start(view, src).then_inc(signal[moe_slot[n]], 16)

        block = ctx.enter_context(nc.Block())

        @block.sync
        def _(sp_):
            def load(n):
                if n >= SLOTS:
                    sp_.wait_ge(*chunks[n - SLOTS][1])
                for view, src in chunks[n][0]:
                    sp_.dma_start(view(n % SLOTS), src).then_inc(chunk_in[n % SLOTS], 16)

            sp_.dma_start(rows[:, :, :], A["x"][0].rearrange("(t p) d -> p t d", p=P)).then_inc(sem("x_in"), 16)
            sp_.dma_start(cst[:, :], consts).then_inc(sem("cst_in"), 16)
            sp_.wait_ge(sem("params_in"), 16 * len(PARAM_ROWS))
            for n in range(moe_first):
                load(n)
            for n in range(6):
                sp_.wait_ge(*chunks[moe_first + n - SLOTS][1])
                expert_load(sp_, n, 0, chunk_in)
            sp_.wait_ge(sem("flag_ready"), 1)
            more = sp_.value_load(flag[0:1, 0:1], min_val=0, max_val=1)
            with sp_.Fori(1, PAIRS) as i:
                for n, name in enumerate(MOE_USED):
                    sp_.wait_ge(sem("moe_" + name), i)
                    expert_load(sp_, n, i, chunk_in)
            with sp_.If(more > 0):
                for n in range(block2_first - SLOTS, block2_first):
                    sp_.wait_ge(*chunks[n][1])
                for n in range(6):
                    expert_load(sp_, n, 0, spare_in)
                with sp_.Fori(1, PAIRS * EXTRA_ROUNDS) as i:
                    e = sp_.snap(i % PAIRS)
                    for n, name in enumerate(MOE_USED):
                        sp_.wait_ge(sem("moe_" + name), i + PAIRS)
                        expert_load(sp_, n, e, spare_in)
                sp_.wait_ge(sem("moe_ys1_done"), PAIRS + PAIRS * EXTRA_ROUNDS)
            for n in range(block2_first, len(chunks)):
                load(n)
            for n, (t, half) in enumerate(((0, 0), (1, 0), (0, 1), (1, 1))):
                sp_.wait_ge(sem("out_ready"), n + 1)
                sp_.dma_start(out[0, t * P:(t + 1) * P, half * 512:half * 512 + 512],
                              orow[:, t, half * 512:half * 512 + 512]).then_inc(sem("out_sent"), 16)
            sp_.wait_ge(sem("out_sent"), 64)

        @block.gpsimd
        def _(pool):
            nc.gpsimd.memset(uT[:, :, 0:2], 0.0).then_inc(sem("pad_ready"), 1)
            pool.dma_start(br[:, 0:GROUPS], A["b_rg"].to_broadcast([P, GROUPS])).then_inc(sem("route_in"), 16)
            pool.dma_start(br[:, GROUPS:], A["b_re"].to_broadcast([P, EXPERTS])).then_inc(sem("route_in"), 16)
            pool.dma_start(wr[:, :, 0:GROUPS], A["w_rg"][0].rearrange("(k p) n -> p k n", p=P)).then_inc(sem("route_in"), 16)
            pool.dma_start(wr[:, :, GROUPS:], A["w_re"][0].rearrange("(k p) n -> p k n", p=P)).then_inc(sem("route_in"), 16)
            pool.dma_start(wfox[:, :, :], cols(w_in2, 3584, HEADS)).then_inc(sem("fox_in"), 16)
            pool.dma_start(fbias[:, :], A["fox_f_bias_2"].rearrange("a h -> h a")).then_inc(sem("fox_in"), 16)
            dense.ready(pool, f"proj{KD - 1}")
            nc.gpsimd.memset(scT, 0.0).then_inc(sem("scores_zeroed"), 1)
            for n in range(len(level_names) - 1):
                pool.wait_ge(sem("decay_ready"), n + 1)
                if n >= 2:
                    small.ready(pool, level_units[level_names[n - 2]][-1])
                nc.gpsimd.tensor_tensor(KE[n % 2], khT, E[n % 2], ALU.mult).then_inc(sem("ke_ready"), 1)
            dense.ready(pool, f"proj_b{KD - 1}")
            pool.dma_start(prows, A["p_2"][0, 0].rearrange("(t p) n -> p t n", p=P)).then_inc(sem("p_in"), 16)
            for m in range(len(split_chunks)):
                if len(halves(m)) == 2:
                    w, rest, lead = halves(m)[1]
                    pool.wait_ge(sem("w_lead"), lead_done[m + 1])
                    nc.gpsimd.tensor_tensor(rest, w, lead.bitcast(F32), ALU.subtract).then_inc(sem("w_rest_b"), 1)

        @block.tensor
        def _(pe):
            mm = nc.tensor.matmul

            def square_sums(name, ready):
                o = small.claim(pe, "ms_" + name)
                for k in range(KD):
                    pe.wait_ge(*ready(k))
                    for t in range(TT):
                        last = mm(o[:, t:t + 1], lhsT=sq[:, k, t * P:(t + 1) * P], rhs=mean_d[:, 0:1],
                                  start=k == 0 and t == 0, stop=k == KD - 1, skip_group_check=True)
                last.then_inc(small.done, 1)

            def token_factors(unit, columns, count):
                o = small.claim(pe, unit)
                pe.wait_ge(sem("inv_norm_ready"), count)
                for n, c in enumerate(columns):
                    last = mm(o[:, n * P:(n + 1) * P], lhsT=nrm[:, 0, c:c + 1].to_broadcast([P, P]), rhs=ident,
                              start=True, stop=True)
                last.then_inc(small.done, 1)

            def token_rows(name, unit, slot, h_ready):
                o = dense.claim(pe, name)
                for k in range(KD):
                    pe.wait_ge(sem(h_ready), k + 1)
                    last = mm(o, lhsT=hT[:, k, unit * P:(unit + 1) * P], rhs=wide(slot)[:, k, :],
                              start=k == 0, stop=k == KD - 1)
                last.then_inc(dense.done, 1)

            def channel_tiles(name, unit, slot, h_ready, moving):
                o = dense.claim(pe, name)
                for j in range(2):
                    at = (2 * unit + j) * P
                    for k in range(KD):
                        pe.wait_ge(sem(h_ready), k + 1)
                        last = mm(o[:, j * T:(j + 1) * T], lhsT=wide(slot)[:, k, at:at + P], rhs=moving[:, k, :],
                                  start=k == 0, stop=k == KD - 1)
                last.then_inc(dense.done, 1)

            def modulation(c):
                o = small.claim(pe, f"ada{c}")
                pe.wait_ge(sem("ada_sums"), c + 1)
                for j in range(COL // P):
                    last = mm(o[:, j:j + 1], lhsT=ada_acc(c)[:, j * P:(j + 1) * P], rhs=ones[:, 0:1], start=True, stop=True)
                last.then_inc(small.done, 1)

            def head_transposes(name, row, ready):
                pe.wait_ge(sem(ready), 1)
                for u in range(2):
                    o = small.claim(pe, f"{name}{u}")
                    for j in range(2):
                        for t in range(TT):
                            c = 2 * u + j
                            last = nc.tensor.transpose(o[:, j * T + t * P:j * T + (t + 1) * P],
                                                       row[:, t, c * P:(c + 1) * P], ident)
                    last.then_inc(small.done, 1)

            def scores(tag, h):
                o = small.claim(pe, f"qk{tag}{h}")
                pe.wait_ge(sem(f"qT_ready{tag}"), h // 4 + 1)
                pe.wait_ge(sem(f"kT_ready{tag}"), h // 4 + 1)
                a = DH * (h % 2)
                mm(o[:, 0:P], lhsT=qT[a:a + DH, h // 2, 0:P], rhs=kT[a:a + DH, h // 2, 0:P], start=True, stop=True)
                mm(o[:, P:SC], lhsT=qT[a:a + DH, h // 2, P:T], rhs=kT[a:a + DH, h // 2, :], start=True,
                   stop=True).then_inc(small.done, 1)

            def probs_transposes(tag, h):
                o = small.claim(pe, f"pt{tag}{h}")
                pe.wait_ge(sem(f"probs_ready{tag}"), h + 1)
                for n in range(3):
                    last = nc.tensor.transpose(o[:, n * P:(n + 1) * P], sp[:, h % 4, n * P:(n + 1) * P], ident)
                last.then_inc(small.done, 1)

            def weighted_values(tag, h):
                o = small.claim(pe, f"pv{tag}{h}")
                pe.wait_ge(sem(f"pT_ready{tag}"), h + 1)
                a = DH * (h % 2)
                p = pT[:, h % 2, :]
                mm(o[a:a + DH, 0:P], lhsT=vrow[:, 0, h * DH:(h + 1) * DH], rhs=p[:, 0:P], start=True, stop=True)
                for t in range(TT):
                    last = mm(o[a:a + DH, P:T], lhsT=vrow[:, t, h * DH:(h + 1) * DH], rhs=p[:, (1 + t) * P:(2 + t) * P],
                              start=t == 0, stop=t == 1)
                last.then_inc(small.done, 1)

            def key_bias(h):
                o = small.claim(pe, f"bias{h}")
                pe.wait_ge(sem("fox_c_ready"), 1)
                mm(o[:, 0:T], lhsT=ident[0:HEADS, h:h + 1].to_broadcast([HEADS, P]), rhs=foxc[:, :], start=True,
                   stop=True).then_inc(small.done, 1)

            def attention_step(tag, names):
                for name in names:
                    h = int(name[-1])
                    if name.startswith("bias"):
                        key_bias(h)
                    elif name.startswith("qk"):
                        scores(tag, h)
                    elif name.startswith("pt"):
                        probs_transposes(tag, h)
                    else:
                        weighted_values(tag, h)

            def branch_products(tag, slot_a, slot_b, ready_a, ready_b):
                for j in range(KD):
                    o = dense.claim(pe, f"proj{tag}{j}")
                    for n, (slot, y) in enumerate(((slot_a, yaT), (slot_b, ybT))):
                        pe.wait_ge(*(ready_a, ready_b)[n])
                        for k in range(CT):
                            last = mm(o[:, n * T:(n + 1) * T], lhsT=tall(slot)[:, k, j * P:(j + 1) * P], rhs=y[:, k, :],
                                      start=k == 0, stop=k == CT - 1)
                    last.then_inc(dense.done, 1)

            pe.wait_ge(sem("cst_in"), 16)
            pe.wait_ge(sem("params_in"), 16 * len(PARAM_ROWS))
            o = small.claim(pe, "params")
            nc.tensor.transpose(o[:, 0:PARAM_N], prow[0:PARAM_N, :], ident[0:PARAM_N, 0:PARAM_N]).then_inc(small.done, 1)
            pe.wait_ge(sem("x_in"), 16)
            for i in range(4):
                o = small.claim(pe, f"x{i}")
                for kk in range(2):
                    for t in range(TT):
                        k = 2 * i + kk
                        last = nc.tensor.transpose(o[:, kk * T + t * P:kk * T + (t + 1) * P],
                                                   rows[:, t, k * P:(k + 1) * P], ident)
                last.then_inc(small.done, 1)
            square_sums("norm1", lambda k: (sem("sq_norm1"), k // 2 + 1))
            for c in range(ADA_EARLY):
                modulation(c)
            token_factors("rs_norm1", range(TT), 1)
            for name in ("q", "k", "v", "xb", "cg", "bg"):
                slot = arrived(pe, name)
                for u in range(2):
                    if name in "qkv":
                        token_rows(f"{name}{u}", u, slot, "h1_ready")
                    else:
                        channel_tiles(f"{name}{u}", u, slot, "h1_ready", hT)
                    if name == "v":
                        head_transposes(("tq", "tk")[u], (qrow, krow)[u], ("q_normed", "k_normed")[u])
                    if name in ("xb", "cg", "bg"):
                        n = 2 * ("xb", "cg", "bg").index(name) + u
                        attention_step("", att1[n])
                    if f"{name}{u}" in ada_at:
                        modulation(ada_at[f"{name}{u}"])
            for u in range(8):
                if u % 2 == 0:
                    slot = arrived(pe, f"gate{u // 2}")
                channel_tiles(f"gate{u}", u % 2, slot, "h1_ready", hT)
                if 6 + u < len(att1):
                    attention_step("", att1[6 + u])
                if f"gate{u}" in ada_at:
                    modulation(ada_at[f"gate{u}"])
            slots = arrived(pe, "pa"), arrived(pe, "pb")
            branch_products("", *slots, (sem("ya_ready"), HEADS), (sem("yb_ready"), 2))
            for u in range(4):
                if u % 2 == 0:
                    slot = arrived(pe, f"wo{u // 2}")
                channel_tiles(f"wo{u}", u % 2, slot, "merged_ready", merged)
            square_sums("norm2", lambda k: (sem("sq_norm2"), k + 1))
            pe.wait_ge(sem("zeros_ready"), 1)
            zero = zeros.bitcast(BF16)
            for u in range(4):
                mm(dense.claim(pe, f"moe{u}"), lhsT=zero[:, 0:P], rhs=zero[:, 0:512], start=True, stop=True)
            token_factors("rs_norm2", range(TT), 2)
            pe.wait_ge(sem("route_in"), 64)
            o = small.claim(pe, "logits")
            for k in range(KD):
                pe.wait_ge(sem("h2_ready"), k + 1)
                for t in range(TT):
                    last = mm(o[:, t * 64:t * 64 + GROUPS + EXPERTS], lhsT=hT[:, k, t * P:(t + 1) * P], rhs=wr[:, k, :],
                              start=k == 0 and t == 0, stop=k == KD - 1, skip_group_check=True)
            last.then_inc(small.done, 1)
            for i in range(4):
                o = small.claim(pe, f"h2r{i}")
                for j in range(4):
                    k = 4 * (i % 2) + j
                    last = nc.tensor.transpose(o[:, j * P:(j + 1) * P], hT[:, k, (i // 2) * P:(i // 2 + 1) * P], ident)
                last.then_inc(small.done, 1)
            o = small.claim(pe, "rank")
            pe.wait_ge(sem("chosen_ready"), 1)
            chosen = rt[:, 0, :, :]
            mm(o[:, 0:32], lhsT=before, rhs=chosen[:, 0, :], start=True, stop=True)
            mm(o[:, 32:64], lhsT=before, rhs=chosen[:, 1, :], start=True, stop=False)
            mm(o[:, 32:64], lhsT=ones, rhs=chosen[:, 0, :], start=False, stop=True)
            mm(o[:, 64:96], lhsT=ones, rhs=chosen[:, 0, :], start=True, stop=False)
            mm(o[:, 64:96], lhsT=ones, rhs=chosen[:, 1, :], start=False, stop=True).then_inc(small.done, 1)
            for name in small_order[n_block1 - 4:n_block1]:
                pe.wait_ge(*small.released[name])
            pe.wait_ge(sem("h2_rows_ready"), 4)

            def gather():
                for n, G in enumerate((GA, GB)):
                    for j in range(4):
                        k = 4 * n + j
                        for t in range(TT):
                            last = mm(G[:, j * P:(j + 1) * P], lhsT=rows[:, t, k * P:(k + 1) * P], rhs=S[:, t, :],
                                      start=t == 0, stop=t == TT - 1)
                    last.then_inc(sem(f"moe_gather{n}_done"), 1)

            def slots_of(e):
                return slice(e * CAP, (e + 1) * CAP)

            def up(n, H, i, signal, base):
                for e in range(2):
                    pe.wait_ge(signal[moe_slot[2 * n + e]], base[2 * n + e] + 16 * i)
                for k in range(KD):
                    for e in range(2):
                        last = mm(H[slots_of(e), :], lhsT=xs[:, k, slots_of(e)], rhs=wide(moe_slot[2 * n + e])[:, k, :],
                                  start=k == 0, stop=k == KD - 1)
                last.then_inc(sem(("moe_w1_used", "moe_w3_used")[n]), 1)

            def pair_of_experts(i, done, ahead, signal, base):
                for n in range(2):
                    pe.wait_ge(sem(f"moe_xs{n}_ready"), i + ahead + 1)
                up(0, HA, i, signal, base)
                up(1, HB, i, signal, base)
                pe.wait_ge(sem("moe_s_ready"), 4 * i + 4 * ahead + 8)
                gather()
                pe.wait_ge(sem("moe_xs0_ready"), i + ahead + 2)
                pe.wait_ge(sem("moe_hid_ready"), i + done + 1)
                for f in range(FT):
                    last = nc.tensor.transpose(GA[:, f * P:(f + 1) * P], hid[:, f * P:(f + 1) * P], ident)
                last.then_inc(sem("moe_hidT_done"), 1)
                pe.wait_ge(sem("moe_xs1_ready"), i + ahead + 2)
                pe.wait_ge(sem("moe_sw_ready"), 4 * i + 4 * done + 4)
                for t in range(TT):
                    last = nc.tensor.transpose(GB[:, t * P:(t + 1) * P], Sw[:, t, :], ident)
                last.then_inc(sem("moe_st_done"), 1)
                for e in range(2):
                    pe.wait_ge(signal[moe_slot[4 + e]], base[4 + e] + 16 * i)
                pe.wait_ge(sem("moe_hidT_ready"), i + done + 1)
                for half, Y in enumerate((HA, HB)):
                    for f in range(FT):
                        for e in range(2):
                            last = mm(Y[slots_of(e), :], lhsT=hidT[:, f, slots_of(e)],
                                      rhs=tall(moe_slot[4 + e])[:, f, half * 512:half * 512 + 512],
                                      start=f == 0, stop=f == FT - 1)
                    last.then_inc(sem(f"moe_ys{half}_done"), 1)
                pe.wait_ge(sem("moe_st_ready"), i + done + 1)
                for half in range(2):
                    pe.wait_ge(sem(f"moe_ys{half}_ready"), i + done + 1)
                    for j in range(4 * half, 4 * half + 4):
                        sums = dense.bank(f"moe{j // 2}")
                        last = mm(sums[:, (j % 2) * T:(j % 2 + 1) * T], lhsT=ys[:, j * P:(j + 1) * P], rhs=ST,
                                  start=False, stop=True, skip_group_check=True)
                last.then_inc(sem("moe_combined"), 1)

            def experts(rounds, done, ahead, signal, base):
                pe.wait_ge(sem("moe_s_ready"), 4 * ahead + 4)
                gather()
                with pe.Fori(0, PAIRS * rounds) as i:
                    pair_of_experts(i, done, ahead, signal, base)
                for n in range(2):
                    pe.wait_ge(sem(f"moe_xs{n}_ready"), PAIRS * rounds + ahead + 1)

            pe.wait_ge(sem("flag_ready"), 1)
            more = pe.value_load(flag[0:1, 0:1], min_val=0, max_val=1)
            experts(1, 0, 0, chunk_in, moe_in_base)
            with pe.If(more > 0):
                experts(EXTRA_ROUNDS, PAIRS, PAIRS + 1, spare_in, [16] * 6)

            square_sums("mix", lambda k: (sem("sq_mix"), k + 1))
            token_factors("rs_mix", range(TT), 3)

            def fox_gate_logits():
                o = small.claim(pe, "fox_f")
                pe.wait_ge(sem("fox_in"), 32)
                for k in range(KD):
                    last = mm(o[0:HEADS, 0:T], lhsT=wfox[:, k, :], rhs=hT[:, k, :], start=k == 0, stop=k == KD - 1)
                last.then_inc(small.done, 1)

            def level(name):
                n = level_names.index(name)
                if name != "diag":
                    pe.wait_ge(sem("qe_ready"), n + 1)
                    pe.wait_ge(sem("ke_ready"), n + 1)
                q, k = (qhT, khT) if name == "diag" else (QE[n % 2], KE[n % 2])
                if name == "cross":
                    o = small.claim(pe, "cross")
                    for h in range(HG):
                        last = mm(o[:, h * P:(h + 1) * P], lhsT=k[:, h, 0:P], rhs=q[:, h, P:T], start=True, stop=True)
                    last.then_inc(small.done, 1)
                    return
                for u, unit in enumerate(level_units[name]):
                    o = small.claim(pe, unit)
                    for j in range(4):
                        h, t = (4 * u + j) // TT, j % TT
                        last = mm(o[:, j * P:(j + 1) * P], lhsT=k[:, h, t * P:(t + 1) * P],
                                  rhs=q[:, h, t * P:(t + 1) * P], start=True, stop=True)
                    last.then_inc(small.done, 1)

            def hgrn_values():
                pe.wait_ge(*small.released["diagb"])
                for u in range(2):
                    o = small.claim(pe, f"ho{u}")
                    for j in range(2):
                        h = 2 * u + j
                        v = irow[:, :, h * P:(h + 1) * P]
                        mm(o[:, j * T:j * T + P], lhsT=v[:, 0, :], rhs=scT[:, 2 * h, :], start=True, stop=True)
                        mm(o[:, j * T + P:(j + 1) * T], lhsT=v[:, 0, :], rhs=scX[:, h, :], start=True, stop=False)
                        last = mm(o[:, j * T + P:(j + 1) * T], lhsT=v[:, 1, :], rhs=scT[:, 2 * h + 1, :],
                                  start=False, stop=True)
                    last.then_inc(small.done, 1)

            def hgrn_norm():
                o = small.claim(pe, "ms_h")
                for c in range(HG * TT):
                    h, t = divmod(c, TT)
                    pe.wait_ge(sem("hsq_ready"), h // 2 + 1)
                    last = mm(o[:, c:c + 1], lhsT=hsq[:, h, t * P:(t + 1) * P], rhs=mean_v[:, 0:1], start=True, stop=True)
                last.then_inc(small.done, 1)

            def between(name):
                for names in after2.get(name, []):
                    if names[0].startswith(("tq", "tk")):
                        which = names[0][1]
                        head_transposes(f"t{which}_b", qrow if which == "q" else krow, f"{which}_normed_b")
                    elif names[0] == "ho0":
                        hgrn_values()
                    elif names[0] == "ms_h":
                        hgrn_norm()
                    elif names[0] == "rs_h0":
                        for u in range(2):
                            token_factors(f"rs_h{u}", range(2 * u * TT, 2 * (u + 1) * TT), 4)
                    elif names[0].startswith(("cross", "lev", "diag")):
                        level("cross" if names[0] == "cross" else names[0][:-1])
                    else:
                        attention_step("_b", names)

            for name in ("hf", "hq", "hi", "fq", "fk", "fv", "hg"):
                slot = arrived(pe, name)
                for u in range(2):
                    if name in ("hi", "fq", "fk", "fv"):
                        token_rows(f"{name}{u}", u, slot, "hm_ready")
                    else:
                        channel_tiles(f"{name}{u}", u, slot, "hm_ready", hT)
                    if name == "hf" and u == 0:
                        fox_gate_logits()
                    between(f"{name}{u}")
            for u in range(8):
                if u % 2 == 0:
                    slot = arrived(pe, f"gate_b{u // 2}")
                channel_tiles(f"gate_b{u}", u % 2, slot, "hm_ready", hT)
                between(f"gate_b{u}")
            slots = arrived(pe, "branch_a"), arrived(pe, "branch_b")
            branch_products("_b", *slots, (sem("ya_ready_b"), 2), (sem("yb_ready_b"), HEADS))
            for u in range(4):
                if u % 2 == 0:
                    slot = arrived(pe, f"wo_b{u // 2}")
                channel_tiles(f"wo_b{u}", u % 2, slot, "merged_ready_b", merged)
            square_sums("ffn", lambda k: (sem("sq_ffn"), k + 1))
            token_factors("rs_ffn", range(TT), 5)

            def three_products(o, m, at, lead, rest, start, stop):
                mm(o, lhsT=lead_at(m, at), rhs=lead, start=start, stop=False, skip_group_check=True)
                mm(o, lhsT=lead_at(m, at), rhs=rest, start=False, stop=False, skip_group_check=True)
                return mm(o, lhsT=rest_at(m, at), rhs=lead, start=False, stop=stop, skip_group_check=True)

            for f in range(FFT):
                m = f // 2
                o = dense.claim(pe, f"ffn{f}")
                for n in range(2):
                    for k in range(KD):
                        pe.wait_ge(sem("h_rest"), k + 1)
                        pe.wait_ge(*((sem("w_rest_a"), m + 1) if k < 4 else (sem("w_rest_b"), rest_pool[m + 1])))
                        last = three_products(o[:, n * T:(n + 1) * T], m, k * COL + n * FC + (f % 2) * P, lead_h[k], rest_h[:, k, :],
                                              k == 0 and n == 0, k == KD - 1)
                last.then_inc(dense.done, 1)
            downs = [dense.claim(pe, f"down{u}") for u in range(4)]
            for c, (first, n_tiles) in enumerate(DOWN):
                m = FFN_CHUNKS + c
                for f in range(first, first + n_tiles):
                    pe.wait_ge(sem("act_rest"), f + 1)
                    pe.wait_ge(*((sem("w_rest_a"), m + 1) if f - first < 2 else (sem("w_rest_b"), rest_pool[m + 1])))
                    for j in range(KD):
                        last = three_products(downs[j // 2][:, (j % 2) * T:(j % 2 + 1) * T], m, (f - first) * D + j * P,
                                              lead_act[f % 4], rest_act[:, f, :], f == 0 and j % 2 == 0, f == FFT - 1)
                        if f == FFT - 1 and j % 2 == 1:
                            last.then_inc(dense.done, 1)
                    if f < FFT - 1:
                        last.then_inc(sem("down_tiles"), 1)
            square_sums("ple", lambda k: (sem("sq_ple"), k + 1))
            token_factors("rs_ple", range(TT), 6)
            o = small.claim(pe, "pp")
            pe.wait_ge(sem("p_in"), 16)
            for k in range(2):
                for t in range(TT):
                    last = nc.tensor.transpose(o[:, k * T + t * P:k * T + (t + 1) * P], prows[:, t, k * P:(k + 1) * P], ident)
            last.then_inc(small.done, 1)

            def result_rows(half):
                for t in range(TT):
                    o = small.claim(pe, f"o{t}{half}")
                    for j in range(4):
                        pe.wait_ge(sem("o_ready"), 4 * half + j + 1)
                        last = nc.tensor.transpose(o[:, j * P:(j + 1) * P], oT[:, 4 * half + j, t * P:(t + 1) * P], ident)
                    last.then_inc(small.done, 1)

            sproj = None
            for j in range(KD):
                if j % 4 == 0:
                    slot = arrived(pe, f"ple_gate{j // 4}")
                o = dense.claim(pe, f"ple{j}")
                for k in range(KD):
                    pe.wait_ge(sem("hp_ready"), k + 1)
                    mm(o[:, 0:T], lhsT=wide(slot)[:, k, (j % 4) * P:(j % 4 + 1) * P], rhs=hT[:, k, :],
                       start=k == 0, stop=k == KD - 1)
                if sproj is None:
                    sproj = arrived(pe, "ple_proj")
                    pe.wait_ge(sem("ppT_ready"), 1)
                for k in range(2):
                    last = mm(o[:, T:2 * T], lhsT=tall(sproj)[:, k, j * P:(j + 1) * P], rhs=ppT[:, k, :],
                              start=k == 0, stop=k == 1)
                last.then_inc(dense.done, 1)
                if j == 5:
                    result_rows(0)
            result_rows(1)

        @block.scalar
        def _(act_):
            af = nc.scalar.activation

            for name, n in PARAM_ROWS:
                a = A[name]
                flat = {2: "a (k p) -> (a k) p", 3: "a b (k p) -> (a b k) p"}[len(a.shape)]
                act_.dma_start(prow[PARAM_AT[name]:PARAM_AT[name] + n, :], a.rearrange(flat, p=P)).then_inc(sem("params_in"), 16)
            for n, name in enumerate(("g_q", "g_k", "fox_q_norm_g_2", "fox_k_norm_g_2")):
                act_.dma_start(gain[:, n, :], A[name].to_broadcast([P, DH])).then_inc(sem("gain_in"), 16)

            def exps(tag, h):
                act_.wait_ge(sem(f"max_ready{tag}"), h + 1)
                for t, (a, b) in enumerate(((0, P), (P, SC))):
                    last = af(sp[:, h % 4, a:b], sp[:, h % 4, a:b], ACT.Exp, bias=aneg[:, h, t:t + 1], scale=SCALE,
                              accum_out=asum[:, h, t:t + 1])
                    last.then_inc(sem(f"exp_ready{tag}"), 1)

            def probs_out(tag, h):
                src = small.ready(act_, f"pt{tag}{h}")
                af(pT[:, h % 2, :], src[:, 0:SC], ACT.Copy).then_inc(sem(f"pT_ready{tag}"), 1)

            def values_out(tag, h, y, ready):
                src = small.ready(act_, f"pv{tag}{h}")
                a = DH * (h % 2)
                af(y[a:a + DH, h // 2, :], src[a:a + DH, 0:T], ACT.Copy).then_inc(sem(ready), 1)

            def attention_step(tag, names, y, ready):
                for name in names:
                    if name.startswith("qk"):
                        exps(tag, int(name[-1]))
                    elif name.startswith("pt"):
                        probs_out(tag, int(name[-1]))
                    elif name.startswith("pv"):
                        values_out(tag, int(name[-1]), y, ready)

            def copy_out(out_, banks, name, ready):
                af(out_, banks.ready(act_, name), ACT.Copy).then_inc(sem(ready), 1)

            def two_tiles(t, u):
                return t[:, 2 * u:2 * u + 2, :]

            src = small.ready(act_, "params")
            af(pcol[:, :], src[:, 0:PARAM_N], ACT.Copy).then_inc(sem("pcol_ready"), 1)
            act_.wait_ge(sem("pcol_ready"), 1)
            af(sc_c[:, 0, :], pc("c"), ACT.Tanh, scale=0.5).then_inc(sem("tanh_c_ready"), 1)
            for i in range(4):
                copy_out(two_tiles(xT, i), small, f"x{i}", "xT_ready")
                act_.wait_ge(sem("xT_ready"), i + 1)
                af(two_tiles(sq, i), two_tiles(xT, i), ACT.Square).then_inc(sem("sq_norm1"), 1)
            act_.wait_ge(sem("lb_sub_ready"), 1)
            af(lbt[:, 2:4, :], lbt[:, 0:2, :], ACT.Exp).then_inc(sem("lb_exp_ready"), 1)

            def modulation_out(c):
                src = small.ready(act_, f"ada{c}")
                n = COL // P
                af(mod[:, c * n:(c + 1) * n], src[:, 0:n], ACT.Copy).then_inc(sem("mod_raw"), 1)

            def modulation_after(unit):
                if unit in ada_at:
                    modulation_out(ada_at[unit])

            for c in range(ADA_EARLY):
                modulation_out(c)
            for k in range(KD):
                act_.wait_ge(sem("h1_scaled"), k + 1)
                af(hT[:, k, :], hT[:, k, :], ACT.Identity, bias=mod[:, k:k + 1]).then_inc(sem("h1_ready"), 1)
            for name, row in (("q", qrow), ("k", krow), ("v", vrow)):
                for u in range(2):
                    copy_out(row[:, u, :], dense, f"{name}{u}", f"{name}_rows")
                    if name == "v":
                        which, dst = (("tq", qT), ("tk", kT))[u]
                        for i in range(2):
                            copy_out(two_tiles(dst, i), small, f"{which}{i}", f"{which[1]}T_ready")
                    modulation_after(f"{name}{u}")
            for u in range(6):
                if u < 2:
                    copy_out(two_tiles(xbT, u), dense, f"xb{u}", "xb_ready")
                attention_step("", att1[u], yaT, "ya_ready")
                modulation_after(f"{('xb', 'cg', 'bg')[u // 2]}{u % 2}")
            for u in range(8):
                src = dense.ready(act_, f"gate{u}")
                af(two_tiles(gates, u), src, ACT.Tanh, scale=0.5).then_inc(sem("gates_ready"), 1)
                if 6 + u < len(att1):
                    attention_step("", att1[6 + u], yaT, "ya_ready")
                modulation_after(f"gate{u}")
            for k in range(KD):
                act_.wait_ge(sem("x1_ready"), k + 1)
                af(sq[:, k, :], xT[:, k, :], ACT.Square).then_inc(sem("sq_norm2"), 1)
            for k in range(KD):
                act_.wait_ge(sem("h2_scaled"), k + 1)
                af(hT[:, k, :], hT[:, k, :], ACT.Identity, bias=mod[:, 3 * KD + k:3 * KD + k + 1]).then_inc(sem("h2_ready"), 1)
            for i in range(4):
                copy_out(rows[:, i // 2, (i % 2) * 512:(i % 2) * 512 + 512], small, f"h2r{i}", "h2_rows_ready")
            act_.wait_ge(sem("route_sub_ready"), 1)
            af(rt[:, 6, :, 0:GROUPS], rt[:, 7, :, 0:GROUPS], ACT.Exp).then_inc(sem("route_exp_ready"), 1)
            act_.wait_ge(sem("second_ready"), 1)
            af(r1[:, 6, :], r1[:, 5, :], ACT.Exp).then_inc(sem("second_exp_ready"), 1)

            def experts(rounds, done, ahead):
                def tokens_out(count):
                    act_.wait_ge(sem("moe_gather0_done"), count)
                    af(xs[:, 0:4, :], GA.rearrange("p (k c) -> p k c", c=P), ACT.Copy).then_inc(sem("moe_xs0_ready"), 1)

                tokens_out(ahead + 1)
                with act_.Fori(0, PAIRS * rounds) as i:
                    act_.wait_ge(sem("moe_w1_used"), i + done + 1)
                    af(sil, HA, ACT.Silu).then_inc(sem("moe_sil_ready"), 1)
                    tokens_out(i + ahead + 2)
                    act_.wait_ge(sem("moe_hidT_done"), i + done + 1)
                    af(hidT, GA.rearrange("p (f c) -> p f c", c=P), ACT.Copy).then_inc(sem("moe_hidT_ready"), 1)
                    act_.wait_ge(sem("moe_ys0_done"), i + done + 1)
                    af(ys[:, 0:512], HA, ACT.Copy).then_inc(sem("moe_ys0_ready"), 1)

            act_.wait_ge(sem("flag_ready"), 1)
            more = act_.value_load(flag[0:1, 0:1], min_val=0, max_val=1)
            experts(1, 0, 0)
            with act_.If(more > 0):
                experts(EXTRA_ROUNDS, PAIRS, PAIRS + 1)
            for k in range(KD):
                act_.wait_ge(sem("x2_ready"), k + 1)
                af(sq[:, k, :], xT[:, k, :], ACT.Square).then_inc(sem("sq_mix"), 1)
            for u in range(2):
                src = dense.ready(act_, f"hf{u}")
                af(two_tiles(khT, u), src, ACT.Exp, scale=-1.0).then_inc(sem("hf_exp"), 1)
                if u == 0:
                    act_.wait_ge(sem("fox_abs_ready"), 1)
                    af(fl[:, 2, :], fl[:, 1, :], ACT.Exp, scale=-1.0).then_inc(sem("fox_exp_ready"), 1)
                    act_.wait_ge(sem("fox_exp_ready"), 1)
                    af(fl[:, 2, :], fl[:, 2, :], ACT.Ln, bias=1.0).then_inc(sem("fox_ln_ready"), 1)
            act_.wait_ge(sem("fg_ready"), 1)
            af(QE[0], QE[0], ACT.Ln).then_inc(sem("logf_ready"), 1)
            for u in range(2):
                src = dense.ready(act_, f"hq{u}")
                af(two_tiles(qhT, u), src, ACT.Tanh, scale=0.5).then_inc(sem("hq_tanh"), 1)
            for u in range(2):
                copy_out(irow[:, u, :], dense, f"hi{u}", "hi_ready")

            def decay(n):
                act_.wait_ge(sem("diff_ready"), n + 1)
                af(E[n % 2], E[n % 2], ACT.Exp).then_inc(sem("decay_ready"), 1)

            decay(0)
            n_level = 1
            for name, row in (("fq", qrow), ("fk", krow), ("fv", vrow)):
                for u in range(2):
                    copy_out(row[:, u, :], dense, f"{name}{u}", f"{name}_rows")
                    decay(n_level)
                    n_level += 1
                    if (name, u) in (("fk", 0), ("fv", 0)):
                        which, dst = (("q", qT), ("k", kT))[name == "fv"]
                        for i in range(2):
                            copy_out(two_tiles(dst, i), small, f"t{which}_b{i}", f"{which}T_ready_b")
            for u in range(2):
                src = dense.ready(act_, f"hg{u}")
                af(two_tiles(sgT, u), src, ACT.Tanh, scale=0.5).then_inc(sem("hg_tanh"), 1)
                if n_level < len(level_names) - 1:
                    decay(n_level)
                    n_level += 1
            for u in range(8):
                src = dense.ready(act_, f"gate_b{u}")
                af(two_tiles(gates, u), src, ACT.Tanh, scale=0.5).then_inc(sem("gates_ready_b"), 1)
                if u == 0:
                    for v in range(2):
                        src = small.ready(act_, f"ho{v}")
                        af(two_tiles(hoT, v), src, ACT.Copy).then_inc(sem("ho_ready"), 1)
                        act_.wait_ge(sem("ho_ready"), v + 1)
                        af(two_tiles(hsq, v), two_tiles(hoT, v), ACT.Square).then_inc(sem("hsq_ready"), 1)
                steps = att2[u:u + 1] if u < 7 else att2[7:]
                for names in steps:
                    attention_step("_b", names, ybT, "yb_ready_b")

            def lead_weights(m):
                n = chunk_of[split_chunks[m]]
                act_.wait_ge(chunk_in[n % SLOTS], arrive_at[n])
                if m >= 2:
                    act_.wait_ge(*chunks[n - 2][1])
                for w, _, lead in halves(m):
                    af(lead, w, ACT.Copy).then_inc(sem("w_lead"), 1)

            act_.wait_ge(sem("merged_ready_b"), KD)
            lead_weights(0)
            for k in range(KD):
                act_.wait_ge(sem("x3_ready"), k + 1)
                af(sq[:, k, :], xT[:, k, :], ACT.Square).then_inc(sem("sq_ffn"), 1)
            def lead_hidden(f):
                act_.wait_ge(sem("act_ready"), f + 1)
                if f >= 4:
                    act_.wait_ge(sem("down_tiles"), f - 3)
                af(lead_act[f % 4], act[:, f, :], ACT.Copy).then_inc(sem("act_lead"), 1)

            for k in range(KD):
                act_.wait_ge(sem("hf_ready"), k + 1)
                af(lead_h[k], hT[:, k, :], ACT.Copy).then_inc(sem("h_lead"), 1)
            small.ready(act_, "ms_ffn")
            for f in range(FFT):
                if f % 2 == 0:
                    lead_weights(f // 2 + 1)
                src = dense.ready(act_, f"ffn{f}")
                if f >= 2:
                    act_.wait_ge(sem("act_ready"), f - 1)
                af(fsil[:, f % 2, :], src[:, 0:T], ACT.Silu).then_inc(sem("fsil_ready"), 1)
            for f in range(4):
                lead_hidden(f)
            for c in range(1, len(DOWN)):
                lead_weights(FFN_CHUNKS + c)
                for f in range(DOWN[c][0], sum(DOWN[c])):
                    lead_hidden(f)
            for k in range(KD):
                act_.wait_ge(sem("x4_ready"), k + 1)
                af(sq[:, k, :], xT[:, k, :], ACT.Square).then_inc(sem("sq_ple"), 1)
            copy_out(ppT, small, "pp", "ppT_ready")

            def result_out(n, t, half):
                copy_out(orow[:, t, half * 512:half * 512 + 512], small, f"o{t}{half}", "out_ready")

            for j in range(KD):
                src = dense.ready(act_, f"ple{j}")
                if j >= 2:
                    act_.wait_ge(sem("o_ready"), j - 1)
                af(thp[j % 2], src[:, 0:T], ACT.Tanh, scale=0.5).then_inc(sem("thp_ready"), 1)
                if j == 5:
                    result_out(0, 0, 0)
                    result_out(1, 1, 0)
            result_out(2, 0, 1)
            result_out(3, 1, 1)

        @block.vector
        def _(dve):
            v = nc.vector
            chain = [0]

            def link(ins):
                chain[0] += 1
                ins.then_inc(sem("dve_chain"), 1)
                dve.wait_ge(sem("dve_chain"), chain[0])

            def release(ins, banks, name):
                ins.then_inc(*banks.freed(name))
                dve.wait_ge(*banks.released[name])

            def inv_sqrt(y, x, a, b, signal=None):
                link(v.tensor_scalar(a.bitcast(I32), x.bitcast(I32), 1, None, ALU.logical_shift_right))
                link(v.tensor_scalar(y.bitcast(I32), a.bitcast(I32), -1.0, float(0x5F3759DF), ALU.mult, ALU.add))
                for step in range(3):
                    link(v.scalar_tensor_tensor(a, y, -0.5, x, ALU.mult, ALU.mult))
                    link(v.tensor_tensor(b, a, y, ALU.mult))
                    last = v.scalar_tensor_tensor(y, b, 1.5, y, ALU.add, ALU.mult)
                    if signal is None or step < 2:
                        link(last)
                    else:
                        last.then_inc(sem(signal), 1)

            def inv_norms(unit, n):
                src = small.ready(dve, unit)
                release(v.tensor_scalar(nrm[:, 1, 0:n], src[:, 0:n], EPS, None, ALU.add), small, unit)
                inv_sqrt(nrm[:, 0, 0:n], nrm[:, 1, 0:n], nrm[:, 2, 0:n], nrm[:, 3, 0:n], "inv_norm_ready")

            def scaled(name, scale, signal):
                factor = small.ready(dve, "rs_" + name)[:, 0:T]
                for k in range(KD):
                    v.scalar_tensor_tensor(hT[:, k, :], xT[:, k, :], scale[:, k:k + 1], factor, ALU.mult,
                                           ALU.mult).then_inc(sem(signal), 1)

            def head_norm(row, n, rope, signal):
                r3 = row.rearrange("p t (h d) -> p (t h) d", d=DH)
                t3 = norm_tmp.rearrange("p (n d) -> p n d", d=DH)
                link(v.tensor_tensor(t3, r3, r3, ALU.mult))
                link(v.tensor_reduce(nstat[:, 0, :], t3, AX.X, ALU.add))
                link(v.tensor_scalar(nstat[:, 1, :], nstat[:, 0, :], 1.0 / DH, EPS, ALU.mult, ALU.add))
                inv_sqrt(nstat[:, 0, :], nstat[:, 1, :], nstat[:, 2, :], nstat[:, 3, :])
                link(v.tensor_tensor(t3, r3, nstat[:, 0, :].unsqueeze(2).to_broadcast([P, TT * HEADS, DH]), ALU.mult))
                last = v.tensor_tensor(r3, t3, gain[:, n, :].unsqueeze(1).to_broadcast([P, TT * HEADS, DH]), ALU.mult)
                if not rope:
                    last.then_inc(sem(signal), 1)
                    return
                link(last)
                r4 = row.rearrange("p t (h d) -> p t h d", d=DH)
                x1, x2 = r4[:, :, :, 0:HALF], r4[:, :, :, HALF:ROT]
                c4, s4 = (z.unsqueeze(2).to_broadcast([P, TT, HEADS, HALF]) for z in (cos, sin))
                t4 = [rtmp[:, i, :].rearrange("p (t h r) -> p t h r", t=TT, h=HEADS) for i in range(4)]
                for dst, a, b in ((0, x1, c4), (1, x2, s4), (2, x2, c4), (3, x1, s4)):
                    last = v.tensor_tensor(t4[dst], a, b, ALU.mult)
                    if dst < 3:
                        last.then_inc(sem("rope_parts"), 1)
                link(last)
                dve.wait_ge(sem("rope_parts"), 3 * (n + 1))
                link(v.tensor_tensor(x1, t4[0], t4[1], ALU.subtract))
                v.tensor_tensor(x2, t4[2], t4[3], ALU.add).then_inc(sem(signal), 1)

            def score_max(tag, h, bias):
                if h >= 4:
                    small.ready(dve, f"pt{tag}{h - 4}")
                mask = causal
                if bias:
                    b = small.ready(dve, f"bias{h}")
                    mask = fmask[:, :]
                    link(v.tensor_tensor(mask[:, 0:P], causal[:, 0:P], b[:, 0:P], ALU.add))
                    release(v.tensor_tensor(mask[:, P:SC], causal[:, P:SC], b[:, 0:T], ALU.add), small, f"bias{h}")
                src = small.ready(dve, f"qk{tag}{h}")
                for t, (a, b) in enumerate(((0, P), (P, SC))):
                    ins = v.tensor_tensor_reduce(out=sp[:, h % 4, a:b], in0=src[:, a:b], in1=mask[:, a:b], scale=1.0,
                                                 scalar=-3e38, op0=ALU.add, op1=ALU.max, accum_out=amax[:, h, t:t + 1])
                    if t == 0:
                        link(ins)
                    else:
                        release(ins, small, f"qk{tag}{h}")
                v.tensor_scalar(aneg[:, h, :], amax[:, h, :], -SCALE, None, ALU.mult).then_inc(sem(f"max_ready{tag}"), 1)

            def normalise(tag, h):
                dve.wait_ge(sem(f"exp_ready{tag}"), 2 * h + 2)
                link(v.reciprocal(ainv[:, h, :], asum[:, h, :]))
                link(v.tensor_scalar(sp[:, h % 4, 0:P], sp[:, h % 4, 0:P], ainv[:, h, 0:1], None, ALU.mult))
                v.tensor_scalar(sp[:, h % 4, P:SC], sp[:, h % 4, P:SC], ainv[:, h, 1:2], None,
                                ALU.mult).then_inc(sem(f"probs_ready{tag}"), 1)

            def two_tiles(t, u):
                return t[:, 2 * u:2 * u + 2, :]

            def pair(src):
                return src.rearrange("p (j t) -> p j t", t=T)

            def merge(tag):
                dve.wait_ge(sem(f"gates_ready{tag}"), 8)
                for j in range(KD):
                    src = dense.ready(dve, f"proj{tag}{j}")
                    v.scalar_tensor_tensor(gates[:, j, :], gates[:, j, :], 1.0, src[:, 0:T], ALU.add,
                                           ALU.mult).then_inc(sem("gate_a" + tag), 1)
                    link(v.scalar_tensor_tensor(gates[:, KD + j, :], gates[:, KD + j, :], 1.0, src[:, T:2 * T], ALU.add,
                                                ALU.mult))
                    dve.wait_ge(sem("gate_a" + tag), j + 1)
                    v.tensor_tensor(merged[:, j, :], gates[:, j, :], gates[:, KD + j, :],
                                    ALU.add).then_inc(sem(f"merged_ready{tag}"), 1)

            def residual(units, factor, ready):
                for u in range(4):
                    src = dense.bank(f"{units}{u}")
                    if units != "moe":
                        dense.ready(dve, f"{units}{u}")
                    for j in range(2):
                        k = 2 * u + j
                        v.scalar_tensor_tensor(xT[:, k, :], src[:, j * T:(j + 1) * T], factor(k), xT[:, k, :], ALU.mult,
                                               ALU.add).then_inc(sem(ready), 1)

            dve.wait_ge(sem("tanh_c_ready"), 1)
            link(v.scalar_tensor_tensor(sc_c[:, 1, :], sc_c[:, 0, :], 1.0, pc("c"), ALU.add, ALU.mult))
            link(v.tensor_scalar(sc_c[:, 2, :], sc_c[:, 1, :], 0.5, None, ALU.mult))
            link(v.tensor_tensor(lbt[:, 4, :], pc("hg_lb_logits_2", 0, HG), pc("hg_lb_logits_2", HG, HG), ALU.max))
            link(v.tensor_tensor(lbt[:, 0, :], pc("hg_lb_logits_2", 0, HG), lbt[:, 4, :], ALU.subtract))
            v.tensor_tensor(lbt[:, 1, :], pc("hg_lb_logits_2", HG, HG), lbt[:, 4, :], ALU.subtract).then_inc(sem("lb_sub_ready"), 1)
            dve.wait_ge(sem("lb_exp_ready"), 1)
            link(v.tensor_tensor(lbt[:, 5, :], lbt[:, 2, :], lbt[:, 3, :], ALU.add))
            link(v.reciprocal(lbt[:, 6, :], lbt[:, 5, :]))
            link(v.tensor_tensor(lbt[:, 7, :], lbt[:, 2, :], lbt[:, 6, :], ALU.mult))
            link(v.tensor_scalar(lbt[:, 4, :], lbt[:, 7, :], -1.0, 1.0, ALU.mult, ALU.add))
            link(v.tensor_scalar(oghalf[:, :], pc("hg_onorm_g_2"), 0.5, None, ALU.mult))
            inv_norms("ms_norm1", TT)

            def modulation(c):
                slot = chunk_of[f"ada{c}"] % SLOTS
                dve.wait_ge(chunk_in[slot], arrive_at[chunk_of[f"ada{c}"]])
                if c >= 2:
                    small.ready(dve, f"ada{c - 2}")
                acc, w = ada_acc(c), wide(slot)
                link(v.tensor_scalar(acc, w[:, 0, :], sc_c[:, 2, 0:1], None, ALU.mult))
                for k in range(1, KD):
                    last = v.scalar_tensor_tensor(acc, w[:, k, :], sc_c[:, 2, k:k + 1], acc, ALU.mult, ALU.add)
                    if k < KD - 1:
                        link(last)
                last.then_inc(sem("ada_sums"), 1)

            for c in range(ADA_EARLY):
                modulation(c)
            dve.wait_ge(sem("mod_raw"), ADA_EARLY)
            link(v.tensor_tensor(mod[:, 0:2 * KD], mod[:, 0:2 * KD], pc("b_ada", 0, 2 * KD), ALU.add))
            link(v.scalar_tensor_tensor(scale1[:, :], mod[:, KD:2 * KD], 1.0, pc("g_norm1"), ALU.add, ALU.mult))
            scaled("norm1", scale1, "h1_scaled")
            modulation(4)
            modulation(5)
            dve.wait_ge(sem("gain_in"), 64)
            dve.wait_ge(sem("q_rows"), 2)
            head_norm(qrow, 0, True, "q_normed")
            modulation(6)
            dve.wait_ge(sem("k_rows"), 2)
            head_norm(krow, 1, True, "k_normed")
            modulation(7)
            dve.wait_ge(sem("pad_ready"), 1)

            def conv(c):
                w = lambda tap: pc("conv_w", tap * CT + c, 1)
                link(v.tensor_scalar(xbT[:, c, :], uT[:, c, 0:T], w(0), pc("conv_b", c, 1), ALU.mult, ALU.add))
                for tap in (1, 2):
                    link(v.scalar_tensor_tensor(xbT[:, c, :], uT[:, c, tap:tap + T], w(tap), xbT[:, c, :], ALU.mult, ALU.add))

            for n in range(HEADS + 1):
                if n in (2, 3):
                    u = n - 2
                    src = dense.ready(dve, f"cg{u}")
                    dve.wait_ge(sem("xb_ready"), u + 1)
                    release(v.tensor_tensor(uT[:, 2 * u:2 * u + 2, 2:T + 2], pair(src), two_tiles(xbT, u), ALU.mult), dense, f"cg{u}")
                if n in (4, 5):
                    u = n - 4
                    src = dense.ready(dve, f"bg{u}")
                    v.tensor_tensor(two_tiles(ybT, u), pair(src), two_tiles(xbT, u), ALU.mult).then_inc(sem("yb_ready"), 1)
                if n < HEADS:
                    score_max("", n, False)
                if n >= 1:
                    normalise("", n - 1)
                if n in (2, 3):
                    conv(2 * (n - 2))
                    conv(2 * (n - 2) + 1)
                if n in (0, 1, 4, 5):
                    modulation({0: 8, 1: 9, 4: 10, 5: 11}[n])
            dve.wait_ge(sem("mod_raw"), ADA)
            link(v.tensor_tensor(mod[:, 2 * KD:], mod[:, 2 * KD:], pc("b_ada", 2 * KD, 4 * KD), ALU.add))
            link(v.scalar_tensor_tensor(scale2[:, :], mod[:, 4 * KD:5 * KD], 1.0, pc("g_norm2"), ALU.add, ALU.mult))
            link(v.tensor_scalar(ga1h[:, :], mod[:, 2 * KD:3 * KD], 0.5, None, ALU.mult))
            merge("")
            residual("wo", lambda k: ga1h[:, k:k + 1], "x1_ready")
            v.memset(zeros, 0.0).then_inc(sem("zeros_ready"), 1)
            inv_norms("ms_norm2", TT)
            scaled("norm2", scale2, "h2_scaled")
            src = small.ready(dve, "logits")
            dve.wait_ge(sem("route_in"), 64)
            release(v.tensor_tensor(lg[:, :, :], src.rearrange("p (t n) -> p t n", n=64)[:, 0:TT, 0:GROUPS + EXPERTS],
                                 br[:, :].unsqueeze(1).to_broadcast([P, TT, GROUPS + EXPERTS]), ALU.add), small, "logits")
            index = cst[:, C_IOTA:C_IOTA + EXPERTS].unsqueeze(1)

            def wide_(a, n):
                return a.unsqueeze(2).to_broadcast([P, TT, n])

            def first_max(values, n, best, one_hot, tmp, least):
                link(v.tensor_reduce(best, values, AX.X, ALU.max))
                link(v.tensor_tensor(tmp, values, wide_(best, n), ALU.is_equal))
                link(v.scalar_tensor_tensor(tmp, tmp, -64.0, index[:, :, 0:n].to_broadcast([P, TT, n]), ALU.mult, ALU.add))
                link(v.tensor_reduce(least, tmp, AX.X, ALU.min))
                link(v.tensor_tensor(one_hot, tmp, wide_(least, n), ALU.is_equal))

            g, e = lg[:, :, 0:GROUPS], lg[:, :, GROUPS:]
            gsel = rt[:, 1, :, 0:GROUPS]
            link(v.memset(rank[:, :, :], -1.0))
            link(v.memset(wgt[:, :, :], 0.0))
            first_max(g, GROUPS, r1[:, 0, :], gsel, rt[:, 2, :, 0:GROUPS], r1[:, 1, :])
            v.tensor_tensor(rt[:, 7, :, 0:GROUPS], g, wide_(r1[:, 0, :], GROUPS), ALU.subtract).then_inc(sem("route_sub_ready"), 1)
            link(v.tensor_scalar(rt[:, 2, :, 0:GROUPS], gsel, BIG, -BIG, ALU.mult, ALU.add))

            def by_group(a):
                return a.rearrange("p t (g n) -> p t g n", g=GROUPS)

            def per_group(a):
                return a.unsqueeze(3).to_broadcast([P, TT, GROUPS, PER_GROUP])

            link(v.tensor_tensor(by_group(rt[:, 3, :, :]), by_group(e), per_group(gsel), ALU.mult))
            link(v.tensor_tensor(by_group(rt[:, 4, :, :]), by_group(rt[:, 3, :, :]), per_group(rt[:, 2, :, 0:GROUPS]), ALU.add))
            first_max(rt[:, 4, :, :], EXPERTS, r1[:, 2, :], rt[:, 1, :, :], rt[:, 3, :, :], r1[:, 1, :])
            link(v.scalar_tensor_tensor(rt[:, 5, :, :], rt[:, 1, :, :], -2.0 * BIG, rt[:, 4, :, :], ALU.mult, ALU.add))
            first_max(rt[:, 5, :, :], EXPERTS, r1[:, 3, :], rt[:, 2, :, :], rt[:, 3, :, :], r1[:, 1, :])
            v.tensor_tensor(rt[:, 0, :, :], rt[:, 1, :, :], rt[:, 2, :, :], ALU.add).then_inc(sem("chosen_ready"), 1)
            v.tensor_tensor(r1[:, 5, :], r1[:, 3, :], r1[:, 2, :], ALU.subtract).then_inc(sem("second_ready"), 1)
            src = small.ready(dve, "rank")
            link(v.scalar_tensor_tensor(rt[:, 5, :, :], src[:, 0:TT * EXPERTS].rearrange("p (t n) -> p t n", t=TT), 1.0,
                                        rt[:, 0, :, :], ALU.add, ALU.mult))

            def slots_of_round(r):
                link(v.tensor_scalar(rank[:, :, r * EXPERTS:(r + 1) * EXPERTS], rt[:, 5, :, :], -1.0 - CAP * r, None, ALU.add))

            def one_hot(dst, col, signal, weighted=False):
                for e_ in range(2):
                    for t in range(TT):
                        place = rank[:, t, bass.ds(col + e_, 1)]
                        into = dst[:, t, e_ * CAP:(e_ + 1) * CAP]
                        if weighted:
                            last = v.tensor_scalar(into, iota, place, wgt[:, t, bass.ds(col + e_, 1)], ALU.is_equal, ALU.mult)
                        else:
                            last = v.tensor_scalar(into, iota, place, None, ALU.is_equal)
                        last.then_inc(sem("moe_" + signal), 1)

            slots_of_round(0)
            one_hot(S, 0, "s_ready")
            release(v.tensor_reduce(flagf[:, 0:1], src[0:1, 64:96], AX.X, ALU.max), small, "rank")
            v.tensor_scalar(flag[:, :], flagf[:, 0:1], float(CAP), None, ALU.is_gt).then_inc(sem("flag_ready"), 1)
            dve.wait_ge(sem("route_exp_ready"), 1)
            link(v.tensor_reduce(r1[:, 7, :], rt[:, 6, :, 0:GROUPS], AX.X, ALU.add))
            dve.wait_ge(sem("second_exp_ready"), 1)
            link(v.tensor_scalar(r1[:, 8, :], r1[:, 6, :], 1.0, None, ALU.add))
            link(v.tensor_tensor(r1[:, 9, :], r1[:, 7, :], r1[:, 8, :], ALU.mult))
            link(v.reciprocal(r1[:, 10, :], r1[:, 9, :]))
            link(v.tensor_tensor(r1[:, 11, :], r1[:, 10, :], r1[:, 6, :], ALU.mult))
            link(v.tensor_tensor(rt[:, 3, :, :], rt[:, 1, :, :], wide_(r1[:, 10, :], EXPERTS), ALU.mult))
            link(v.tensor_tensor(rt[:, 4, :, :], rt[:, 2, :, :], wide_(r1[:, 11, :], EXPERTS), ALU.mult))
            for r in range(1 + EXTRA_ROUNDS):
                link(v.tensor_tensor(wgt[:, :, r * EXPERTS:(r + 1) * EXPERTS], rt[:, 3, :, :], rt[:, 4, :, :], ALU.add))
            for r in range(1, 1 + EXTRA_ROUNDS):
                slots_of_round(r)

            def experts(first_round, rounds, done, ahead):
                col0 = first_round * EXPERTS

                def tokens_out(count):
                    dve.wait_ge(sem("moe_gather1_done"), count)
                    v.tensor_copy(xs[:, 4:8, :], GB.rearrange("p (k c) -> p k c", c=P)).then_inc(sem("moe_xs1_ready"), 1)

                if first_round > 0:
                    one_hot(S, col0, "s_ready")
                tokens_out(ahead + 1)
                with dve.Fori(0, PAIRS * rounds) as i:
                    one_hot(S, 2 * i + col0 + 2, "s_ready")
                    one_hot(Sw, 2 * i + col0, "sw_ready", True)
                    dve.wait_ge(sem("moe_sil_ready"), i + done + 1)
                    dve.wait_ge(sem("moe_w3_used"), i + done + 1)
                    v.tensor_tensor(hid, sil, HB, ALU.mult).then_inc(sem("moe_hid_ready"), 1)
                    tokens_out(i + ahead + 2)
                    dve.wait_ge(sem("moe_st_done"), i + done + 1)
                    v.tensor_copy(ST, GB[:, 0:T]).then_inc(sem("moe_st_ready"), 1)
                    dve.wait_ge(sem("moe_ys1_done"), i + done + 1)
                    v.tensor_copy(ys[:, 512:1024], HB).then_inc(sem("moe_ys1_ready"), 1)
                dve.wait_ge(sem("moe_combined"), PAIRS * rounds + done)

            dve.wait_ge(sem("flag_ready"), 1)
            more = dve.value_load(flag[0:1, 0:1], min_val=0, max_val=1)
            experts(0, 1, 0, 0)
            with dve.If(more > 0):
                experts(1, EXTRA_ROUNDS, PAIRS, PAIRS + 1)
            residual("moe", lambda k: mod[:, 5 * KD + k:5 * KD + k + 1], "x2_ready")
            inv_norms("ms_mix", TT)
            scaled("mix", pc("norm_mix_g_2"), "hm_ready")
            src = small.ready(dve, "fox_f")
            dve.wait_ge(sem("fox_in"), 32)
            release(v.tensor_scalar(fl[:, 0, :], src[0:HEADS, 0:T], fbias[:, 0:1], None, ALU.add), small, "fox_f")
            v.scalar_tensor_tensor(fl[:, 1, :], fl[:, 0, :], -1.0, fl[:, 0, :], ALU.mult, ALU.max).then_inc(sem("fox_abs_ready"), 1)
            link(v.tensor_scalar(fl[:, 0, :], fl[:, 0, :], 0.0, None, ALU.min))
            dve.wait_ge(sem("fox_ln_ready"), 1)
            link(v.tensor_tensor(fl[:, 1, :], fl[:, 0, :], fl[:, 2, :], ALU.subtract))
            link(v.tensor_tensor_scan(fl[:, 2, :], ones[0:HEADS, 0:1].to_broadcast([HEADS, T]), fl[:, 1, :], 0.0, ALU.mult, ALU.add))
            v.tensor_scalar(foxc[:, :], fl[:, 2, :], -1.0 / SCALE, None, ALU.mult).then_inc(sem("fox_c_ready"), 1)
            dve.wait_ge(sem("hf_exp"), 2)
            fg = QE[0]
            link(v.tensor_scalar(khT, khT, 1.0, None, ALU.add))
            link(v.reciprocal(fg, khT))
            for h in range(HG):
                last = v.tensor_scalar(fg[:, h, :], fg[:, h, :], lbt[:, 4, h:h + 1], lbt[:, 7, h:h + 1], ALU.mult, ALU.add)
                if h < HG - 1:
                    last.then_inc(sem("fg_parts"), 1)
            link(last)
            dve.wait_ge(sem("fg_parts"), HG - 1)
            v.tensor_scalar(khT, fg, -0.5, 0.5, ALU.mult, ALU.add).then_inc(sem("fg_ready"), 1)
            dve.wait_ge(sem("logf_ready"), 1)
            for h in range(HG):
                for t in range(TT):
                    last = v.tensor_tensor_scan(bT[:, h, t * P:(t + 1) * P], ones, fg[:, h, t * P:(t + 1) * P], 0.0,
                                                ALU.mult, ALU.add)
                    if (h, t) != (HG - 1, TT - 1):
                        last.then_inc(sem("scans"), 1)
            link(last)
            dve.wait_ge(sem("scans"), HG * TT - 1)
            for u in range(2):
                src = dense.ready(dve, f"hq{u}")
                dve.wait_ge(sem("hq_tanh"), u + 1)
                release(v.scalar_tensor_tensor(two_tiles(qhT, u), two_tiles(qhT, u), 1.0, pair(src), ALU.add, ALU.mult), dense, f"hq{u}")

            def differences(n):
                name = level_names[n]
                if n >= 2:
                    dve.wait_ge(sem("ke_ready"), n - 1)
                    dve.wait_ge(sem("qe_ready"), n - 1)
                if name == "cross":
                    b, d = bT, E[n % 2]
                    v.tensor_tensor(d[:, :, 0:P], b[:, :, P - 1:P].to_broadcast([P, HG, P]), b[:, :, 0:P],
                                    ALU.subtract).then_inc(sem("left_parts"), 1)
                    last = v.tensor_copy(d[:, :, P:T], b[:, :, P:T])
                else:
                    m = int(name[3:])
                    b, d = (z.rearrange("p h (n two m) -> p (h n) two m", two=2, m=m) for z in (bT, E[n % 2]))
                    mid = b[:, :, 0, m - 1:m].to_broadcast([P, HG * T // (2 * m), m])
                    v.tensor_tensor(d[:, :, 0, :], mid, b[:, :, 0, :], ALU.subtract).then_inc(sem("left_parts"), 1)
                    last = v.tensor_tensor(d[:, :, 1, :], b[:, :, 1, :], mid, ALU.subtract)
                dve.wait_ge(sem("left_parts"), n + 1)
                last.then_inc(sem("diff_ready"), 1)

            def decayed_queries(n):
                dve.wait_ge(sem("decay_ready"), n + 1)
                if n >= 2:
                    small.ready(dve, level_units[level_names[n - 2]][-1])
                v.tensor_tensor(QE[n % 2], qhT, E[n % 2], ALU.mult).then_inc(sem("qe_ready"), 1)

            def scores_out(n):
                name = level_names[n]
                if name == "cross":
                    src = small.ready(dve, "cross")
                    release(v.tensor_copy(scX.rearrange("p h t -> p (h t)"), src), small, "cross")
                    return
                at = C_IDENT if name == "diag" else C_LEVEL + (n - 1) * P
                mask = cst[:, at:at + P].bitcast(I32).unsqueeze(1).to_broadcast([P, 4, P])
                for u, unit in enumerate(level_units[name]):
                    src = small.ready(dve, unit)
                    release(v.copy_predicated(scT[:, 4 * u:4 * u + 4, :], mask, src.rearrange("p (n t) -> p n t", t=P)), small, unit)

            dve.wait_ge(sem("scores_zeroed"), 1)
            n_levels = len(level_names)
            for step in range(n_levels + 1):
                if step < n_levels - 1:
                    differences(step)
                if 1 <= step < n_levels:
                    decayed_queries(step - 1)
                if step >= 2:
                    scores_out(step - 2)
                if step == 2:
                    dve.wait_ge(sem("fq_rows"), 2)
                    head_norm(qrow, 2, False, "q_normed_b")
                if step == 4:
                    dve.wait_ge(sem("fk_rows"), 2)
                    head_norm(krow, 3, False, "k_normed_b")
            scores_out(n_levels - 1)
            for u in range(2):
                src = dense.ready(dve, f"hg{u}")
                dve.wait_ge(sem("hg_tanh"), u + 1)
                release(v.scalar_tensor_tensor(two_tiles(sgT, u), two_tiles(sgT, u), 1.0, pair(src), ALU.add, ALU.mult), dense, f"hg{u}")

            def hgrn_out():
                for u in range(2):
                    src = small.ready(dve, f"rs_h{u}")
                    dve.wait_ge(sem("ho_ready"), u + 1)
                    release(v.scalar_tensor_tensor(two_tiles(hoT, u), two_tiles(hoT, u), oghalf[:, 0:1], pair(src), ALU.mult,
                                                   ALU.mult), small, f"rs_h{u}")
                    v.tensor_tensor(two_tiles(yaT, u), two_tiles(hoT, u), two_tiles(sgT, u),
                                    ALU.mult).then_inc(sem("ya_ready_b"), 1)

            for n in range(HEADS + 1):
                if n < HEADS:
                    score_max("_b", n, True)
                if n >= 1:
                    normalise("_b", n - 1)
                if n == 1:
                    inv_norms("ms_h", HG * TT)
                if n == 2:
                    hgrn_out()
            merge("_b")

            def rest_weights(m):
                w, rest, lead = halves(m)[0]
                dve.wait_ge(sem("w_lead"), lead_done[m] + 1)
                v.tensor_tensor(rest, w, lead.bitcast(F32), ALU.subtract).then_inc(sem("w_rest_a"), 1)

            rest_weights(0)
            residual("wo_b", lambda k: 0.5, "x3_ready")
            inv_norms("ms_ffn", TT)
            factor = small.ready(dve, "rs_ffn")[:, 0:T]
            for n in range(KD + 2):
                if n < KD:
                    v.scalar_tensor_tensor(hT[:, n, :], xT[:, n, :], pc("norm_ffn_g_2", n, 1), factor, ALU.mult,
                                           ALU.mult).then_inc(sem("hf_ready"), 1)
                if n >= 2:
                    k = n - 2
                    dve.wait_ge(sem("h_lead"), k + 1)
                    v.tensor_tensor(rest_h[:, k, :], hT[:, k, :], lead_h[k].bitcast(F32), ALU.subtract).then_inc(sem("h_rest"), 1)

            def rest_hidden(f):
                dve.wait_ge(sem("act_lead"), f + 1)
                v.tensor_tensor(rest_act[:, f, :], act[:, f, :], lead_act[f % 4].bitcast(F32), ALU.subtract).then_inc(sem("act_rest"), 1)

            for f in range(FFT):
                if f % 2 == 0:
                    rest_weights(f // 2 + 1)
                src = dense.bank(f"ffn{f}")
                dve.wait_ge(sem("fsil_ready"), f + 1)
                v.tensor_tensor(act[:, f, :], fsil[:, f % 2, :], src[:, T:2 * T], ALU.mult).then_inc(sem("act_ready"), 1)
            for f in range(4):
                rest_hidden(f)
            for c in range(1, len(DOWN)):
                rest_weights(FFN_CHUNKS + c)
                for f in range(DOWN[c][0], sum(DOWN[c])):
                    rest_hidden(f)
            residual("down", lambda k: 1.0, "x4_ready")
            inv_norms("ms_ple", TT)
            scaled("ple", pc("norm_ple_g_2"), "hp_ready")
            for j in range(KD):
                dve.wait_ge(sem("thp_ready"), j + 1)
                src = dense.ready(dve, f"ple{j}")
                release(v.scalar_tensor_tensor(oT[:, j, :], thp[j % 2], 1.0, src[:, T:2 * T], ALU.add, ALU.mult), dense, f"ple{j}")
                v.scalar_tensor_tensor(oT[:, j, :], oT[:, j, :], 0.5, xT[:, j, :], ALU.mult, ALU.add).then_inc(sem("o_ready"), 1)


_INS = ["x", "c", "w_ada", "b_ada", "g_norm1", "g_norm2", "w_in", "g_q", "g_k", "conv_w", "conv_b", "w_pa", "w_pb",
        "w_o", "w_rg", "b_rg", "w_re", "b_re", "w1", "w3", "w2", "p_2", "norm_mix_g_2", "w_in_2", "hg_lb_logits_2",
        "hg_onorm_g_2", "fox_f_bias_2", "fox_q_norm_g_2", "fox_k_norm_g_2", "w_branch_a_2", "w_branch_b_2", "w_out_2",
        "norm_ffn_g_2", "w_ffn_gate_2", "w_ffn_up_2", "w_ffn_down_2", "norm_ple_g_2", "w_ple_gate_2", "w_ple_proj_2"]


def kernel(**inputs):
    import concourse.bacc as _bacc
    from concourse.bass_utils import run_bass_kernel_spmd as _run

    nc = _bacc.Bacc("TRN2", target_bir_lowering=False, num_devices=1)
    arrays, args = {}, {}
    for name in _INS:
        a = np.ascontiguousarray(inputs[name])
        arrays[f"in_{name}"] = a
        args[name] = nc.dram_tensor(f"in_{name}", a.shape, mybir.dt.from_np(a.dtype), kind="ExternalInput").ap()
    arrays["constants"] = constant_table()
    consts = nc.dram_tensor("constants", (P, C_ALL), F32, kind="ExternalInput").ap()
    out = nc.dram_tensor("out", (1, T, D), F32, kind="ExternalOutput").ap()
    two_blocks(nc, args, consts, out)
    r = _run(nc, [arrays], core_ids=[0])
    return r.results[0]["out"]
```
